# Optimizing a Trainium2 kernel written in Bass

```python
import jax, jax.numpy as jnp
from jax import lax
import numpy as np

D_MODEL = 1024
BATCH = 1
SEQ = 256
DEPTH = 1
DEC_BATCH = 8
DEC_SEQ = 4
PAST_LEN = 2048
PAGE_SIZE = 128

MOBA_HEADS = 8
MOBA_HEAD_DIM = 64
MOBA_WIDTH = MOBA_HEADS * MOBA_HEAD_DIM
MOBA_BLOCK = 256
MOBA_TOPK = 3
MOBA_QCHUNK = 16
ROPE_THETA = 500000.0
ROPE_DIM = MOBA_HEAD_DIM // 4
GLA_HEADS = 4
GLA_DK = 64
GLA_DV = 128
GLA_KEY_WIDTH = GLA_HEADS * GLA_DK
GLA_WIDTH = GLA_HEADS * GLA_DV
GLA_LOWRANK = 16
GLA_TAU = 16.0
GLA_CHUNK = 64
MIX_WIDTH = MOBA_WIDTH + GLA_WIDTH
IN_SPLITS = (MOBA_WIDTH, 2 * MOBA_WIDTH, 3 * MOBA_WIDTH,
             3 * MOBA_WIDTH + GLA_KEY_WIDTH,
             3 * MOBA_WIDTH + 2 * GLA_KEY_WIDTH,
             3 * MOBA_WIDTH + 2 * GLA_KEY_WIDTH + GLA_WIDTH,
             3 * MOBA_WIDTH + 2 * GLA_KEY_WIDTH + 2 * GLA_WIDTH)
IN_COLS = 3 * MOBA_WIDTH + 2 * GLA_KEY_WIDTH + 2 * GLA_WIDTH + GLA_LOWRANK
MEM_LEN = 256
MEM_HEADS = 4
MEM_HEAD_DIM = D_MODEL // MEM_HEADS
PEER_HEADS = 8
PEER_NKEYS = 128
PEER_EXPERTS = PEER_NKEYS * PEER_NKEYS
PEER_DQ = 256
PEER_TOPK = 16
PEER_TOKEN_CHUNK = 256
EPS = 1e-6
NEG = -1e30

kernel_name = 'moba_gla_peer_hybrid_step'

def rmsnorm(x, g):
    xf = x.astype(jnp.float32)
    y = xf * lax.rsqrt(jnp.mean(xf * xf, axis=-1, keepdims=True) + EPS)
    return (y * g.astype(jnp.float32)).astype(x.dtype)

def partial_rope(x, pos):
    half = ROPE_DIM // 2
    inv_freq = 1.0 / (ROPE_THETA ** (jnp.arange(half, dtype=jnp.float32) * (2.0 / ROPE_DIM)))
    ang = pos.astype(jnp.float32)[:, None] * inv_freq[None, :]
    cos = jnp.cos(ang)[:, None, :]
    sin = jnp.sin(ang)[:, None, :]
    xr = x[..., :ROPE_DIM].astype(jnp.float32)
    x1, x2 = xr[..., :half], xr[..., half:]
    rot = jnp.concatenate([x1 * cos - x2 * sin, x2 * cos + x1 * sin], axis=-1)
    return jnp.concatenate([rot.astype(x.dtype), x[..., ROPE_DIM:]], axis=-1)

def joint_softmax(parts):
    sizes = [p.shape[-1] for p in parts]
    p = jax.nn.softmax(jnp.concatenate(parts, axis=-1), axis=-1)
    return jnp.split(p, [int(s) for s in np.cumsum(sizes)[:-1]], axis=-1)

def select_blocks(gate, n_past):
    nb = gate.shape[-1]
    npad = max(nb, MOBA_TOPK)
    gate = jnp.pad(gate, [(0, 0)] * (gate.ndim - 1) + [(0, npad - nb)])
    gate = jnp.where(jnp.arange(npad) < n_past[:, None, None], gate, NEG)
    _, idx = lax.top_k(gate, MOBA_TOPK)
    idx = jnp.minimum(idx, max(nb - 1, 0))
    valid = jnp.arange(MOBA_TOPK) < n_past[:, None, None]
    return idx, valid

def mixer_inputs(h, pos, w_in, w_alpha_up, b_alpha):
    B, T, _ = h.shape
    z = h @ w_in
    qm, km, vm, qg, kg, vg, rg, ag = jnp.split(z, list(IN_SPLITS), axis=-1)
    qm = partial_rope(qm.reshape(B, T, MOBA_HEADS, MOBA_HEAD_DIM), pos)
    km = partial_rope(km.reshape(B, T, MOBA_HEADS, MOBA_HEAD_DIM), pos)
    vm = vm.reshape(B, T, MOBA_HEADS, MOBA_HEAD_DIM)
    qg = qg.reshape(B, T, GLA_HEADS, GLA_DK) * (GLA_DK ** -0.5)
    kg = kg.reshape(B, T, GLA_HEADS, GLA_DK)
    vg = vg.reshape(B, T, GLA_HEADS, GLA_DV)
    log_a = jax.nn.log_sigmoid((ag @ w_alpha_up + b_alpha).astype(jnp.float32)) / GLA_TAU
    return qm, km, vm, qg, kg, vg, rg, log_a.reshape(B, T, GLA_HEADS, GLA_DK)

def moba_prompt(q, k, v):
    B, S, H, dh = q.shape
    nblk = -(-S // MOBA_BLOCK)
    pad = nblk * MOBA_BLOCK - S
    kb = jnp.pad(k, ((0, 0), (0, pad), (0, 0), (0, 0))).reshape(B, nblk, MOBA_BLOCK, H, dh)
    vb = jnp.pad(v, ((0, 0), (0, pad), (0, 0), (0, 0))).reshape(B, nblk, MOBA_BLOCK, H, dh)
    kmean = jnp.mean(kb.astype(jnp.float32), axis=2)
    pos = jnp.arange(S)
    gate = jnp.einsum('bshd,bjhd->bshj', q.astype(jnp.float32), kmean)
    sel, valid = select_blocks(gate, pos // MOBA_BLOCK)
    nc = S // MOBA_QCHUNK
    qch = q.reshape(B, nc, MOBA_QCHUNK, H, dh).swapaxes(0, 1)
    selch = sel.reshape(B, nc, MOBA_QCHUNK, H, MOBA_TOPK).swapaxes(0, 1)
    valch = valid.reshape(nc, MOBA_QCHUNK, 1, MOBA_TOPK)
    bidx = jnp.arange(B)[:, None, None, None]
    hidx = jnp.arange(H)[None, None, :, None]
    lpos = jnp.arange(MOBA_BLOCK)
    scale = dh ** -0.5

    def attend(args):
        qc, selc, valc, c = args
        q0 = c * MOBA_QCHUNK
        qpos = q0 + jnp.arange(MOBA_QCHUNK)
        blk = q0 // MOBA_BLOCK
        ks = kb[bidx, selc, :, hidx, :]
        vs = vb[bidx, selc, :, hidx, :]
        kl = lax.dynamic_index_in_dim(kb, blk, axis=1, keepdims=False)
        vl = lax.dynamic_index_in_dim(vb, blk, axis=1, keepdims=False)
        s_sel = jnp.einsum('bqhd,bqhkld->bqhkl', qc, ks).astype(jnp.float32) * scale
        s_sel = jnp.where(valc[..., None], s_sel, NEG).reshape(B, MOBA_QCHUNK, H, MOBA_TOPK * MOBA_BLOCK)
        s_loc = jnp.einsum('bqhd,blhd->bqhl', qc, kl).astype(jnp.float32) * scale
        m_loc = (blk * MOBA_BLOCK + lpos)[None, :] <= qpos[:, None]
        s_loc = jnp.where(m_loc[:, None, :], s_loc, NEG)
        p_sel, p_loc = joint_softmax([s_sel, s_loc])
        p_sel = p_sel.reshape(B, MOBA_QCHUNK, H, MOBA_TOPK, MOBA_BLOCK).astype(v.dtype)
        return (jnp.einsum('bqhkl,bqhkld->bqhd', p_sel, vs)
                + jnp.einsum('bqhl,blhd->bqhd', p_loc.astype(v.dtype), vl))

    out = lax.map(attend, (qch, selch, valch, jnp.arange(nc)))
    return out.swapaxes(0, 1).reshape(B, S, H, dh)

def moba_sample(q, k_new, v_new, cache_k, cache_v, page_table):
    DB, T, H, dh = q.shape
    n_pages = page_table.shape[1]
    past = n_pages * PAGE_SIZE
    ppb = MOBA_BLOCK // PAGE_SIZE
    n_full = past // MOBA_BLOCK
    qpos = past + jnp.arange(T)
    qblk = qpos // MOBA_BLOCK
    scale = dh ** -0.5
    page_sum = jnp.sum(cache_k, axis=1, dtype=jnp.float32)
    kmean = page_sum[page_table[:, :n_full * ppb]].reshape(DB, n_full, ppb, H, dh).sum(axis=2) / MOBA_BLOCK
    gate = jnp.einsum('bthd,bjhd->bthj', q.astype(jnp.float32), kmean)
    sel, valid = select_blocks(gate, qblk)
    lp = jnp.minimum(sel[..., None] * ppb + jnp.arange(ppb), n_pages - 1)
    phys = page_table[jnp.arange(DB)[:, None, None, None, None], lp]
    hidx = jnp.arange(H)[None, None, :, None, None]
    ks = cache_k[phys, :, hidx, :].reshape(DB, T, H, MOBA_TOPK, MOBA_BLOCK, dh)
    vs = cache_v[phys, :, hidx, :].reshape(DB, T, H, MOBA_TOPK, MOBA_BLOCK, dh)
    own_lp = jnp.minimum(qblk[:, None] * ppb + jnp.arange(ppb), n_pages - 1)
    phys_own = page_table[:, own_lp]
    ko = cache_k[phys_own].reshape(DB, T, MOBA_BLOCK, H, dh)
    vo = cache_v[phys_own].reshape(DB, T, MOBA_BLOCK, H, dh)
    m_own = (qblk[:, None] * MOBA_BLOCK + jnp.arange(MOBA_BLOCK)[None, :]) < past
    tt = jnp.arange(T)
    m_new = (qblk[:, None] == qblk[None, :]) & (tt[None, :] <= tt[:, None])
    s_sel = jnp.einsum('bthd,bthkld->bthkl', q, ks).astype(jnp.float32) * scale
    s_sel = jnp.where(valid[..., None], s_sel, NEG).reshape(DB, T, H, MOBA_TOPK * MOBA_BLOCK)
    s_own = jnp.where(m_own[:, None, :], jnp.einsum('bthd,btlhd->bthl', q, ko).astype(jnp.float32) * scale, NEG)
    s_new = jnp.where(m_new[:, None, :], jnp.einsum('bthd,bshd->bths', q, k_new).astype(jnp.float32) * scale, NEG)
    p_sel, p_own, p_new = joint_softmax([s_sel, s_own, s_new])
    p_sel = p_sel.reshape(DB, T, H, MOBA_TOPK, MOBA_BLOCK).astype(vs.dtype)
    return (jnp.einsum('bthkl,bthkld->bthd', p_sel, vs)
            + jnp.einsum('bthl,btlhd->bthd', p_own.astype(vo.dtype), vo)
            + jnp.einsum('bths,bshd->bthd', p_new.astype(v_new.dtype), v_new))

def gla_chunked(q, k, v, log_a, s0):
    B, T, H, dk = q.shape
    dv = v.shape[-1]
    C = GLA_CHUNK if T % GLA_CHUNK == 0 else T
    n = T // C

    def to_chunks(a):
        return a.astype(jnp.float32).reshape(B, n, C, H, a.shape[-1]).swapaxes(0, 1)

    causal = jnp.tril(jnp.ones((C, C), dtype=bool))[None, :, :, None, None]

    def step(S, inp):
        qc, kc, vc, ac = inp
        A = jnp.cumsum(ac, axis=1)
        decay = jnp.exp(jnp.where(causal, A[:, :, None] - A[:, None, :], NEG))
        att = jnp.einsum('bthd,bshd,btshd->bths', qc, kc, decay)
        o = jnp.einsum('bths,bshv->bthv', att, vc) + jnp.einsum('bthk,bhkv->bthv', qc * jnp.exp(A), S)
        A_last = A[:, -1]
        S = jnp.exp(A_last)[..., None] * S + jnp.einsum('bshk,bshv->bhkv', kc * jnp.exp(A_last[:, None] - A), vc)
        return S, o

    S, o = lax.scan(step, s0.astype(jnp.float32), (to_chunks(q), to_chunks(k), to_chunks(v), to_chunks(log_a)))
    return o.swapaxes(0, 1).reshape(B, T, H, dv), S

def mixer_output(o_moba, o_gla, rg, g_gla_out, w_out):
    B, T = o_moba.shape[:2]
    og = rmsnorm(o_gla, g_gla_out).reshape(B, T, GLA_WIDTH) * jax.nn.silu(rg)
    return jnp.concatenate([o_moba.reshape(B, T, MOBA_WIDTH), og], axis=-1) @ w_out

def memory_kv(mem, g_mem_kv, w_mem_k, w_mem_v):
    B = mem.shape[0]
    m = rmsnorm(mem, g_mem_kv)
    mk = (m @ w_mem_k).reshape(B, MEM_LEN, MEM_HEADS, MEM_HEAD_DIM)
    mv = (m @ w_mem_v).reshape(B, MEM_LEN, MEM_HEADS, MEM_HEAD_DIM)
    return mk, mv

def memory_attend(h, mk, mv, w_mem_q, w_mem_o):
    B, T, _ = h.shape
    q = (h @ w_mem_q).reshape(B, T, MEM_HEADS, MEM_HEAD_DIM)
    s = jnp.einsum('bthd,bmhd->bhtm', q, mk).astype(jnp.float32) * (MEM_HEAD_DIM ** -0.5)
    p = jax.nn.softmax(s, axis=-1).astype(mv.dtype)
    o = jnp.einsum('bhtm,bmhd->bthd', p, mv).reshape(B, T, D_MODEL)
    return o @ w_mem_o

def peer_ffn(h, w_peer_q, peer_sub_keys, expert_u, expert_v):
    B, T, D = h.shape
    n = B * T
    chunk = PEER_TOKEN_CHUNK if n % PEER_TOKEN_CHUNK == 0 else n

    def route_and_mix(xc):
        c = xc.shape[0]
        qv = (xc @ w_peer_q).reshape(c, PEER_HEADS, 2, PEER_DQ // 2)
        s = jnp.einsum('chpd,phkd->chpk', qv, peer_sub_keys).astype(jnp.float32)
        top_s, top_i = lax.top_k(s, PEER_TOPK)
        cand_s = (top_s[:, :, 0, :, None] + top_s[:, :, 1, None, :]).reshape(c, PEER_HEADS, PEER_TOPK * PEER_TOPK)
        cand_i = (top_i[:, :, 0, :, None] * PEER_NKEYS + top_i[:, :, 1, None, :]).reshape(c, PEER_HEADS, PEER_TOPK * PEER_TOPK)
        fin_s, fin_pos = lax.top_k(cand_s, PEER_TOPK)
        eid = jnp.take_along_axis(cand_i, fin_pos, axis=-1)
        g = jax.nn.softmax(fin_s, axis=-1)
        u = expert_u[eid]
        a = jax.nn.gelu(jnp.einsum('chkd,cd->chk', u, xc).astype(jnp.float32), approximate=False)
        return jnp.einsum('chk,chkd->cd', (g * a).astype(xc.dtype), expert_v[eid])

    out = lax.map(route_and_mix, h.reshape(n // chunk, chunk, D))
    return out.reshape(B, T, D)

def decoder_layer(x, pos, moba_fn, gla_s0, mem_k, mem_v, g_mix, w_in, w_alpha_up, b_alpha, g_gla_out, w_out,
                  g_mem_q, w_mem_q, w_mem_o, g_ffn, w_peer_q, peer_sub_keys, expert_u, expert_v):
    h = rmsnorm(x, g_mix)
    qm, km, vm, qg, kg, vg, rg, log_a = mixer_inputs(h, pos, w_in, w_alpha_up, b_alpha)
    o_moba = moba_fn(qm, km, vm)
    o_gla, s_new = gla_chunked(qg, kg, vg, log_a, gla_s0)
    x = x + mixer_output(o_moba, o_gla.astype(x.dtype), rg, g_gla_out, w_out)
    x = x + memory_attend(rmsnorm(x, g_mem_q), mem_k, mem_v, w_mem_q, w_mem_o)
    x = x + peer_ffn(rmsnorm(x, g_ffn), w_peer_q, peer_sub_keys, expert_u, expert_v)
    return x, km, vm, s_new

def setup_inputs(seed: int = 0) -> dict:
    key = jax.random.key(seed)
    k = jax.random.split(key, 27)
    n_pages = PAST_LEN // PAGE_SIZE
    n_used = DEC_BATCH * n_pages
    n_pool = n_used + max(1, n_used // 4)
    L = DEPTH
    f32 = jnp.float32

    def nrm(kk, shape, scale=1.0):
        return scale * jax.random.normal(kk, shape, f32)

    def gain(kk, shape):
        return 1.0 + 0.01 * jax.random.normal(kk, shape, f32)

    return {
        'x_prompt': nrm(k[0], (BATCH, SEQ, D_MODEL)),
        'x_sample': nrm(k[1], (DEC_BATCH, DEC_SEQ, D_MODEL)),
        'cache_k': nrm(k[2], (L, n_pool, PAGE_SIZE, MOBA_HEADS, MOBA_HEAD_DIM)),
        'cache_v': nrm(k[3], (L, n_pool, PAGE_SIZE, MOBA_HEADS, MOBA_HEAD_DIM)),
        'state_gla': nrm(k[4], (L, DEC_BATCH, GLA_HEADS, GLA_DK, GLA_DV)),
        'cache_mem_k': nrm(k[5], (L, DEC_BATCH, MEM_LEN, MEM_HEADS, MEM_HEAD_DIM)),
        'cache_mem_v': nrm(k[6], (L, DEC_BATCH, MEM_LEN, MEM_HEADS, MEM_HEAD_DIM)),
        'page_table': jax.random.permutation(k[7], n_pool)[:n_used].reshape(DEC_BATCH, n_pages).astype(jnp.int32),
        'mem_prompt': nrm(k[8], (BATCH, MEM_LEN, D_MODEL)),
        'g_mix': gain(k[9], (L, D_MODEL)),
        'w_in': nrm(k[10], (L, D_MODEL, IN_COLS), D_MODEL ** -0.5),
        'w_alpha_up': nrm(k[11], (L, GLA_LOWRANK, GLA_KEY_WIDTH), GLA_LOWRANK ** -0.5),
        'b_alpha': nrm(k[12], (L, GLA_KEY_WIDTH), 0.1),
        'g_gla_out': gain(k[13], (L, GLA_DV)),
        'w_out': nrm(k[14], (L, MIX_WIDTH, D_MODEL), MIX_WIDTH ** -0.5),
        'g_mem_q': gain(k[15], (L, D_MODEL)),
        'g_mem_kv': gain(k[16], (L, D_MODEL)),
        'w_mem_q': nrm(k[17], (L, D_MODEL, D_MODEL), D_MODEL ** -0.5),
        'w_mem_k': nrm(k[18], (L, D_MODEL, D_MODEL), D_MODEL ** -0.5),
        'w_mem_v': nrm(k[19], (L, D_MODEL, D_MODEL), D_MODEL ** -0.5),
        'w_mem_o': nrm(k[20], (L, D_MODEL, D_MODEL), D_MODEL ** -0.5),
        'g_ffn': gain(k[21], (L, D_MODEL)),
        'w_peer_q': nrm(k[22], (L, D_MODEL, PEER_HEADS * PEER_DQ), D_MODEL ** -0.5),
        'peer_sub_keys': nrm(k[23], (L, 2, PEER_HEADS, PEER_NKEYS, PEER_DQ // 2), (PEER_DQ // 2) ** -0.5),
        'expert_u': nrm(k[24], (L, PEER_EXPERTS, D_MODEL), D_MODEL ** -0.5),
        'expert_v': nrm(k[25], (L, PEER_EXPERTS, D_MODEL), PEER_HEADS ** -0.5),
        'g_final': gain(k[26], (D_MODEL,)),
    }

def reference(x_prompt, x_sample, cache_k, cache_v, state_gla, cache_mem_k, cache_mem_v, page_table, mem_prompt,
              g_mix, w_in, w_alpha_up, b_alpha, g_gla_out, w_out, g_mem_q, g_mem_kv, w_mem_q, w_mem_k, w_mem_v,
              w_mem_o, g_ffn, w_peer_q, peer_sub_keys, expert_u, expert_v, g_final):
    B, S, _ = x_prompt.shape
    DB, T, _ = x_sample.shape
    past = page_table.shape[1] * PAGE_SIZE
    pos_prompt = jnp.arange(S)
    pos_sample = past + jnp.arange(T)
    xp, xs = x_prompt, x_sample
    kp_l, vp_l, sp_l, mkp_l, mvp_l, ks_l, vs_l, ss_l = [], [], [], [], [], [], [], []
    for l in range(DEPTH):
        shared = (g_mix[l], w_in[l], w_alpha_up[l], b_alpha[l], g_gla_out[l], w_out[l],
                  g_mem_q[l], w_mem_q[l], w_mem_o[l], g_ffn[l], w_peer_q[l], peer_sub_keys[l],
                  expert_u[l], expert_v[l])
        mk_p, mv_p = memory_kv(mem_prompt, g_mem_kv[l], w_mem_k[l], w_mem_v[l])
        s0 = jnp.zeros((B, GLA_HEADS, GLA_DK, GLA_DV), jnp.float32)
        xp, k_p, v_p, s_p = decoder_layer(xp, pos_prompt, moba_prompt, s0, mk_p, mv_p, *shared)
        ck, cv = cache_k[l], cache_v[l]
        xs, k_s, v_s, s_s = decoder_layer(
            xs, pos_sample, lambda q, kk, vv: moba_sample(q, kk, vv, ck, cv, page_table),
            state_gla[l], cache_mem_k[l], cache_mem_v[l], *shared)
        kp_l.append(k_p)
        vp_l.append(v_p)
        sp_l.append(s_p.astype(state_gla.dtype))
        mkp_l.append(mk_p)
        mvp_l.append(mv_p)
        ks_l.append(k_s)
        vs_l.append(v_s)
        ss_l.append(s_s.astype(state_gla.dtype))
    y_prompt = rmsnorm(xp, g_final)
    y_sample = rmsnorm(xs, g_final)
    k_prompt = jnp.stack(kp_l)
    v_prompt = jnp.stack(vp_l)
    gla_state_prompt = jnp.stack(sp_l)
    mem_k_prompt = jnp.stack(mkp_l)
    mem_v_prompt = jnp.stack(mvp_l)
    k_sample = jnp.stack(ks_l)
    v_sample = jnp.stack(vs_l)
    gla_state_sample = jnp.stack(ss_l)
    return (y_prompt, y_sample, k_prompt, v_prompt, gla_state_prompt, mem_k_prompt, mem_v_prompt,
            k_sample, v_sample, gla_state_sample)


_drawn_inputs = setup_inputs


def setup_inputs(seed=0):
    import zlib

    import numpy as np

    out = dict(_drawn_inputs(seed))
    spreads = {}
    factors = {'g_mix': 3.067,
     'g_gla_out': 4.578,
     'g_mem_q': 8.0,
     'g_mem_kv': 5.687,
     'g_ffn': 25.168,
     'g_final': 31.23}
    for name, (base, spread) in spreads.items():
        noise = np.random.default_rng([zlib.crc32(name.encode()), seed]).standard_normal(out[name].shape)
        drawn = base * np.exp(spread * noise) if base else spread * noise
        out[name] = __import__('jax').numpy.asarray(drawn.astype(out[name].dtype))
    for name, factor in factors.items():
        out[name] = (out[name] * factor).astype(out[name].dtype)
    return out
```

```python
from contextlib import ExitStack

import numpy as np

import concourse.bass as bass
from concourse import mybir

F32 = mybir.dt.float32
I32 = mybir.dt.int32
U32 = mybir.dt.uint32
ALU = mybir.AluOpType
ACT = mybir.ActivationFunctionType
AX = mybir.AxisListType

P = 128
D = 1024
KC = D // P
NP_TOK, NS_TOK = 256, 32
T = NP_TOK + NS_TOK
TW, TO = [128, 128, 32], [0, 128, 256]
NB, NT = 8, 4
MH, MD = 8, 64
NPAGE, PAGE, NPOOL = 16, 128, 160
NBLK = 8
PAST = NPAGE * PAGE
GC = 32
EPS = 1e-6
NEG = -1e30
NKEY, NEXP, PH, TOPK = 128, 128 * 128, 8, 16
NPAIR = PH * TOPK
WSLOT, GSLOT = 3, 12


CONSTS = [("ident", 128), ("rope", 48), ("causal", 512), ("newmask", 64), ("gmask", 1024), ("gmask_s", 1024),
          ("reset", T), ("bmask", 256), ("rowmask", 8), ("iota", 16), ("ones", 32)]
COFF = {}
_o = 0
for _n, _w in CONSTS:
    COFF[_n] = (_o, _w)
    _o += _w
CW = _o


def shape_constants():
    c = np.zeros((P, CW), np.float32)

    def put(name, a):
        o, w = COFF[name]
        c[:a.shape[0], o:o + w] = a.reshape(a.shape[0], w)

    p = np.arange(P)
    put("ident", np.eye(P, dtype=np.float32))
    inv = (1.0 / (np.float32(500000.0) ** (np.arange(8, dtype=np.float32) * np.float32(2.0 / 16)))).astype(np.float32)
    rope = np.zeros((P, 3, 16), np.float32)
    for i in range(3):
        pos = p + P * i if i < 2 else PAST + p % NT
        ang = pos.astype(np.float32)[:, None] * inv[None, :]
        rope[:, i, 0:8], rope[:, i, 8:16] = np.cos(ang), np.sin(ang)
    put("rope", rope)
    k = np.arange(256)
    put("causal", np.stack([np.where(k[None] <= (p + P * i)[:, None], 0, NEG) for i in range(2)], 1).astype(np.float32))
    nb, ns = np.arange(32) // NT, np.arange(32) % NT
    b4, t = p // 32, p % NT
    put("newmask", np.stack([np.where((nb[None] == (g * 4 + b4)[:, None]) & (ns[None] <= t[:, None]), 0, NEG)
                             for g in range(2)], 1).astype(np.float32))
    tt, ss = np.arange(32)[None, :, None], np.arange(32)[None, None, :]
    sp = (p % 32)[:, None, None]
    put("gmask", ((ss == sp) & (tt >= ss)).astype(np.float32))
    put("gmask_s", ((ss == sp) & (tt >= ss) & (tt // NT == ss // NT)).astype(np.float32))
    r = np.ones(T, np.float32)
    r[0:NP_TOK:GC] = 0
    r[NP_TOK::NT] = 0
    put("reset", np.tile(r, (P, 1)))
    put("bmask", np.tile((nb[None, :] == np.arange(8)[:, None]).astype(np.float32).reshape(1, 256), (P, 1)))
    put("rowmask", ((p[:, None] // NT) == np.arange(8)[None]).astype(np.float32))
    put("iota", np.tile(np.arange(16, dtype=np.float32), (P, 1)))
    put("ones", np.ones((P, 32), np.float32))
    return c


class Lane:

    def __init__(self, banks, full, free):
        self.banks, self.full, self.free = banks, full, free
        self.filled = self.taken = 0

    def open(self, pe):
        n, r = self.filled, len(self.banks)
        self.filled += 1
        if n >= r:
            pe.wait_ge(self.free, n - r + 1)
        return self.banks[n % r]

    def take(self, eng):
        self.taken += 1
        eng.wait_ge(self.full, self.taken)
        return self.banks[(self.taken - 1) % len(self.banks)]


def bc(ap, axis, n):
    a = ap.unsqueeze(axis)
    shape = list(a.shape)
    shape[axis] = n
    return a.to_broadcast(shape)


def hybrid_step(nc, x_prompt, x_sample, cache_k, cache_v, state_gla, cache_mem_k, cache_mem_v, page_table, mem_prompt,
                g_mix, w_in, w_alpha_up, b_alpha, g_gla_out, w_out, g_mem_q, g_mem_kv, w_mem_q, w_mem_k, w_mem_v,
                w_mem_o, g_ffn, w_peer_q, peer_sub_keys, expert_u, expert_v, g_final, consts,
                y_prompt, y_sample, k_prompt, v_prompt, gla_prompt, mem_k_prompt, mem_v_prompt,
                k_sample, v_sample, gla_sample):
    ctx = ExitStack()
    with ctx:
        def sb(name, shape, dt=F32):
            return ctx.enter_context(nc.sbuf_tensor(name, shape, dt))

        sems = {}

        def S(name):
            if name not in sems:
                sems[name] = ctx.enter_context(nc.semaphore(name))
            return sems[name]

        cst = sb("cst", [P, CW])

        def C(name, *dims):
            o, w = COFF[name]
            a = cst[:, o:o + w]
            if len(dims) == 2:
                a = a.rearrange("p (a b) -> p a b", b=dims[1])
            return a

        ident = C("ident")
        rope = C("rope", 3, 16)
        causal = C("causal", 2, 256)
        newmask = C("newmask", 2, 32)
        reset, iota, ones = C("reset"), C("iota"), C("ones")
        bmask = C("bmask", 8, 32)
        rowmask = C("rowmask")
        gains = sb("gains", [P, 3, KC])
        g_ffn_t = sb("g_ffn_t", [P, KC])
        g_row = sb("g_row", [P, D])
        g_gla_b = sb("g_gla_b", [P, 128])
        b_al = sb("b_al", [P, 2])
        w_al = sb("w_al", [16, 256])
        pages_ix = sb("pages_ix", [1, NB * NPAGE], I32)
        x = sb("x", [P, 3, D])
        hT = sb("hT", [P, KC, T])
        xs = sb("xs", [P, D])
        stat = sb("stat", [P, 64])
        ring = sb("ring", [P, WSLOT * KC * 512])
        wslot = [ring[:, s * 4096:(s + 1) * 4096] for s in range(WSLOT)]
        gslot = [ring[:, s * D:(s + 1) * D] for s in range(GSLOT)]
        zone = sb("zone", [P, 15 * 512])
        ARENA = 20000
        arena = sb("arena", [P, ARENA])

        class Carve:

            def __init__(self, start=0):
                self.at = start

            def __call__(self, *dims):
                n = int(np.prod(dims))
                a = arena[:, self.at:self.at + n]
                self.at += n
                assert self.at <= ARENA, self.at
                if len(dims) == 2:
                    return a.rearrange("p (a b) -> p a b", b=dims[1])
                if len(dims) == 3:
                    return a.rearrange("p (a b c) -> p a b c", b=dims[1], c=dims[2])
                if len(dims) == 4:
                    return a.rearrange("p (a b c d) -> p a b c d", b=dims[1], c=dims[2], d=dims[3])
                return a

        zq, zk, zv, zg, zr = [zone[:, j * 1536:(j + 1) * 1536].rearrange("p (a b) -> p a b", b=512) for j in range(5)]
        memkv = [zone[:, j * 2048:(j + 1) * 2048].rearrange("p (a b) -> p a b", b=D) for j in range(3)]

        ar = Carve()
        qT, kT = ar(4, T), ar(4, T)
        keep = ar.at
        gT, la, eA, qe, dk = ar(4, T), ar(2, T), ar(2, T), ar(2, T), ar(2, T)
        agT = ar(T)
        qem = ar(2, NB, 32)
        kdn = ar(3, 256)
        kdm = ar(NB, 256)
        X = [ar(32, 32), ar(32, 32)]
        masked = ar(16, 32)
        att = ar(3, 4, 32)
        St_p = ar(9, 2, 128)
        St_s = ar(NB, 2, 128)
        St_n = ar(NB, 2, 128)
        o_n = zq
        t1, t2 = xs[:, 0:T], xs[:, 512:512 + T]
        ar = Carve(keep)
        QB = ar(4, NB, 8)
        Sb = ar(8, 256)
        pT = ar(16, 128)
        Sm = ar(PAST + 32)
        sT = ar(NPAGE, 128)
        sTn, pTn = ar(128), ar(128)
        kTp = [ar(4, 128) for _ in range(4)]
        sel = ar(3, 8)
        pages = ar(12, 512)
        NSLOT = 12
        ar = Carve()
        q2T = ar(KC, T)
        memx = ar(2, D)
        mkn, mvn = ar(2, D), ar(2, D)
        mkT = ar(KC, 256)
        mkTs = [ar(KC, 256) for _ in range(2)]
        S2 = ar(4, 256)
        p2T = ar(8, 128)
        sT2 = ar(2, 128)
        ar = Carve()
        qvT = ar(16, T)
        skT = ar(16, 128)
        xn = ar(3, D)
        sc, sc2 = ar(4, 128), ar(4, 128)
        ts = ar(16, 16)
        tif = ar(16, 16)
        cand, cand2 = ar(256), ar(256)
        fs = ar(PH, TOPK)
        pa, pb = ar(PH, TOPK), ar(PH, TOPK)
        i1, i2 = ar(PH, TOPK), ar(PH, TOPK)
        gate = ar(3, NPAIR)
        eidf = ar(3, NPAIR)
        coefT = ar(T)
        hot = zone[:, 0:2048].rearrange("p (a b c) -> p a b c", b=TOPK, c=TOPK)
        accT = zone[:, 2048:3072].rearrange("p (a b) -> p a b", b=128)
        xns = zone[:, 3072:4096]
        skn = zone[:, 4096:6144].rearrange("p (a b) -> p a b", b=128)
        ti = sb("ti", [P, 16, 16], U32)
        fpos = sb("fpos", [P, PH, TOPK], U32)
        eid = sb("eid", [P, 3, NPAIR], I32)
        eid_s = sb("eid_s", [P, 32], I32)
        eidT = sb("eidT", [P, T], I32)
        dots = sb("dots", [P, 3, NPAIR])
        dots_s = sb("dots_s", [P, 32])
        sel_ix = sb("sel_ix", [P, 8], U32)

        bank = [ctx.enter_context(nc.psum_tensor(f"bank{j}", [P, 512], F32)) for j in range(8)]
        dl = Lane(bank[0:4], S("d_full"), S("d_free"))
        al = Lane(bank[4:6], S("a_full"), S("a_free"))
        el = Lane(bank[6:8], S("e_full"), S("e_free"))

        def wsrc(w, c0, n):
            return w[0, :, c0:c0 + n].rearrange("(c p) n -> p c n", p=P)

        stream = [wsrc(w_in, 0, 512), wsrc(w_in, 512, 512), wsrc(w_in, 1536, 512), wsrc(w_in, 3072, 16),
                  wsrc(w_in, 1024, 512), wsrc(w_in, 2048, 512), wsrc(w_in, 2560, 512)]
        stream += [wsrc(w_out, 512 * j, 512) for j in range(2)]
        stream += [wsrc(w_mem_q, 512 * j, 512) for j in range(2)]
        stream += [wsrc(w_mem_k, 512 * j, 512) for j in range(2)]
        stream += [wsrc(w_mem_v, 512 * j, 512) for j in range(2)]
        stream += [wsrc(w_mem_o, 512 * j, 512) for j in range(2)]
        stream += [wsrc(w_peer_q, 0, 2048)[:, :, 512 * j:512 * j + 512] for j in range(4)]
        roots = []
        w_done = []
        page_done, mem_done, gather_done = [], [], []
        u_total = {}

        block = ctx.enter_context(nc.Block())

        @block.tensor
        def _(pe):
            seen = {}

            def need(name, n=1):
                seen[name] = seen.get(name, 0) + n
                pe.wait_ge(S(name), seen[name])

            def weights(n):
                k = len(w_done)
                pe.wait_ge(S(f"w{k % WSLOT}"), 16 * (k // WSLOT + 1))
                return wslot[k % WSLOT][:, 0:KC * n].rearrange("p (c n) -> p c n", c=KC)

            def natural(src, lane, n=512, tiles=(0, 1, 2)):
                w = weights(n)
                for i in tiles:
                    o = lane.open(pe)
                    for c in range(KC):
                        mm = pe.matmul(o[0:TW[i], 0:n], src[:, c, TO[i]:TO[i] + TW[i]], w[:, c, :],
                                       start=(c == 0), stop=(c == KC - 1))
                    mm.then_inc(lane.full, 1)
                w_done.append((lane.full, lane.filled))

            def transposed(src, lane, n=512):
                w = weights(n)
                for f in range(0, n, P):
                    m = min(P, n - f)
                    o = lane.open(pe)
                    for c in range(KC):
                        mm = pe.matmul(o[0:m, 0:T], w[:, c, f:f + m], src[:, c, :], start=(c == 0), stop=(c == KC - 1))
                    mm.then_inc(lane.full, 1)
                w_done.append((lane.full, lane.filled))

            def turn(blocks, rows, lane=None):
                lane = lane or dl
                o = lane.open(pe)
                for j, b in enumerate(blocks):
                    mm = pe.transpose(o[0:b.shape[1], j * 128:j * 128 + rows], b, ident[0:rows, 0:rows])
                mm.then_inc(lane.full, 1)

            def norm_turns(tiles):
                for i in tiles:
                    need("xs_ready")
                    for j in range(2):
                        turn([xs[0:TW[i], (4 * j + q) * P:(4 * j + q + 1) * P] for q in range(4)], TW[i])

            pe.wait_ge(S("consts"), 16)
            norm_turns((0, 1, 2))
            need("hT_ready", 6)
            natural(hT, al)
            natural(hT, al)
            transposed(hT, al)
            transposed(hT, al, 16)
            natural(hT, al)
            natural(hT, al)
            natural(hT, al)
            need("rope_done", 3)
            for i in range(3):
                for z in (zq, zk):
                    turn([z[0:TW[i], i, q * P:(q + 1) * P] for q in range(4)], TW[i])
            need("gT_ready", 5)
            pe.wait_ge(S("small"), 16 * 7)
            for f in range(2):
                o = dl.open(pe)
                pe.matmul(o[:, 0:T], w_al[:, f * P:(f + 1) * P], agT[0:16, :], start=True, stop=True).then_inc(dl.full, 1)
            need("kd_ready", 1)
            for i in range(3):
                turn([dk[:, f, TO[i]:TO[i] + TW[i]] for f in range(2)], P)
            need("kdn_ready", 3)
            need("z_ready", 9)
            for c in range(NP_TOK // GC):
                i, q = c // 4, 32 * (c % 4)
                o = dl.open(pe)
                for f in range(2):
                    mm = pe.matmul(o[:, f * 256:(f + 1) * 256], kdn[q:q + 32, i, f * P:(f + 1) * P],
                                   zg[q:q + 32, i, f * 256:(f + 1) * 256], start=True, stop=True)
                mm.then_inc(dl.full, 1)
            need("kdm_ready", 1)
            for b in range(NB):
                o = dl.open(pe)
                for f in range(2):
                    mm = pe.matmul(o[:, f * 256:(f + 1) * 256], kdm[0:32, b, f * P:(f + 1) * P],
                                   zg[0:32, 2, f * 256:(f + 1) * 256], start=True, stop=True)
                mm.then_inc(dl.full, 1)
            for i in range(3):
                n = 4 if i < 2 else 1
                for f in range(2):
                    os = [dl.open(pe) for _ in range(4)]
                    for c in range(n):
                        need("pairs_ready")
                        buf = X[c % 2]
                        for r in range(2):
                            for h in range(2):
                                mm = pe.matmul(os[2 * r + h][32 * c:32 * c + 32, :], ones[64 * r:64 * r + 64, :],
                                               buf[64 * r:64 * r + 64, 16 * h:16 * h + 16, :], start=True, stop=True)
                                if c == n - 1:
                                    mm.then_inc(dl.full, 1)
                        if c < n - 1:
                            mm.then_inc(S("pairs_used"), 1)
            need("att_ready", 24)
            need("qe_ready", 1)
            need("state_ready", 8)
            pe.wait_ge(S("state_in"), 32)
            for i in range(3):
                for r in range(2):
                    o = dl.open(pe)
                    kr = slice(64 * r, 64 * r + 64)
                    for f in range(2):
                        h = 2 * f + r
                        to, cols = slice(f * P, (f + 1) * P), slice(h * P, (h + 1) * P)
                        for q in range(4 if i < 2 else 1):
                            c = 4 * i + q
                            rows = slice(32 * q, 32 * q + 32)
                            mm = pe.matmul(o[rows, to], att[rows, i, h, :], zg[rows, i, cols], start=True, stop=(c == 0),
                                           skip_group_check=True)
                        for q in range(4 if i < 2 else 0):
                            c = 4 * i + q
                            if c > 0:
                                mm = pe.matmul(o[32 * q:32 * q + 32, to], qe[kr, f, c * GC:(c + 1) * GC],
                                               St_p[kr, c, f, :], start=False, stop=True, skip_group_check=True)
                        for b in range(NB if i == 2 else 0):
                            mm = pe.matmul(o[0:32, to], qem[kr, f, b, :], St_s[kr, b, f, :],
                                           start=False, stop=(b == NB - 1), skip_group_check=True)
                    mm.then_inc(dl.full, 1)
            for i in range(3):
                need("og_ready")
                turn([o_n[0:TW[i], i, q * P:(q + 1) * P] for q in range(4)], TW[i])
            need("qkT_ready", 6)
            for i in range(2):
                for g in range(4):
                    o = dl.open(pe)
                    r = g % 2
                    for j in range(2):
                        hp = g // 2 * 2 + j
                        mm = pe.matmul(o[:, j * 256:(j + 1) * 256], qT[64 * r:64 * r + 64, hp, TO[i]:TO[i] + P],
                                       kT[64 * r:64 * r + 64, hp, 0:256], start=True, stop=True)
                    mm.then_inc(dl.full, 1)
                need("p_ready")
                for g in range(4):
                    turn([Sb[:, 2 * g + j // 2, (j % 2) * P:(j % 2 + 1) * P] for j in range(4)], P)
                need("pT_ready", 4)
                o = dl.open(pe)
                for h in range(MH):
                    for kt in range(2):
                        mm = pe.matmul(o[64 * (h % 2):64 * (h % 2) + 64, (h // 2) * P:(h // 2 + 1) * P],
                                       zv[:, kt, h * MD:(h + 1) * MD], pT[:, 2 * h + kt, :],
                                       start=(kt == 0), stop=(kt == 1), skip_group_check=True)
                mm.then_inc(dl.full, 1)
            need("QB_ready")
            np_ = 0
            nturn = 0

            def page_slot():
                nonlocal np_
                pe.wait_ge(S(f"page{np_ % NSLOT}"), 16 * (np_ // NSLOT + 1))
                np_ += 1
                return pages[:, (np_ - 1) % NSLOT, :]

            for g in range(2):
                for b4 in range(4):
                    b = 4 * g + b4
                    so = el.open(pe)

                    def page_scores(j):
                        need("kTd" if j % 2 == 0 else "kTa")
                        for hp in range(4):
                            mm = pe.matmul(so[:, j * 32 + hp * 8:j * 32 + hp * 8 + 8], kTp[j % 4][:, hp, :], QB[:, hp, b, :],
                                           start=True, stop=True)
                        return mm

                    for j in range(NPAGE):
                        kp = page_slot()
                        lane = dl if j % 2 == 0 else al
                        turn([kp[:, q * P:(q + 1) * P] for q in range(4)], P, lane)
                        page_done.append((lane.full, lane.filled))
                        if j:
                            page_scores(j - 1)
                    page_scores(NPAGE - 1).then_inc(el.full, 1)
                o = dl.open(pe)
                for hp in range(4):
                    mm = pe.matmul(o[0:32, 0:128].rearrange("p (b x) -> p b x", b=4)[:, :, hp * 8:hp * 8 + 8],
                                   kT[:, hp, NP_TOK:T], QB[:, hp, 4 * g:4 * g + 4, :], start=True, stop=True)
                mm.then_inc(dl.full, 1)
                need("sT_ready", 4)
                for m in range(4):
                    turn([sT[:, 4 * m + j, :] for j in range(4)], P)
                need("sTn_ready")
                turn([sTn[0:32, :]], 32)
                need("ps_ready")
                for m in range(4):
                    turn([Sm[:, (4 * m + j) * P:(4 * m + j + 1) * P] for j in range(4)], P)
                turn([Sm[:, PAST:PAST + 32]], P)
                need("psT_ready", 5)
                o = el.open(pe)
                for b4 in range(4):
                    for j in range(NPAGE):
                        vp = page_slot()
                        for hp in range(4):
                            c = b4 * 32 + hp * 8
                            mm = pe.matmul(o[:, c:c + 8], vp[:, hp * P:(hp + 1) * P], pT[:, j, c:c + 8],
                                           start=(b4 == 0 and j == 0 and hp == 0), stop=False, skip_group_check=True)
                        nturn += 1
                        mm.then_inc(S("v_used"), 1)
                        page_done.append((S("v_used"), nturn))
                    for hp in range(4):
                        c = b4 * 32 + hp * 8
                        mm = pe.matmul(o[:, c:c + 8], zv[0:32, 2, hp * P:(hp + 1) * P], pTn[0:32, c:c + 8],
                                       start=False, stop=(b4 == 3 and hp == 3), skip_group_check=True)
                mm.then_inc(el.full, 1)
            need("mixT_ready", 3 + 2 + 4)
            natural(hT, dl)
            natural(hT, dl)
            norm_turns((0, 1, 2))
            need("hT_ready", 6)
            transposed(hT, al)
            transposed(hT, al)
            norm_turns((0, 1))
            need("hT_ready", 4)
            for _ in range(4):
                natural(hT, al, tiles=(0, 1))
            need("mk_ready", 8)
            for i in range(2):
                for g in range(2):
                    turn([mkn[:, i, (4 * g + j) * P:(4 * g + j + 1) * P] for j in range(4)], P)
            need("mkT_ready", 4)
            need("q2T_ready", 8)
            for i in range(2):
                for g in range(2):
                    o = dl.open(pe)
                    for j in range(2):
                        for c in range(2):
                            f = 4 * g + 2 * j + c
                            mm = pe.matmul(o[:, j * 256:(j + 1) * 256], q2T[:, f, TO[i]:TO[i] + P], mkT[:, f, :],
                                           start=(c == 0), stop=(c == 1))
                    mm.then_inc(dl.full, 1)
                need("p2_ready")
                for g in range(2):
                    turn([S2[:, 2 * g + j // 2, (j % 2) * P:(j % 2 + 1) * P] for j in range(4)], P)
                need("p2T_ready", 2)
                for g in range(2):
                    o = dl.open(pe)
                    for j in range(4):
                        f = 4 * g + j
                        for kt in range(2):
                            mm = pe.matmul(o[:, j * P:(j + 1) * P], mvn[:, kt, f * P:(f + 1) * P], p2T[:, f // 2 * 2 + kt, :],
                                           start=(kt == 0), stop=(kt == 1))
                    mm.then_inc(dl.full, 1)
            so = el.open(pe)
            nm = 0
            for b in range(NB):
                pe.wait_ge(S(f"mem{nm % 3}"), 16 * (nm // 3 + 1))
                mk = memkv[nm % 3]
                nm += 1
                for kt in range(2):
                    for g in range(2):
                        turn([mk[:, kt, (4 * g + j) * P:(4 * g + j + 1) * P] for j in range(4)], P)
                mem_done.append((dl.full, dl.filled))
                need("mkTs_ready", 4)
                for kt in range(2):
                    for h in range(4):
                        for c in range(2):
                            mm = pe.matmul(so[:, kt * 128 + b * 16 + h * 4:kt * 128 + b * 16 + h * 4 + 4],
                                           mkTs[b % 2][:, 2 * h + c, kt * P:(kt + 1) * P],
                                           q2T[:, 2 * h + c, NP_TOK + 4 * b:NP_TOK + 4 * b + 4], start=(c == 0), stop=(c == 1))
            mm.then_inc(el.full, 1)
            need("sT2_ready")
            turn([sT2[:, kt, :] for kt in range(2)], P)
            need("p2_ready")
            turn([S2[:, 0, kt * P:(kt + 1) * P] for kt in range(2)], P)
            need("p2T_ready")
            o = el.open(pe)
            for b in range(NB):
                pe.wait_ge(S(f"mem{nm % 3}"), 16 * (nm // 3 + 1))
                mv = memkv[nm % 3]
                nm += 1
                for f in range(8):
                    for kt in range(2):
                        c = b * 16 + (f // 2) * 4
                        mm = pe.matmul(o[:, f * 32 + b * 4:f * 32 + b * 4 + 4], mv[:, kt, f * P:(f + 1) * P],
                                       p2T[:, kt, c:c + 4], start=(kt == 0), stop=(kt == 1))
                if b < NB - 1:
                    mm.then_inc(S("mv_used"), 1)
                    mem_done.append((S("mv_used"), b + 1))
            mm.then_inc(el.full, 1)
            need("o2T_ready", 5)
            natural(hT, dl)
            natural(hT, dl)
            norm_turns((0, 1, 2))
            need("hT_ready", 6)
            for _ in range(4):
                transposed(hT, al)
            pe.wait_ge(S("subkeys"), 32)
            for g in range(4):
                turn([skn[:, 4 * g + j, :] for j in range(4)], P)
            need("skT_ready", 4)
            need("qvT_ready", 16)
            for i in range(3):
                for g in range(4):
                    o = dl.open(pe)
                    for j in range(4):
                        f = 4 * g + j
                        mm = pe.matmul(o[0:TW[i], j * P:(j + 1) * P], qvT[:, f, TO[i]:TO[i] + TW[i]],
                                       skT[:, (f % 2) * PH + f // 2, :], start=True, stop=True)
                    mm.then_inc(dl.full, 1)
                need("eid_ready")
                turn([eidf[0:TW[i], i, :]], TW[i])
            n_v = 0
            n_u = 128 + 128 + 32
            for i in range(3):
                need("coef_ready")
                turn([gate[0:TW[i], i, :]], TW[i])
            for i in range(3):
                need("coefT_ready")
                oo = [el.open(pe), el.open(pe)]
                for t in range(TW[i]):
                    n = n_u + n_v
                    pe.wait_ge(S(f"g{n % GSLOT}"), 16 * (n // GSLOT + 1))
                    n_v += 1
                    for f in range(8):
                        c = (f % 4) * 128 + t
                        mm = pe.matmul(oo[f // 4][:, c:c + 1], gslot[n % GSLOT][:, f * P:(f + 1) * P],
                                       coefT[:, TO[i] + t:TO[i] + t + 1], start=True, stop=True)
                        if t == TW[i] - 1 and f in (3, 7):
                            mm.then_inc(el.full, 1)
                    if t < TW[i] - 1:
                        u_total["v"] = u_total.get("v", 0) + 1
                        mm.then_inc(S("vrow_used"), 1)
                        gather_done.append((S("vrow_used"), u_total["v"]))
                    else:
                        gather_done.append((el.full, el.filled))
                need("accT_ready", 2)
                for g in range(2):
                    o = dl.open(pe)
                    for j in range(4):
                        mm = pe.transpose(o[0:TW[i], j * P:(j + 1) * P], accT[:, 4 * g + j, 0:TW[i]], ident)
                    mm.then_inc(dl.full, 1)

        @block.vector
        def _(v):
            counts = {}

            def link(ins, name="v_chain"):
                counts[name] = counts.get(name, 0) + 1
                ins.then_inc(S(name), 1)
                v.wait_ge(S(name), counts[name])

            def freed(ins, lane):
                ins.then_inc(lane.free, 1)
                v.wait_ge(lane.free, lane.taken)

            seen = {}

            def need(name, n=1):
                seen[name] = seen.get(name, 0) + n
                v.wait_ge(S(name), seen[name])

            def signal(name):
                link(v.memset(stat[:, 63:64], 0.0), name)

            def rsqrt_mean(dst, src, n):
                link(v.tensor_scalar(dst, src, 1.0 / n, EPS, ALU.mult, ALU.add), "to_sqrt")
                roots.append(dst)
                need("sqrt_done")
                link(v.reciprocal(dst, dst))

            def norm(src, w, name="xs_ready"):
                link(v.tensor_tensor_reduce(xs[0:w, :], src, src, 1.0, 0.0, ALU.mult, ALU.add, stat[0:w, 0:1]))
                rsqrt_mean(stat[0:w, 1:2], stat[0:w, 0:1], D)
                link(v.tensor_scalar(xs[0:w, :], src, stat[0:w, 1:2], None, ALU.mult), name)

            def norm_stage(src, gain, tiles, after=None):
                for i in tiles:
                    norm(src[0:TW[i], i, :], TW[i])
                    if after:
                        after(i)
                    for j in range(2):
                        o = dl.take(v)[:, :].rearrange("p (a b) -> p a b", b=128)[:, :, 0:TW[i]]
                        link(v.tensor_tensor(hT[:, 4 * j:4 * j + 4, TO[i]:TO[i] + TW[i]], o,
                                             bc(gain[:, 4 * j:4 * j + 4], 2, TW[i]), ALU.mult), "hT_ready")
                        freed(v.memset(stat[:, 62:63], 0.0), dl)

            def empty(dst, src_of, name, lane=None, op=None):
                lane = lane or dl
                o = lane.take(v)
                link(op(dst, src_of(o)) if op else v.tensor_copy(dst, src_of(o)), name)
                freed(v.memset(stat[:, 62:63], 0.0), lane)

            def as4(o, n=4, w=128):
                return o[:, 0:n * 128].rearrange("p (a b) -> p a b", b=128)[:, :, 0:w]

            def softmax(buf, heads, name):
                b = buf[:, 0:heads, :]
                m = stat[:, 2:2 + heads]
                link(v.tensor_reduce(m, b, AX.X, ALU.max))
                link(v.tensor_tensor(b, b, bc(m, 2, 256), ALU.subtract), "to_exp")
                need("exp_done")
                link(v.tensor_reduce(m, b, AX.X, ALU.add))
                link(v.reciprocal(m, m))
                link(v.tensor_tensor(b, b, bc(m, 2, 256), ALU.mult), name)

            v.wait_ge(S("consts"), 16)
            v.wait_ge(S("small"), 16 * 7)
            v.wait_ge(S("x_in"), 48)
            norm_stage(x, gains[:, 0, :], (0, 1, 2))
            need("qk_ready", 6)
            rt = [xs[:, 64 * j:64 * j + 64].rearrange("p (h d) -> p h d", h=8) for j in range(4)]
            for i in range(3):
                w = TW[i]
                for n, z in enumerate((zq, zk)):
                    zz = z[0:w, i, :].rearrange("p (h d) -> p h d", h=8)
                    x1, x2 = zz[:, :, 0:8], zz[:, :, 8:16]
                    co, si = bc(rope[0:w, i, 0:8], 1, 8), bc(rope[0:w, i, 8:16], 1, 8)
                    a = [r[0:w] for r in rt]
                    link(v.tensor_tensor(a[0], x1, co, ALU.mult))
                    link(v.tensor_tensor(a[1], x2, si, ALU.mult))
                    link(v.tensor_tensor(a[2], x2, co, ALU.mult))
                    link(v.tensor_tensor(a[3], x1, si, ALU.mult))
                    link(v.tensor_tensor(x1, a[0], a[1], ALU.subtract))
                    link(v.tensor_tensor(x2, a[2], a[3], ALU.add), "rope_done" if n else "v_chain")
            for i in range(3):
                for z in (qT, kT):
                    empty(z[:, :, TO[i]:TO[i] + TW[i]], lambda o: as4(o, 4, TW[i]), "qkT_ready")
            for f in range(2):
                empty(t1, lambda o: o[:, 0:T], "v_chain",
                      op=lambda d, s: v.tensor_scalar(d, s, b_al[:, f:f + 1], None, ALU.add))
                link(v.tensor_scalar(t2, t1, -1.0, None, ALU.mult))
                link(v.tensor_scalar(la[:, f, :], t1, 0.0, None, ALU.min))
                link(v.tensor_tensor(t1, t1, t2, ALU.min), "to_log1p")
                need("log1p_done")
                link(v.tensor_tensor(la[:, f, :], la[:, f, :], t1, ALU.subtract))
                link(v.tensor_scalar(la[:, f, :], la[:, f, :], 1.0 / 16, None, ALU.mult))
                link(v.tensor_tensor_scan(t2, reset, la[:, f, :], 0.0, ALU.mult, ALU.add))
                link(v.tensor_copy(la[:, f, :], t2))
            for f in range(2):
                for lo, n, c in ((0, 8, GC), (NP_TOK, NB, NT)):
                    A = la[:, f, lo:lo + n * c].rearrange("p (a b) -> p a b", b=c)
                    link(v.tensor_tensor(dk[:, f, lo:lo + n * c].rearrange("p (a b) -> p a b", b=c),
                                         A[:, :, c - 1:c].to_broadcast([P, n, c]), A, ALU.subtract))
            signal("A_ready")
            need("eA_done")
            link(v.tensor_tensor(dk, dk, gT[:, 2:4, :], ALU.mult), "kd_ready")
            link(v.tensor_tensor(qe, eA, gT[:, 0:2, :], ALU.mult))
            for f in range(2):
                link(v.tensor_tensor(qem[:, f, :, :], bc(qe[:, f, NP_TOK:T], 1, NB), bmask, ALU.mult))
            signal("qe_ready")
            for i in range(3):
                empty(kdn[0:TW[i], i, :], lambda o: o[0:TW[i], 0:256], "kdn_ready")
            link(v.tensor_tensor(kdm[0:32, :, :], bc(kdn[0:32, 2, :], 1, NB), bc(rowmask[0:32, :], 2, 256), ALU.mult),
                 "kdm_ready")
            for c in range(NP_TOK // GC):
                o = dl.take(v)
                for f in range(2):
                    for r in range(2):
                        rr = slice(64 * r, 64 * r + 64)
                        u = o[rr, f * 256 + r * 128:f * 256 + r * 128 + 128]
                        if c == 0:
                            link(v.tensor_copy(St_p[rr, 1, f, :], u))
                        else:
                            link(v.scalar_tensor_tensor(St_p[rr, c + 1, f, :], St_p[rr, c, f, :],
                                                        eA[rr, f, c * GC + GC - 1:c * GC + GC], u, ALU.mult, ALU.add))
                signal("state_ready")
                freed(v.memset(stat[:, 62:63], 0.0), dl)
            v.wait_ge(S("state_in"), 32)
            for b in range(NB):
                o = dl.take(v)
                for f in range(2):
                    for r in range(2):
                        rr = slice(64 * r, 64 * r + 64)
                        a = NP_TOK + b * NT + NT - 1
                        link(v.scalar_tensor_tensor(St_n[rr, b, f, :], St_s[rr, b, f, :], eA[rr, f, a:a + 1],
                                                    o[rr, f * 256 + r * 128:f * 256 + r * 128 + 128], ALU.mult, ALU.add))
                freed(v.memset(stat[:, 62:63], 0.0), dl)
            signal("newstate_ready")
            used = 0
            for i in range(3):
                n = 4 if i < 2 else 1
                for f in range(2):
                    for c in range(n):
                        buf = X[c % 2]
                        if c >= 2:
                            v.wait_ge(S("pairs_used"), used + c - 1)
                        s0 = TO[i] + c * GC
                        A, q, k = la[:, f, s0:s0 + 32], gT[:, f, s0:s0 + 32], gT[:, 2 + f, s0:s0 + 32]
                        link(v.tensor_tensor(buf, bc(A, 2, 32), bc(A, 1, 32), ALU.subtract))
                        link(v.tensor_scalar(buf, buf, 0.0, None, ALU.min), "to_decay")
                        need("decay_done")
                        link(v.tensor_tensor(buf, buf, bc(k, 1, 32), ALU.mult))
                        link(v.tensor_tensor(buf, buf, bc(q, 2, 32), ALU.mult), "pairs_ready")
                    used += n - 1
                    w = TW[i]
                    gm = C("gmask", 32, 32) if i < 2 else C("gmask_s", 32, 32)
                    for r in range(2):
                        for h in range(2):
                            o = dl.take(v)[0:w, :].rearrange("p (a b) -> p a b", b=32)
                            link(v.tensor_tensor(masked[0:w], o, gm[0:w, 16 * h:16 * h + 16, :], ALU.mult))
                            freed(v.memset(stat[:, 62:63], 0.0), dl)
                            link(v.tensor_reduce(att[0:w, i, 2 * f + r, 16 * h:16 * h + 16], masked[0:w], AX.X, ALU.add),
                                 "att_ready")
            for i in range(3):
                w = TW[i]
                for r in range(2):
                    empty(o_n[0:w, i, :].rearrange("p (f r d) -> p r f d", r=2, d=128)[:, r],
                          lambda o: o[0:w, 0:256].rearrange("p (f d) -> p f d", d=128), "v_chain")
                oo = o_n[0:w, i, :].rearrange("p (h d) -> p h d", h=4)
                m = stat[0:w, 2:6]
                sq = xs[0:w, 0:512].rearrange("p (h d) -> p h d", h=4)
                link(v.tensor_tensor(sq, oo, oo, ALU.mult))
                link(v.tensor_reduce(m, sq, AX.X, ALU.add))
                rsqrt_mean(m, m, 128)
                link(v.tensor_tensor(oo, oo, bc(m, 2, 128), ALU.mult))
                link(v.tensor_tensor(oo, oo, bc(g_gla_b[0:w, :], 1, 4), ALU.mult))
                if i == 0:
                    v.wait_ge(S("z_ready"), 9)
                link(v.tensor_tensor(o_n[0:w, i, :], o_n[0:w, i, :], zr[0:w, i, :], ALU.mult), "og_ready")
            for i in range(3):
                empty(hT[:, 4:8, TO[i]:TO[i] + TW[i]], lambda o: as4(o, 4, TW[i]), "mixT_ready")
            v.wait_ge(S("stored1"), 16 * 4)
            link(v.memset(QB, 0.0))
            for r in range(2):
                rr = slice(64 * r, 64 * r + 64)
                for hp in range(4):
                    link(v.tensor_copy(QB[rr, hp, :, 4 * r:4 * r + 4],
                                       qT[rr, hp, NP_TOK:T].rearrange("p (b t) -> p b t", t=4)))
            signal("QB_ready")
            for i in range(2):
                for g in range(4):
                    h = g // 2 * 4 + g % 2
                    empty(Sb[:, h:h + 3:2, :], lambda o: o[:, :].rearrange("p (a b) -> p a b", b=256), "v_chain",
                          op=lambda d, s: v.scalar_tensor_tensor(d, s, MD ** -0.5, bc(causal[:, i, :], 1, 2),
                                                                 ALU.mult, ALU.add))
                softmax(Sb, 8, "p_ready")
                for g in range(4):
                    empty(pT[:, 4 * g:4 * g + 4, :], as4, "pT_ready")
                empty(hT[:, 0:4, TO[i]:TO[i] + P], as4, "mixT_ready")
            for g in range(2):
                for b4 in range(4):
                    for j in range(0, NPAGE, 2):
                        empty(kTp[j % 4], as4, "kTd")
                    empty(sT[:, :, 32 * b4:32 * b4 + 32], lambda o: o[:, :].rearrange("p (a b) -> p a b", b=32),
                          "sT_ready", el)
                empty(sTn[0:32, :], lambda o: o[0:32, 0:128], "sTn_ready")
                for m in range(4):
                    empty(Sm[:, 512 * m:512 * m + 512], lambda o: o[:, :], "v_chain",
                          op=lambda d, s: v.tensor_scalar(d, s, MD ** -0.5, None, ALU.mult))
                empty(Sm[:, PAST:PAST + 32], lambda o: o[:, 0:32], "v_chain",
                      op=lambda d, s: v.scalar_tensor_tensor(d, s, MD ** -0.5, newmask[:, g, :], ALU.mult, ALU.add))
                past = Sm[:, 0:PAST].rearrange("p (a b) -> p a b", b=256)
                gt, top, pen = stat[:, 8:16], stat[:, 16:24], stat[:, 24:32]
                link(v.tensor_reduce(gt, past, AX.X, ALU.add))
                link(v.max(top, gt))
                link(v.max_index(sel_ix[:, :], top, gt))
                link(v.tensor_copy(top, sel_ix[:, :]))
                link(v.tensor_tensor(sel, bc(iota[:, 0:8], 1, 3), bc(top[:, 0:3], 2, 8), ALU.is_equal))
                link(v.tensor_reduce(pen, sel.rearrange("p a b -> p b a"), AX.X, ALU.add))
                link(v.tensor_scalar(pen, pen, 1.0, -NEG, ALU.subtract, ALU.mult))
                link(v.tensor_tensor(past, past, bc(pen, 2, 256), ALU.add))
                m = stat[:, 32:33]
                link(v.tensor_reduce(m, Sm, AX.X, ALU.max))
                link(v.tensor_scalar(m, m, -1.0, None, ALU.mult), "to_exps")
                need("exps_done")
                link(v.reciprocal(stat[:, 34:35], stat[:, 33:34]))
                link(v.tensor_scalar(Sm, Sm, stat[:, 34:35], None, ALU.mult), "ps_ready")
                for k in range(4):
                    empty(pT[:, 4 * k:4 * k + 4, :], as4, "psT_ready")
                empty(pTn[0:32, :], lambda o: o[0:32, 0:128], "psT_ready")
                o = el.take(v)[:, 0:128].rearrange("p (b h t) -> p h b t", b=4, h=4)
                for r in range(2):
                    rr = slice(64 * r, 64 * r + 64)
                    dst = hT[rr, 0:4, NP_TOK + 16 * g:NP_TOK + 16 * g + 16].rearrange("p h (b t) -> p h b t", t=4)
                    link(v.tensor_copy(dst, o[rr, :, :, 4 * r:4 * r + 4]), "mixT_ready")
                freed(v.memset(stat[:, 62:63], 0.0), el)

            def residual():
                for c in range(2):
                    for i in range(3):
                        d = x[0:TW[i], i, 512 * c:512 * c + 512]
                        empty(d, lambda o: o[0:TW[i], :], "v_chain",
                              op=lambda d, s: v.tensor_tensor(d, d, s, ALU.add))

            residual()
            norm_stage(x, gains[:, 1, :], (0, 1, 2))
            need("q2T_ready", 8)
            v.wait_ge(S("mem_in"), 32)
            norm_stage(memx, gains[:, 2, :], (0, 1))
            for i in range(2):
                for g in range(2):
                    empty(mkT[:, 4 * g:4 * g + 4, i * P:(i + 1) * P], as4, "mkT_ready")
            for i in range(2):
                for g in range(2):
                    empty(S2[:, 2 * g:2 * g + 2, :], lambda o: o[:, :].rearrange("p (a b) -> p a b", b=256), "v_chain",
                          op=lambda d, s: v.tensor_scalar(d, s, 1.0 / 16, None, ALU.mult))
                softmax(S2, 4, "p2_ready")
                for g in range(2):
                    empty(p2T[:, 4 * g:4 * g + 4, :], as4, "p2T_ready")
                for g in range(2):
                    empty(hT[:, 4 * g:4 * g + 4, TO[i]:TO[i] + P], as4, "o2T_ready")
            for b in range(NB):
                for kt in range(2):
                    for g in range(2):
                        empty(mkTs[b % 2][:, 4 * g:4 * g + 4, kt * P:(kt + 1) * P], as4, "mkTs_ready")
            empty(sT2, lambda o: as4(o, 2), "sT2_ready", el)
            empty(S2[:, 0, :], lambda o: o[:, 0:256], "v_chain",
                  op=lambda d, s: v.tensor_scalar(d, s, 1.0 / 16, None, ALU.mult))
            softmax(S2, 1, "p2_ready")
            empty(p2T[:, 0:2, :], lambda o: as4(o, 2), "p2T_ready")
            empty(hT[:, :, NP_TOK:T], lambda o: o[:, 0:256].rearrange("p (a b) -> p a b", b=32), "o2T_ready", el)
            residual()
            v.wait_ge(S("stored2"), 16 * 2)
            v.wait_ge(S("g_row"), 16)

            def scaled_rows(i):
                link(v.tensor_tensor(xn[0:TW[i], i, :], xs[0:TW[i], :], g_row[0:TW[i], :], ALU.mult))

            norm_stage(x, g_ffn_t, (0, 1, 2), scaled_rows)
            for g in range(4):
                link(v.tensor_copy(xns[32 * g:32 * g + 32, :], xn[0:32, 2, :]), "g_row_used")
            for g in range(4):
                empty(skT[:, 4 * g:4 * g + 4, :], as4, "skT_ready")

            def top16(vals, spare, out_v, out_i):
                link(v.max(out_v[:, 0:8], vals))
                link(v.max_index(out_i[:, 0:8], out_v[:, 0:8], vals))
                link(v.match_replace(spare, out_v[:, 0:8], vals, -3e38))
                link(v.max(out_v[:, 8:16], spare))
                link(v.max_index(out_i[:, 8:16], out_v[:, 8:16], spare))

            for i in range(3):
                w = TW[i]
                for g in range(4):
                    empty(sc[0:w, :, :], lambda o: as4(o)[0:w], "v_chain")
                    for j in range(4):
                        f = 4 * g + j
                        top16(sc[0:w, j, :], sc2[0:w, j, :], ts[0:w, f, :], ti[0:w, f, :])
                link(v.tensor_copy(tif[0:w], ti[0:w, :, :]))
                for h in range(PH):
                    link(v.tensor_tensor(cand[0:w, :].rearrange("p (a b) -> p a b", b=16), bc(ts[0:w, 2 * h, :], 2, 16),
                                         bc(ts[0:w, 2 * h + 1, :], 1, 16), ALU.add))
                    top16(cand[0:w, :], cand2[0:w, :], fs[0:w, h, :], fpos[0:w, h, :])
                link(v.tensor_single_scalar(ti[0:w, 0:8, :], fpos[0:w], 4, ALU.logical_shift_right))
                link(v.tensor_single_scalar(ti[0:w, 8:16, :], fpos[0:w], 15, ALU.bitwise_and))
                link(v.tensor_copy(pa[0:w], ti[0:w, 0:8, :]))
                link(v.tensor_copy(pb[0:w], ti[0:w, 8:16, :]))
                for half, (pos, key) in enumerate(((pa, i1), (pb, i2))):
                    for h in range(PH):
                        link(v.tensor_tensor(hot[0:w, h], bc(iota[0:w, :], 1, 16), bc(pos[0:w, h, :], 2, 16), ALU.is_equal))
                        link(v.tensor_tensor(hot[0:w, h], hot[0:w, h], bc(tif[0:w, 2 * h + half, :], 1, 16), ALU.mult))
                    link(v.tensor_reduce(key[0:w], hot[0:w], AX.X, ALU.add))
                ef = eidf[0:w, i, :].rearrange("p (h k) -> p h k", h=PH)
                link(v.scalar_tensor_tensor(ef, i1[0:w], float(NKEY), i2[0:w], ALU.mult, ALU.add))
                link(v.tensor_copy(eid[0:w, i, :], eidf[0:w, i, :]), "eid_ready")
                if i == 2:
                    for g in range(4):
                        link(v.tensor_copy(eid_s[32 * g:32 * g + 32, :], eid[0:32, 2, 32 * g:32 * g + 32]), "eid_s_ready")
                gg = gate[0:w, i, :].rearrange("p (h k) -> p h k", h=PH)
                m = stat[0:w, 40:48]
                link(v.tensor_tensor(gg, fs[0:w], fs[0:w, :, 0:1].to_broadcast([w, PH, TOPK]), ALU.subtract), "to_exp")
                need("exp_done")
                link(v.tensor_reduce(m, gg, AX.X, ALU.add))
                link(v.reciprocal(m, m))
                link(v.tensor_tensor(gg, gg, bc(m, 2, 16), ALU.mult))
                empty(eidT[:, TO[i]:TO[i] + w], lambda o: o[:, 0:w], "eidT_ready")
            n = 0
            for i in range(3):
                w, m = (TW[i], NPAIR) if i < 2 else (P, 32)
                for j in range(m):
                    v.wait_ge(S(f"g{n % GSLOT}"), 16 * (n // GSLOT + 1))
                    row = gslot[n % GSLOT]
                    dst, xr = (dots[:, i, j:j + 1], xn[:, i, :]) if i < 2 else (dots_s[:, j:j + 1], xns)
                    link(v.tensor_tensor_reduce(row, row, xr, 1.0, 0.0, ALU.mult, ALU.add, dst), "dot_done")
                    n += 1
                if i == 2:
                    for g in range(4):
                        link(v.tensor_copy(dots[0:32, 2, 32 * g:32 * g + 32], dots_s[32 * g:32 * g + 32, :]))
                signal("to_gelu")
                need("gelu_done")
                w = TW[i]
                link(v.tensor_tensor(gate[0:w, i, :], gate[0:w, i, :], dots[0:w, i, :], ALU.mult), "coef_ready")
                empty(coefT[:, TO[i]:TO[i] + w], lambda o: o[:, 0:w], "coefT_ready")
            v.wait_ge(S("g_row"), 32)
            for i in range(3):
                w = TW[i]
                for g in range(2):
                    empty(accT[:, 4 * g:4 * g + 4, 0:w], lambda o: as4(o, 4, w), "accT_ready", el)
                for g in range(2):
                    empty(x[0:w, i, 512 * g:512 * g + 512], lambda o: o[0:w, :], "v_chain",
                          op=lambda d, s: v.tensor_tensor(d, d, s, ALU.add))
                norm(x[0:w, i, :], w, "v_chain")
                link(v.tensor_tensor(x[0:w, i, :], xs[0:w, :], g_row[0:w, :], ALU.mult), "y_ready")

        @block.scalar
        def _(a):
            counts, seen = {}, {}

            def link(ins, name="a_chain"):
                counts[name] = counts.get(name, 0) + 1
                ins.then_inc(S(name), 1)
                a.wait_ge(S(name), counts[name])

            def need(name, n=1):
                seen[name] = seen.get(name, 0) + n
                a.wait_ge(S(name), seen[name])

            def empty(dst, src_of, name, scale=1.0, func=ACT.Copy):
                o = al.take(a)
                link(a.activation(dst, src_of(o), func, scale=scale), name)
                link(a.activation(junk, junk, ACT.Copy), "a_free")

            junk = sb("junk", [1, 1])[:, :]
            a.wait_ge(S("consts"), 16)
            link(a.activation(junk, cst[0:1, 0:1], ACT.Copy))

            def square_roots(n):
                for _ in range(n):
                    r = roots[seen.get("to_sqrt", 0)]
                    need("to_sqrt")
                    link(a.activation(r, r, ACT.Sqrt), "sqrt_done")

            square_roots(3)
            for z in (zq, zk):
                for i in range(3):
                    empty(z[0:TW[i], i, :], lambda o: o[0:TW[i], :], "qk_ready")
            for f in range(4):
                empty(gT[:, f, :], lambda o: o[:, 0:T], "gT_ready", scale=0.125 if f < 2 else 1.0)
            empty(agT[0:16, :], lambda o: o[0:16, 0:T], "gT_ready")
            for z in (zv, zg, zr):
                for i in range(3):
                    empty(z[0:TW[i], i, :], lambda o: o[0:TW[i], :], "z_ready", func=ACT.Silu if z is zr else ACT.Copy)
            for f in range(2):
                need("to_log1p")
                link(a.activation(t1, t1, ACT.Exp))
                link(a.activation(t1, t1, ACT.Ln, bias=1.0), "log1p_done")
            need("A_ready")
            link(a.activation(eA, la, ACT.Exp))
            link(a.activation(dk, dk, ACT.Exp), "eA_done")
            for c in range(18):
                need("to_decay")
                buf = X[c % 4 % 2 if c < 16 else 0]
                link(a.activation(buf, buf, ACT.Exp), "decay_done")
            square_roots(3)
            for i in range(2):
                need("to_exp")
                link(a.activation(Sb, Sb, ACT.Exp), "exp_done")
            for g in range(2):
                for b4 in range(4):
                    for j in range(1, NPAGE, 2):
                        empty(kTp[j % 4], lambda o: o[:, :].rearrange("p (a b) -> p a b", b=128), "kTa")
                need("to_exps")
                link(a.activation(Sm, Sm, ACT.Exp, bias=stat[:, 32:33], accum_out=stat[:, 33:34]), "exps_done")
            a.wait_ge(S("stored1"), 16 * 4)
            square_roots(3)
            for f in range(8):
                empty(q2T[:, f, :], lambda o: o[:, 0:T], "q2T_ready")
            square_roots(2)
            for dst in (mkn, mvn):
                for c in range(2):
                    for i in range(2):
                        empty(dst[:, i, 512 * c:512 * c + 512], lambda o: o[:, :], "mk_ready")
            for i in range(2):
                need("to_exp")
                link(a.activation(S2, S2, ACT.Exp), "exp_done")
            need("to_exp")
            link(a.activation(S2[:, 0, :], S2[:, 0, :], ACT.Exp), "exp_done")
            a.wait_ge(S("stored2"), 16 * 2)
            square_roots(3)
            for f in range(16):
                empty(qvT[:, f, :], lambda o: o[:, 0:T], "qvT_ready")
            for i in range(3):
                need("to_exp")
                link(a.activation(gate[0:TW[i], i, :], gate[0:TW[i], i, :], ACT.Exp), "exp_done")
            for i in range(3):
                need("to_gelu")
                link(a.activation(dots[0:TW[i], i, :], dots[0:TW[i], i, :], ACT.Gelu), "gelu_done")
            square_roots(3)

        @block.sync
        def _(sp):
            sp.dma_start(cst[:, :], consts).then_inc(S("consts"), 16)
            xp = x_prompt[0].rearrange("(i p) d -> i p d", p=P)
            xsm = x_sample.rearrange("b t d -> (b t) d")
            for i in range(2):
                sp.dma_start(x[:, i, :], xp[i]).then_inc(S("x_in"), 16)
            sp.dma_start(x[0:32, 2, :], xsm).then_inc(S("x_in"), 16)
            with nc.allow_non_contiguous_dma(reason="gains with features on partitions"):
                for n, g in enumerate((g_mix, g_mem_q, g_mem_kv)):
                    sp.dma_start(gains[:, n, :], g[0].rearrange("(c p) -> p c", p=P)).then_inc(S("small"), 16)
                sp.dma_start(g_ffn_t[:, :], g_ffn[0].rearrange("(c p) -> p c", p=P)).then_inc(S("small"), 16)
                sp.dma_start(b_al[:, :], b_alpha[0].rearrange("(c p) -> p c", p=P)).then_inc(S("small"), 16)
            sp.dma_start(w_al[:, :], w_alpha_up[0]).then_inc(S("small"), 16)
            sp.dma_start(g_gla_b[:, :], g_gla_out[0].partition_broadcast(P)).then_inc(S("small"), 16)
            sp.dma_start(g_row[:, :], g_ffn[0].partition_broadcast(P)).then_inc(S("g_row"), 16)
            for k, src in enumerate(stream):
                if k >= WSLOT:
                    sp.wait_ge(*w_done[k - WSLOT])
                n = src.shape[2]
                sp.dma_start(wslot[k % WSLOT][:, 0:KC * n].rearrange("p (c n) -> p c n", c=KC), src)\
                  .then_inc(S(f"w{k % WSLOT}"), 16)
            sp.wait_ge(S("g_row_used"), 4)
            sp.dma_start(g_row[:, :], g_final.partition_broadcast(P)).then_inc(S("g_row"), 16)
            for i in range(2):
                sp.wait_ge(S("y_ready"), i + 1)
                sp.dma_start(y_prompt[0].rearrange("(i p) d -> i p d", p=P)[i], x[:, i, :]).then_inc(S("y_out"), 16)
            sp.wait_ge(S("y_ready"), 3)
            sp.dma_start(y_sample.rearrange("b t d -> (b t) d"), x[0:32, 2, :]).then_inc(S("y_out"), 16)
            sp.wait_ge(S("y_out"), 48)
            sp.wait_ge(S("stored1"), 64)
            sp.wait_ge(S("stored2"), 32)
            sp.wait_ge(S("kv_out"), 96)

        @block.gpsimd
        def _(g):
            g.dma_start(pages_ix[:, :], page_table.rearrange("b n -> (b n)").rearrange("(o n) -> o n", o=1))\
             .then_inc(S("table_in"), 16)
            for f in range(2):
                g.dma_start(St_s[:, :, f, :], state_gla[0, :, 2 * f:2 * f + 2].rearrange("b r k v -> (r k) b v"))\
                 .then_inc(S("state_in"), 16)
            g.wait_ge(S("table_in"), 16)
            g.wait_ge(S("rope_done"), 3)
            g.wait_ge(S("z_ready"), 9)
            for z, op_, os_ in ((zk, k_prompt, k_sample), (zv, v_prompt, v_sample)):
                for i in range(2):
                    g.dma_start(op_[0, 0].rearrange("(i p) h d -> i p (h d)", p=P)[i], z[:, i, :]).then_inc(S("kv_out"), 16)
                g.dma_start(os_[0].rearrange("b t h d -> (b t) (h d)"), z[0:32, 2, :]).then_inc(S("kv_out"), 16)
            g.wait_ge(S("newstate_ready"), 1)
            for f in range(2):
                g.dma_start(gla_sample[0, :, 2 * f:2 * f + 2].rearrange("b r k v -> (r k) b v"), St_n[:, :, f, :])\
                 .then_inc(S("stored1"), 16)
                g.dma_start(gla_prompt[0, 0, 2 * f:2 * f + 2].rearrange("r k v -> (r k) v"), St_p[:, 8, f, :])\
                 .then_inc(S("stored1"), 16)
            g.wait_ge(S("stored1"), 64)
            g.wait_ge(S("og_ready"), 3)
            g.wait_ge(S("mixT_ready"), 3)
            n = 0
            for gg in range(2):
                for cache in (cache_k, cache_v):
                    for b4 in range(4):
                        for j in range(NPAGE):
                            at = (4 * gg + b4) * NPAGE + j
                            page = g.value_load(pages_ix[0:1, at:at + 1], min_val=0, max_val=NPOOL - 1)
                            if n >= NSLOT:
                                g.wait_ge(*page_done[n - NSLOT])
                            g.dma_start(pages[:, n % NSLOT, :],
                                        cache[0, bass.ds(page, 1)].rearrange("a p h d -> (a p) (h d)"))\
                             .then_inc(S(f"page{n % NSLOT}"), 16)
                            n += 1
            g.wait_ge(S("mixT_ready"), 9)
            g.wait_ge(S("kv_out"), 96)
            for i in range(2):
                g.dma_start(memx[:, i, :], mem_prompt[0].rearrange("(i p) d -> i p d", p=P)[i]).then_inc(S("mem_in"), 16)
            n = 0
            for cache in (cache_mem_k, cache_mem_v):
                if cache is cache_mem_v:
                    g.wait_ge(S("mk_ready"), 8)
                    for src, dst in ((mkn, mem_k_prompt), (mvn, mem_v_prompt)):
                        g.dma_start(dst[0, 0].rearrange("(i p) h d -> p i (h d)", p=P), src).then_inc(S("stored2"), 16)
                for b in range(NB):
                    if n >= 3:
                        g.wait_ge(*mem_done[n - 3])
                    g.dma_start(memkv[n % 3], cache[0, b].rearrange("(k p) h d -> p k (h d)", p=P))\
                     .then_inc(S(f"mem{n % 3}"), 16)
                    n += 1
            g.wait_ge(S("o2T_ready"), 5)
            for p_ in range(2):
                g.dma_start(skn[:, 8 * p_:8 * p_ + 8, :], peer_sub_keys[0, p_].rearrange("h k d -> k h d"))\
                 .then_inc(S("subkeys"), 16)
            n = 0

            def gather(table, idx, width):
                nonlocal n
                if n >= GSLOT:
                    g.wait_ge(*done[n - GSLOT])
                g.indirect_dma_start(gslot[n % GSLOT][0:width, :], None, table[0], bass.IndirectOffsetOnAxis(ap=idx, axis=0))\
                 .then_inc(S(f"g{n % GSLOT}"), 16)
                n += 1

            done = [(S("dot_done"), k + 1) for k in range(288)] + gather_done
            g.wait_ge(*w_done[-1])
            for i in range(3):
                g.wait_ge(S("eid_ready"), i + 1)
                if i == 2:
                    g.wait_ge(S("eid_s_ready"), 4)
                for j in range(NPAIR if i < 2 else 32):
                    gather(expert_u, eid[:, i, j:j + 1] if i < 2 else eid_s[:, j:j + 1], P)
            g.wait_ge(S("eidT_ready"), 3)
            for t in range(T):
                gather(expert_v, eidT[:, t:t + 1], P)


_INS = ['x_prompt', 'x_sample', 'cache_k', 'cache_v', 'state_gla', 'cache_mem_k', 'cache_mem_v', 'page_table',
        'mem_prompt', 'g_mix', 'w_in', 'w_alpha_up', 'b_alpha', 'g_gla_out', 'w_out', 'g_mem_q', 'g_mem_kv', 'w_mem_q',
        'w_mem_k', 'w_mem_v', 'w_mem_o', 'g_ffn', 'w_peer_q', 'peer_sub_keys', 'expert_u', 'expert_v', 'g_final']
_OUTS = [(1, 256, 1024), (8, 4, 1024), (1, 1, 256, 8, 64), (1, 1, 256, 8, 64), (1, 1, 4, 64, 128),
         (1, 1, 256, 4, 256), (1, 1, 256, 4, 256), (1, 8, 4, 8, 64), (1, 8, 4, 8, 64), (1, 8, 4, 64, 128)]


def kernel(**inputs):
    import numpy as _np
    import concourse.bacc as _bacc
    from concourse import mybir as _mybir
    from concourse.bass_utils import run_bass_kernel_spmd as _run

    nc = _bacc.Bacc("TRN2", target_bir_lowering=False, num_devices=1)
    arrays, args = {}, []
    for name in _INS + ["consts"]:
        a = shape_constants() if name == "consts" else _np.ascontiguousarray(inputs[name])
        arrays[f"in_{name}_dram"] = a
        args.append(nc.dram_tensor(f"in_{name}_dram", a.shape, _mybir.dt.from_np(a.dtype), kind="ExternalInput").ap())
    for i, shape in enumerate(_OUTS):
        args.append(nc.dram_tensor(f"out_{i}_dram", shape, _mybir.dt.float32, kind="ExternalOutput").ap())
    hybrid_step(nc, *args)
    r = _run(nc, [arrays], core_ids=[0])
    return tuple(r.results[0][f"out_{i}_dram"] for i in range(len(_OUTS)))
```

```python
from contextlib import ExitStack

import numpy as np

import concourse.bass as bass
from concourse import mybir

F32 = mybir.dt.float32
I32 = mybir.dt.int32
U32 = mybir.dt.uint32
ALU = mybir.AluOpType
ACT = mybir.ActivationFunctionType
AX = mybir.AxisListType

P = 128
D = 1024
KC = D // P
NP_TOK, NS_TOK = 256, 32
T = NP_TOK + NS_TOK
TW, TO = [128, 128, 32], [0, 128, 256]
NB, NT = 8, 4
MH, MD = 8, 64
NPAGE, PAGE, NPOOL = 16, 128, 160
NBLK = 8
PAST = NPAGE * PAGE
GC = 32
EPS = 1e-6
NEG = -1e30
NKEY, NEXP, PH, TOPK = 128, 128 * 128, 8, 16
NPAIR = PH * TOPK
NBLK_ALL = NB * NBLK
RUN = 16
WSLOT, KSLOT, GSLOT = 3, 12, 18


CONSTS = [("ident", 128), ("rope", 48), ("causal", 512), ("newmask", 64), ("gmask", 1024), ("gmask_s", 1024),
          ("reset", T), ("bmask", 256), ("rowmask", 8), ("iota", 16), ("ones", 32), ("fold", 32), ("half_row", 1)]
COFF = {}
_o = 0
for _n, _w in CONSTS:
    COFF[_n] = (_o, _w)
    _o += _w
CW = _o


def shape_constants():
    c = np.zeros((P, CW), np.float32)

    def put(name, a):
        o, w = COFF[name]
        c[:a.shape[0], o:o + w] = a.reshape(a.shape[0], w)

    p = np.arange(P)
    put("ident", np.eye(P, dtype=np.float32))
    inv = (1.0 / (np.float32(500000.0) ** (np.arange(8, dtype=np.float32) * np.float32(2.0 / 16)))).astype(np.float32)
    rope = np.zeros((P, 3, 16), np.float32)
    for i in range(3):
        pos = p + P * i if i < 2 else PAST + p % NT
        ang = pos.astype(np.float32)[:, None] * inv[None, :]
        rope[:, i, 0:8], rope[:, i, 8:16] = np.cos(ang), np.sin(ang)
    put("rope", rope)
    k = np.arange(256)
    put("causal", np.stack([np.where(k[None] <= (p + P * i)[:, None], 0, NEG) for i in range(2)], 1).astype(np.float32))
    nb, ns = np.arange(32) // NT, np.arange(32) % NT
    b4, t = p // 32, p % NT
    put("newmask", np.stack([np.where((nb[None] == (g * 4 + b4)[:, None]) & (ns[None] <= t[:, None]), 0, NEG)
                             for g in range(2)], 1).astype(np.float32))
    tt, ss = np.arange(32)[None, :, None], np.arange(32)[None, None, :]
    sp = (p % 32)[:, None, None]
    put("gmask", ((ss == sp) & (tt >= ss)).astype(np.float32))
    put("gmask_s", ((ss == sp) & (tt >= ss) & (tt // NT == ss // NT)).astype(np.float32))
    r = np.ones(T, np.float32)
    r[0:NP_TOK:GC] = 0
    r[NP_TOK::NT] = 0
    put("reset", np.tile(r, (P, 1)))
    put("bmask", np.tile((nb[None, :] == np.arange(8)[:, None]).astype(np.float32).reshape(1, 256), (P, 1)))
    put("rowmask", ((p[:, None] // NT) == np.arange(8)[None]).astype(np.float32))
    put("iota", np.tile(np.arange(16, dtype=np.float32), (P, 1)))
    put("ones", np.ones((P, 32), np.float32))
    put("fold", (p[:, None] % 32 == np.arange(32)[None]).astype(np.float32))
    put("half_row", (p % 64).astype(np.float32)[:, None])
    return c


class Lane:

    def __init__(self, banks, full, free):
        self.banks, self.full, self.free = banks, full, free
        self.filled = self.taken = 0

    def open(self, pe):
        n, r = self.filled, len(self.banks)
        self.filled += 1
        if n >= r:
            pe.wait_ge(self.free, n - r + 1)
        return self.banks[n % r]

    def take(self, eng):
        self.taken += 1
        eng.wait_ge(self.full, self.taken)
        return self.banks[(self.taken - 1) % len(self.banks)]


def bc(ap, axis, n):
    a = ap.unsqueeze(axis)
    shape = list(a.shape)
    shape[axis] = n
    return a.to_broadcast(shape)


def hybrid_step(nc, x_prompt, x_sample, cache_k, cache_v, state_gla, cache_mem_k, cache_mem_v, page_table, mem_prompt,
                g_mix, w_in, w_alpha_up, b_alpha, g_gla_out, w_out, g_mem_q, g_mem_kv, w_mem_q, w_mem_k, w_mem_v,
                w_mem_o, g_ffn, w_peer_q, peer_sub_keys, expert_u, expert_v, g_final, consts,
                y_prompt, y_sample, k_prompt, v_prompt, gla_prompt, mem_k_prompt, mem_v_prompt,
                k_sample, v_sample, gla_sample):
    ctx = ExitStack()
    with ctx:
        def sb(name, shape, dt=F32):
            return ctx.enter_context(nc.sbuf_tensor(name, shape, dt))

        sems = {}

        def S(name):
            if name not in sems:
                sems[name] = ctx.enter_context(nc.semaphore(name))
            return sems[name]

        cst = sb("cst", [P, CW])

        def C(name, *dims):
            o, w = COFF[name]
            a = cst[:, o:o + w]
            if len(dims) == 2:
                a = a.rearrange("p (a b) -> p a b", b=dims[1])
            return a

        ident = C("ident")
        rope = C("rope", 3, 16)
        causal = C("causal", 2, 256)
        newmask = C("newmask", 2, 32)
        reset, iota, ones = C("reset"), C("iota"), C("ones")
        bmask = C("bmask", 8, 32)
        rowmask = C("rowmask")
        gains = sb("gains", [P, 3, KC])
        g_ffn_t = sb("g_ffn_t", [P, KC])
        g_row = sb("g_row", [P, D])
        g_gla_b = sb("g_gla_b", [P, 128])
        b_al = sb("b_al", [P, 2])
        w_al = sb("w_al", [16, 256])
        table = sb("table", [P, NB * NPAGE], I32)
        block_ix = sb("block_ix", [P, NBLK_ALL], I32)
        x = sb("x", [P, 3, D])
        hT = sb("hT", [P, KC, T])
        xs = sb("xs", [P, D])
        stat = sb("stat", [P, 64])
        ring = sb("ring", [P, WSLOT * KC * 512])
        wslot = [ring[:, s * 4096:(s + 1) * 4096] for s in range(WSLOT)]
        gslot = [ring[:, s * D:(s + 1) * D] for s in range(KSLOT)]
        kslot = [ring[:, s * D:(s + 1) * D].rearrange("p (a b) -> p a b", b=512) for s in range(KSLOT)]
        zone = sb("zone", [P, 15 * 512])
        ARENA = 20000
        arena = sb("arena", [P, ARENA])

        class Carve:

            def __init__(self, start=0):
                self.at = start

            def __call__(self, *dims):
                n = int(np.prod(dims))
                a = arena[:, self.at:self.at + n]
                self.at += n
                assert self.at <= ARENA, self.at
                if len(dims) == 2:
                    return a.rearrange("p (a b) -> p a b", b=dims[1])
                if len(dims) == 3:
                    return a.rearrange("p (a b c) -> p a b c", b=dims[1], c=dims[2])
                if len(dims) == 4:
                    return a.rearrange("p (a b c d) -> p a b c d", b=dims[1], c=dims[2], d=dims[3])
                return a

        zq, zk, zv, zg, zr = [zone[:, j * 1536:(j + 1) * 1536].rearrange("p (a b) -> p a b", b=512) for j in range(5)]
        memkv = [zone[:, j * 2048:(j + 1) * 2048].rearrange("p (a b) -> p a b", b=D) for j in range(3)]

        ar = Carve()
        qT, kT = ar(4, T), ar(4, T)
        QB = ar(4, NB, 32)
        Sm = [ar(PAST + 32), None]
        keep = ar.at
        flat = hT[:, :, :].rearrange("p c t -> p (c t)")

        def head_block(a):
            return a.rearrange("p (a b) -> p a b", b=256)

        kTp = [[head_block(a) for a in (flat[:, 0:D], flat[:, D:2 * D], g_row[:, :])]]
        gT, la, eA, qe, dk = ar(4, T), ar(2, T), ar(2, T), ar(2, T), ar(2, T)
        qem = dk[:, 0:2, 0:256].rearrange("p f (b t) -> p f b t", t=32)
        kdn = ar(3, 256)
        X = [ar(32, 32) for _ in range(3)]
        kdm = arena[:, ar.at - 2048:ar.at].rearrange("p (a b) -> p a b", b=256)
        att = ar(3, 4, 32)
        St_p = ar(8, 2, 128)
        St_s = ar(NB, 2, 128)
        St_n = ar(NB, 2, 128)
        o_n = zq
        t1, t2, agT = xs[:, 0:T], xs[:, T:2 * T], xs[:, 2 * T:3 * T]
        masked = xs[:, 0:512].rearrange("p (a b) -> p a b", b=32)
        ar = Carve(keep)
        Sb = ar(8, 256)
        pT = ar(16, 128)
        pTs = ar(16, 128)
        Sm[1] = ar(PAST + 32)
        pTn = ar(128)
        osb = ar(512)
        kTp.append([head_block(ar(D)) for _ in range(3)])
        sel = ar(3, 8)
        ar = Carve()
        q2T = ar(KC, T)
        memx = ar(2, D)
        mkn, mvn = ar(2, D), ar(2, D)
        mkT = ar(KC, 256)
        mkTs = [ar(KC, 256) for _ in range(2)]
        S2 = ar(4, 256)
        p2T = ar(8, 128)
        sT2 = ar(2, 128)
        ar = Carve()
        qvT = ar(16, T)
        skT = ar(16, 128)
        xn = ar(3, D)
        sc, sc2 = ar(4, 128), ar(4, 128)
        ts = ar(16, 16)
        tif = ar(16, 16)
        cand, cand2 = ar(256), ar(256)
        fs = ar(PH, TOPK)
        pa, pb = ar(PH, TOPK), ar(PH, TOPK)
        i1, i2 = ar(PH, TOPK), ar(PH, TOPK)
        gate = ar(3, NPAIR)
        eidf = ar(3, NPAIR)
        gate_s = ar(32)
        gslot += [ar(D) for _ in range(GSLOT - KSLOT)]
        diag = [ar(128) for _ in range(4)]
        hot = zone[:, 0:2048].rearrange("p (a b c) -> p a b c", b=TOPK, c=TOPK)
        xns = zone[:, 3072:4096]
        skn = zone[:, 4096:6144].rearrange("p (a b) -> p a b", b=128)
        ti = sb("ti", [P, 16, 16], U32)
        fpos = sb("fpos", [P, PH, TOPK], U32)
        eid = sb("eid", [P, 3, NPAIR], I32)
        eid_s = sb("eid_s", [P, 32], I32)
        dots = sb("dots", [P, 3, NPAIR])
        dots_s = sb("dots_s", [P, 32])
        sel_ix = sb("sel_ix", [P, 8], U32)

        bank = [ctx.enter_context(nc.psum_tensor(f"bank{j}", [P, 512], F32)) for j in range(8)]
        dl = Lane(bank[0:4], S("d_full"), S("d_free"))
        al = Lane(bank[4:6], S("a_full"), S("a_free"))
        el = Lane(bank[6:8], S("e_full"), S("e_free"))

        def wsrc(w, c0, n):
            return w[0, :, c0:c0 + n].rearrange("(c p) n -> p c n", p=P)

        stream = [wsrc(w_in, 0, 512), wsrc(w_in, 512, 512), wsrc(w_in, 1536, 512), wsrc(w_in, 3072, 16),
                  wsrc(w_in, 1024, 512), wsrc(w_in, 2048, 512), wsrc(w_in, 2560, 512)]
        stream += [wsrc(w_out, 512 * j, 512) for j in range(2)]
        stream += [wsrc(w_mem_q, 512 * j, 512) for j in range(2)]
        stream += [wsrc(w_mem_k, 512 * j, 512) for j in range(2)]
        stream += [wsrc(w_mem_v, 512 * j, 512) for j in range(2)]
        stream += [wsrc(w_mem_o, 512 * j, 512) for j in range(2)]
        stream += [wsrc(w_peer_q, 0, 2048)[:, :, 512 * j:512 * j + 512] for j in range(4)]
        runs = [(i, k) for i in range(3) for k in range((NPAIR if i < 2 else 32) // RUN)]
        rows = []
        for m in range(len(runs) + 1):
            for kind, q in (("u", m), ("v", m - 1)):
                if 0 <= q < len(runs):
                    i, k = runs[q]
                    rows += [(kind, i, RUN * k + j) for j in range(RUN)]
        row_at = {r: n for n, r in enumerate(rows)}
        v_done = {}
        roots = []
        w_done = []
        block_done, mem_done = [], []

        block = ctx.enter_context(nc.Block())

        @block.tensor
        def _(pe):
            seen = {}

            def need(name, n=1):
                seen[name] = seen.get(name, 0) + n
                pe.wait_ge(S(name), seen[name])

            def weights(n):
                k = len(w_done)
                pe.wait_ge(S(f"w{k % WSLOT}"), 16 * (k // WSLOT + 1))
                return wslot[k % WSLOT][:, 0:KC * n].rearrange("p (c n) -> p c n", c=KC)

            def natural(src, lane, n=512, tiles=(0, 1, 2)):
                w = weights(n)
                for i in tiles:
                    o = lane.open(pe)
                    for c in range(KC):
                        mm = pe.matmul(o[0:TW[i], 0:n], src[:, c, TO[i]:TO[i] + TW[i]], w[:, c, :],
                                       start=(c == 0), stop=(c == KC - 1))
                    mm.then_inc(lane.full, 1)
                w_done.append((lane.full, lane.filled))

            def transposed(src, lane, n=512):
                w = weights(n)
                for f in range(0, n, P):
                    m = min(P, n - f)
                    o = lane.open(pe)
                    for c in range(KC):
                        mm = pe.matmul(o[0:m, 0:T], w[:, c, f:f + m], src[:, c, :], start=(c == 0), stop=(c == KC - 1))
                    mm.then_inc(lane.full, 1)
                w_done.append((lane.full, lane.filled))

            def turn(blocks, rows, lane=None):
                lane = lane or dl
                o = lane.open(pe)
                for j, b in enumerate(blocks):
                    mm = pe.transpose(o[0:b.shape[1], j * 128:j * 128 + rows], b, ident[0:rows, 0:rows])
                mm.then_inc(lane.full, 1)

            def norm_turns(tiles):
                for i in tiles:
                    need("xs_ready")
                    for j in range(2):
                        turn([xs[0:TW[i], (4 * j + q) * P:(4 * j + q + 1) * P] for q in range(4)], TW[i])

            pe.wait_ge(S("consts"), 16)
            norm_turns((0, 1, 2))
            need("hT_ready", 6)
            natural(hT, al)
            natural(hT, al)
            transposed(hT, al)
            transposed(hT, al, 16)
            natural(hT, al)
            natural(hT, al)
            natural(hT, al)
            need("rope_done", 3)
            for i in range(3):
                for z in (zq, zk):
                    turn([z[0:TW[i], i, q * P:(q + 1) * P] for q in range(4)], TW[i])
            need("gT_ready", 5)
            pe.wait_ge(S("small"), 16 * 7)
            for f in range(2):
                o = dl.open(pe)
                pe.matmul(o[:, 0:T], w_al[:, f * P:(f + 1) * P], agT[0:16, :], start=True, stop=True).then_inc(dl.full, 1)
            need("kd_ready", 1)
            for i in range(3):
                turn([dk[:, f, TO[i]:TO[i] + TW[i]] for f in range(2)], P)
            need("kdn_ready", 3)
            need("z_ready", 9)
            for c in range(NP_TOK // GC):
                i, q = c // 4, 32 * (c % 4)
                o = dl.open(pe)
                for f in range(2):
                    mm = pe.matmul(o[:, f * 256:(f + 1) * 256], kdn[q:q + 32, i, f * P:(f + 1) * P],
                                   zg[q:q + 32, i, f * 256:(f + 1) * 256], start=True, stop=True)
                mm.then_inc(dl.full, 1)
            need("kdm_ready", 1)
            for b in range(NB):
                o = dl.open(pe)
                for f in range(2):
                    mm = pe.matmul(o[:, f * 256:(f + 1) * 256], kdm[0:32, b, f * P:(f + 1) * P],
                                   zg[0:32, 2, f * 256:(f + 1) * 256], start=True, stop=True)
                mm.then_inc(dl.full, 1)
            nblk = 0
            nkey = 0
            scores = None
            order = [(4 * g + b4, 2 * q + h) for g in range(2) for q in range(4) for b4 in range(4) for h in range(2)]

            def next_block():
                nonlocal nblk
                pe.wait_ge(S(f"kv{nblk % KSLOT}"), 16 * (nblk // KSLOT + 1))
                nblk += 1
                return kslot[(nblk - 1) % KSLOT]

            def key_turns():
                kb = next_block()
                for half in range(2):
                    turn([kb[:, half, q * P:(q + 1) * P] for q in range(4)], P, al)
                block_done.append((al.full, al.filled))

            def key_scores():
                nonlocal nkey, scores
                b, blk = order[nkey]
                if nkey % 8 == 0:
                    scores = el.open(pe)
                b4 = b % 4
                need("kT_ready", 2)
                for hp in range(4):
                    mm = pe.matmul(scores[32 * b4:32 * b4 + 32, (blk % 2) * 256:(blk % 2) * 256 + 256], QB[:, hp, b, :],
                                   kTp[b // 4][nkey % 3][:, hp, :], start=(hp == 0), stop=(hp == 3), skip_group_check=True)
                mm.then_inc(*((el.full, 1) if nkey % 8 == 7 else (S("kT_used"), 1)))
                nkey += 1

            need("QB_ready")
            unit = 0
            for i in range(3):
                n = 4 if i < 2 else 1
                for f in range(2):
                    os = [dl.open(pe) for _ in range(4)]
                    for c in range(n):
                        buf = X[unit % 3]
                        need("pairs_ready")
                        for r in range(2):
                            for h in range(2):
                                mm = pe.matmul(os[2 * r + h][32 * c:32 * c + 32, :], ones[64 * r:64 * r + 64, :],
                                               buf[64 * r:64 * r + 64, 16 * h:16 * h + 16, :], start=True, stop=True)
                                if c == n - 1:
                                    mm.then_inc(dl.full, 1)
                        if c < n - 1:
                            mm.then_inc(S("pairs_used"), 1)
                        if unit < 16:
                            for _ in range(2):
                                key_turns()
                                key_scores()
                        unit += 1
            need("att_ready", 24)
            need("qe_ready", 1)
            need("state_ready", 8)
            pe.wait_ge(S("state_in"), 32)
            for i in range(3):
                for r in range(2):
                    o = dl.open(pe)
                    kr = slice(64 * r, 64 * r + 64)
                    for f in range(2):
                        h = 2 * f + r
                        to, cols = slice(f * P, (f + 1) * P), slice(h * P, (h + 1) * P)
                        for q in range(4 if i < 2 else 1):
                            c = 4 * i + q
                            rows = slice(32 * q, 32 * q + 32)
                            mm = pe.matmul(o[rows, to], att[rows, i, h, :], zg[rows, i, cols], start=True, stop=(c == 0),
                                           skip_group_check=True)
                        for q in range(4 if i < 2 else 0):
                            c = 4 * i + q
                            if c > 0:
                                mm = pe.matmul(o[32 * q:32 * q + 32, to], qe[kr, f, c * GC:(c + 1) * GC],
                                               St_p[kr, c - 1, f, :], start=False, stop=True, skip_group_check=True)
                        for b in range(NB if i == 2 else 0):
                            mm = pe.matmul(o[0:32, to], qem[kr, f, b, :], St_s[kr, b, f, :],
                                           start=False, stop=(b == NB - 1), skip_group_check=True)
                    mm.then_inc(dl.full, 1)
            for i in range(3):
                need("og_ready")
                turn([o_n[0:TW[i], i, q * P:(q + 1) * P] for q in range(4)], TW[i])
            need("qkT_ready", 6)
            for i in range(2):
                for g in range(4):
                    o = dl.open(pe)
                    r = g % 2
                    for j in range(2):
                        hp = g // 2 * 2 + j
                        mm = pe.matmul(o[:, j * 256:(j + 1) * 256], qT[64 * r:64 * r + 64, hp, TO[i]:TO[i] + P],
                                       kT[64 * r:64 * r + 64, hp, 0:256], start=True, stop=True)
                    mm.then_inc(dl.full, 1)
                need("p_ready")
                for g in range(4):
                    turn([Sb[:, 2 * g + j // 2, (j % 2) * P:(j % 2 + 1) * P] for j in range(4)], P)
                need("pT_ready", 4)
                o = dl.open(pe)
                for h in range(MH):
                    for kt in range(2):
                        mm = pe.matmul(o[64 * (h % 2):64 * (h % 2) + 64, (h // 2) * P:(h // 2 + 1) * P],
                                       zv[:, kt, h * MD:(h + 1) * MD], pT[:, 2 * h + kt, :],
                                       start=(kt == 0), stop=(kt == 1), skip_group_check=True)
                mm.then_inc(dl.full, 1)
            key_turns()
            for k in range(32):
                if k < 31:
                    key_turns()
                key_scores()
            for g in range(2):
                o = dl.open(pe)
                for b4 in range(4):
                    for hp in range(4):
                        mm = pe.matmul(o[32 * b4:32 * b4 + 32, 0:32], QB[:, hp, 4 * g + b4, :], kT[:, hp, NP_TOK:T],
                                       start=(hp == 0), stop=(hp == 3), skip_group_check=True)
                mm.then_inc(dl.full, 1)
            for g in range(2):
                need("ps_ready")
                for m in range(4):
                    turn([Sm[g][:, (4 * m + j) * P:(4 * m + j + 1) * P] for j in range(4)], P)
                turn([Sm[g][:, PAST:PAST + 32]], P)
                need("psT_ready", 5)
                o = el.open(pe)
                for b4 in range(4):
                    rows_ = slice(32 * b4, 32 * b4 + 32)
                    for j in range(NPAGE):
                        if j % 2 == 0:
                            vb = next_block()
                        mm = pe.matmul(o[rows_, :], pTs[:, j, rows_], vb[:, j % 2, :], start=(j == 0), stop=False,
                                       skip_group_check=True)
                        if j % 2:
                            mm.then_inc(S("v_used"), 1)
                            block_done.append((S("v_used"), 8 * (4 * g + b4) + j // 2 + 1))
                    mm = pe.matmul(o[rows_, :], pTn[0:32, rows_], zv[0:32, 2, :], start=False, stop=True,
                                   skip_group_check=True)
                mm.then_inc(el.full, 1)
                need("osb_ready")
                turn([osb[:, q * P:(q + 1) * P] for q in range(4)], P)
            need("mixT_ready", 3 + 2 + 16)
            natural(hT, dl)
            natural(hT, dl)
            norm_turns((0, 1, 2))
            need("hT_ready", 6)
            transposed(hT, al)
            transposed(hT, al)
            norm_turns((0, 1))
            need("hT_ready", 4)
            for _ in range(4):
                natural(hT, al, tiles=(0, 1))
            need("mk_ready", 8)
            for i in range(2):
                for g in range(2):
                    turn([mkn[:, i, (4 * g + j) * P:(4 * g + j + 1) * P] for j in range(4)], P)
            need("mkT_ready", 4)
            need("q2T_ready", 8)
            for i in range(2):
                for g in range(2):
                    o = dl.open(pe)
                    for j in range(2):
                        for c in range(2):
                            f = 4 * g + 2 * j + c
                            mm = pe.matmul(o[:, j * 256:(j + 1) * 256], q2T[:, f, TO[i]:TO[i] + P], mkT[:, f, :],
                                           start=(c == 0), stop=(c == 1))
                    mm.then_inc(dl.full, 1)
                need("p2_ready")
                for g in range(2):
                    turn([S2[:, 2 * g + j // 2, (j % 2) * P:(j % 2 + 1) * P] for j in range(4)], P)
                need("p2T_ready", 2)
                for g in range(2):
                    o = dl.open(pe)
                    for j in range(4):
                        f = 4 * g + j
                        for kt in range(2):
                            mm = pe.matmul(o[:, j * P:(j + 1) * P], mvn[:, kt, f * P:(f + 1) * P], p2T[:, f // 2 * 2 + kt, :],
                                           start=(kt == 0), stop=(kt == 1))
                    mm.then_inc(dl.full, 1)
            so = el.open(pe)
            nm = 0
            for b in range(NB):
                pe.wait_ge(S(f"mem{nm % 3}"), 16 * (nm // 3 + 1))
                mk = memkv[nm % 3]
                nm += 1
                for kt in range(2):
                    for g in range(2):
                        turn([mk[:, kt, (4 * g + j) * P:(4 * g + j + 1) * P] for j in range(4)], P)
                mem_done.append((dl.full, dl.filled))
                need("mkTs_ready", 4)
                for kt in range(2):
                    for h in range(4):
                        for c in range(2):
                            mm = pe.matmul(so[:, kt * 128 + b * 16 + h * 4:kt * 128 + b * 16 + h * 4 + 4],
                                           mkTs[b % 2][:, 2 * h + c, kt * P:(kt + 1) * P],
                                           q2T[:, 2 * h + c, NP_TOK + 4 * b:NP_TOK + 4 * b + 4], start=(c == 0), stop=(c == 1))
            mm.then_inc(el.full, 1)
            need("sT2_ready")
            turn([sT2[:, kt, :] for kt in range(2)], P)
            need("p2_ready")
            turn([S2[:, 0, kt * P:(kt + 1) * P] for kt in range(2)], P)
            need("p2T_ready")
            o = el.open(pe)
            for b in range(NB):
                pe.wait_ge(S(f"mem{nm % 3}"), 16 * (nm // 3 + 1))
                mv = memkv[nm % 3]
                nm += 1
                for f in range(8):
                    for kt in range(2):
                        c = b * 16 + (f // 2) * 4
                        mm = pe.matmul(o[:, f * 32 + b * 4:f * 32 + b * 4 + 4], mv[:, kt, f * P:(f + 1) * P],
                                       p2T[:, kt, c:c + 4], start=(kt == 0), stop=(kt == 1))
                if b < NB - 1:
                    mm.then_inc(S("mv_used"), 1)
                    mem_done.append((S("mv_used"), b + 1))
            mm.then_inc(el.full, 1)
            need("o2T_ready", 5)
            natural(hT, dl)
            natural(hT, dl)
            norm_turns((0, 1, 2))
            need("hT_ready", 6)
            for _ in range(4):
                transposed(hT, al)
            pe.wait_ge(S("subkeys"), 32)
            for g in range(4):
                turn([skn[:, 4 * g + j, :] for j in range(4)], P)
            need("skT_ready", 4)
            need("qvT_ready", 16)

            def router_scores(i):
                for g in range(4):
                    o = dl.open(pe)
                    for j in range(4):
                        f = 4 * g + j
                        mm = pe.matmul(o[0:TW[i], j * P:(j + 1) * P], qvT[:, f, TO[i]:TO[i] + TW[i]],
                                       skT[:, (f % 2) * PH + f // 2, :], start=True, stop=True)
                    mm.then_inc(dl.full, 1)

            router_scores(0)
            router_scores(1)
            nv = 0
            for m, (i, k) in enumerate(runs):
                w = TW[i]
                if k == 0:
                    oo = [el.open(pe), el.open(pe)]
                last = k == len([r for r in runs if r[0] == i]) - 1
                for j in range(RUN):
                    n = row_at["v", i, k * RUN + j]
                    pe.wait_ge(S(f"g{n % GSLOT}"), 16 * (n // GSLOT + 1))
                    need("diag_ready")
                    for c in range(2):
                        mm = pe.matmul(oo[c][0:w, :], diag[nv % 4][:, 0:w], gslot[n % GSLOT][:, 512 * c:512 * c + 512],
                                       start=(k == 0 and j == 0), stop=(last and j == RUN - 1), skip_group_check=True)
                        if last and j == RUN - 1:
                            mm.then_inc(el.full, 1)
                    nv += 1
                    if not (last and j == RUN - 1):
                        mm.then_inc(S("v_row_used"), 1)
                        v_done[nv - 1] = (S("v_row_used"), nv - sum(1 for q in v_done if v_done[q][0] is el.full))
                    else:
                        v_done[nv - 1] = (el.full, el.filled)
                if (i, k) == (0, 4):
                    router_scores(2)

        @block.vector
        def _(v):
            counts = {}

            def link(ins, name="v_chain"):
                counts[name] = counts.get(name, 0) + 1
                ins.then_inc(S(name), 1)
                v.wait_ge(S(name), counts[name])

            def freed(ins, lane):
                ins.then_inc(lane.free, 1)
                v.wait_ge(lane.free, lane.taken)

            seen = {}

            def need(name, n=1):
                seen[name] = seen.get(name, 0) + n
                v.wait_ge(S(name), seen[name])

            def signal(name):
                link(v.memset(stat[:, 63:64], 0.0), name)

            def rsqrt_mean(dst, src, n):
                link(v.tensor_scalar(dst, src, 1.0 / n, EPS, ALU.mult, ALU.add), "to_sqrt")
                roots.append(dst)
                need("sqrt_done")
                link(v.reciprocal(dst, dst))

            def norm(src, w, name="xs_ready"):
                link(v.tensor_tensor_reduce(xs[0:w, :], src, src, 1.0, 0.0, ALU.mult, ALU.add, stat[0:w, 0:1]))
                rsqrt_mean(stat[0:w, 1:2], stat[0:w, 0:1], D)
                link(v.tensor_scalar(xs[0:w, :], src, stat[0:w, 1:2], None, ALU.mult), name)

            def norm_stage(src, gain, tiles, after=None):
                for i in tiles:
                    norm(src[0:TW[i], i, :], TW[i])
                    if after:
                        after(i)
                    for j in range(2):
                        o = dl.take(v)[:, :].rearrange("p (a b) -> p a b", b=128)[:, :, 0:TW[i]]
                        link(v.tensor_tensor(hT[:, 4 * j:4 * j + 4, TO[i]:TO[i] + TW[i]], o,
                                             bc(gain[:, 4 * j:4 * j + 4], 2, TW[i]), ALU.mult), "hT_ready")
                        freed(v.memset(stat[:, 62:63], 0.0), dl)

            def empty(dst, src_of, name, lane=None, op=None):
                lane = lane or dl
                o = lane.take(v)
                link(op(dst, src_of(o)) if op else v.tensor_copy(dst, src_of(o)), name)
                freed(v.memset(stat[:, 62:63], 0.0), lane)

            def as4(o, n=4, w=128):
                return o[:, 0:n * 128].rearrange("p (a b) -> p a b", b=128)[:, :, 0:w]

            def softmax(buf, heads, name):
                b = buf[:, 0:heads, :]
                m = stat[:, 2:2 + heads]
                link(v.tensor_reduce(m, b, AX.X, ALU.max))
                link(v.tensor_tensor(b, b, bc(m, 2, 256), ALU.subtract), "to_exp")
                need("exp_done")
                link(v.tensor_reduce(m, b, AX.X, ALU.add))
                link(v.reciprocal(m, m))
                link(v.tensor_tensor(b, b, bc(m, 2, 256), ALU.mult), name)

            v.wait_ge(S("consts"), 16)
            v.wait_ge(S("small"), 16 * 7)
            v.wait_ge(S("table_in"), 16)
            link(v.tensor_copy(xs[:, 0:128], table[:, :]))
            for r in range(2):
                rr = slice(64 * r, 64 * r + 64)
                link(v.tensor_scalar(xs[rr, 128:192], xs[rr, r:128:2], 64.0, C("half_row")[rr, :], ALU.mult, ALU.add))
            link(v.tensor_copy(block_ix[:, :], xs[:, 128:192]), "block_ix_ready")
            v.wait_ge(S("x_in"), 48)
            norm_stage(x, gains[:, 0, :], (0, 1, 2))
            need("qk_ready", 6)
            rt = [xs[:, 64 * j:64 * j + 64].rearrange("p (h d) -> p h d", h=8) for j in range(4)]
            for i in range(3):
                w = TW[i]
                for n, z in enumerate((zq, zk)):
                    zz = z[0:w, i, :].rearrange("p (h d) -> p h d", h=8)
                    x1, x2 = zz[:, :, 0:8], zz[:, :, 8:16]
                    co, si = bc(rope[0:w, i, 0:8], 1, 8), bc(rope[0:w, i, 8:16], 1, 8)
                    a = [r[0:w] for r in rt]
                    link(v.tensor_tensor(a[0], x1, co, ALU.mult))
                    link(v.tensor_tensor(a[1], x2, si, ALU.mult))
                    link(v.tensor_tensor(a[2], x2, co, ALU.mult))
                    link(v.tensor_tensor(a[3], x1, si, ALU.mult))
                    link(v.tensor_tensor(x1, a[0], a[1], ALU.subtract))
                    link(v.tensor_tensor(x2, a[2], a[3], ALU.add), "rope_done" if n else "v_chain")
            for i in range(3):
                for z in (qT, kT):
                    empty(z[:, :, TO[i]:TO[i] + TW[i]], lambda o: as4(o, 4, TW[i]), "qkT_ready")
            link(v.memset(QB, 0.0))
            for r in range(2):
                rr = slice(64 * r, 64 * r + 64)
                for hp in range(4):
                    link(v.tensor_copy(QB[rr, hp, :, 8 * hp + 4 * r:8 * hp + 4 * r + 4],
                                       qT[rr, hp, NP_TOK:T].rearrange("p (b t) -> p b t", t=4)))
            signal("QB_ready")
            for f in range(2):
                empty(t1, lambda o: o[:, 0:T], "v_chain",
                      op=lambda d, s: v.tensor_scalar(d, s, b_al[:, f:f + 1], None, ALU.add))
                link(v.tensor_scalar(t2, t1, -1.0, None, ALU.mult))
                link(v.tensor_scalar(la[:, f, :], t1, 0.0, None, ALU.min))
                link(v.tensor_tensor(t1, t1, t2, ALU.min), "to_log1p")
                need("log1p_done")
                link(v.tensor_tensor(la[:, f, :], la[:, f, :], t1, ALU.subtract))
                link(v.tensor_scalar(la[:, f, :], la[:, f, :], 1.0 / 16, None, ALU.mult))
                link(v.tensor_tensor_scan(t2, reset, la[:, f, :], 0.0, ALU.mult, ALU.add))
                link(v.tensor_copy(la[:, f, :], t2))
            for f in range(2):
                for lo, n, c in ((0, 8, GC), (NP_TOK, NB, NT)):
                    A = la[:, f, lo:lo + n * c].rearrange("p (a b) -> p a b", b=c)
                    link(v.tensor_tensor(dk[:, f, lo:lo + n * c].rearrange("p (a b) -> p a b", b=c),
                                         A[:, :, c - 1:c].to_broadcast([P, n, c]), A, ALU.subtract))
            signal("A_ready")
            need("eA_done")
            link(v.tensor_tensor(dk, dk, gT[:, 2:4, :], ALU.mult), "kd_ready")
            link(v.tensor_tensor(qe, eA, gT[:, 0:2, :], ALU.mult))
            for i in range(3):
                empty(kdn[0:TW[i], i, :], lambda o: o[0:TW[i], 0:256], "kdn_ready")
            for f in range(2):
                link(v.tensor_tensor(qem[:, f, :, :], bc(qe[:, f, NP_TOK:T], 1, NB), bmask, ALU.mult))
            signal("qe_ready")
            link(v.tensor_tensor(kdm[0:32, :, :], bc(kdn[0:32, 2, :], 1, NB), bc(rowmask[0:32, :], 2, 256), ALU.mult),
                 "kdm_ready")
            for c in range(NP_TOK // GC):
                o = dl.take(v)
                for f in range(2):
                    for r in range(2):
                        rr = slice(64 * r, 64 * r + 64)
                        u = o[rr, f * 256 + r * 128:f * 256 + r * 128 + 128]
                        if c == 0:
                            link(v.tensor_copy(St_p[rr, 0, f, :], u))
                        else:
                            link(v.scalar_tensor_tensor(St_p[rr, c, f, :], St_p[rr, c - 1, f, :],
                                                        eA[rr, f, c * GC + GC - 1:c * GC + GC], u, ALU.mult, ALU.add))
                signal("state_ready")
                freed(v.memset(stat[:, 62:63], 0.0), dl)
            v.wait_ge(S("state_in"), 32)
            for b in range(NB):
                o = dl.take(v)
                for f in range(2):
                    for r in range(2):
                        rr = slice(64 * r, 64 * r + 64)
                        a = NP_TOK + b * NT + NT - 1
                        link(v.scalar_tensor_tensor(St_n[rr, b, f, :], St_s[rr, b, f, :], eA[rr, f, a:a + 1],
                                                    o[rr, f * 256 + r * 128:f * 256 + r * 128 + 128], ALU.mult, ALU.add))
                freed(v.memset(stat[:, 62:63], 0.0), dl)
            signal("newstate_ready")
            units = [(i, f, c) for i in range(3) for f in range(2) for c in range(4 if i < 2 else 1)]

            def ends(n):
                return n + 1 == len(units) or units[n + 1][0:2] != units[n][0:2]

            def decay(n):
                i, f, c = units[n]
                if n >= 3:
                    v.wait_ge(S("pairs_used"), sum(not ends(q) for q in range(n - 2)))
                s0 = TO[i] + c * GC
                A = la[:, f, s0:s0 + 32]
                link(v.tensor_tensor(X[n % 3], bc(A, 2, 32), bc(A, 1, 32), ALU.subtract))
                link(v.tensor_scalar(X[n % 3], X[n % 3], 0.0, None, ALU.min), "to_decay")

            def sample_scores(g, q):
                empty(Sm[g][:, 512 * q:512 * q + 512], lambda o: o[:, :], "v_chain", el,
                      op=lambda d, s: v.tensor_scalar(d, s, MD ** -0.5, None, ALU.mult))

            decay(0)
            for n, (i, f, c) in enumerate(units):
                if n + 1 < len(units):
                    decay(n + 1)
                buf, s0 = X[n % 3], TO[i] + c * GC
                q, k = gT[:, f, s0:s0 + 32], gT[:, 2 + f, s0:s0 + 32]
                need("decay_done")
                link(v.tensor_tensor(buf, buf, bc(k, 1, 32), ALU.mult))
                link(v.tensor_tensor(buf, buf, bc(q, 2, 32), ALU.mult), "pairs_ready")
                if n >= 5 and n % 4 == 1:
                    sample_scores(0, (n - 5) // 4)
                if not ends(n):
                    continue
                w = TW[i]
                gm = C("gmask", 32, 32) if i < 2 else C("gmask_s", 32, 32)
                for r in range(2):
                    for h in range(2):
                        o = dl.take(v)[0:w, :].rearrange("p (a b) -> p a b", b=32)
                        link(v.tensor_tensor(masked[0:w], o, gm[0:w, 16 * h:16 * h + 16, :], ALU.mult))
                        freed(v.memset(stat[:, 62:63], 0.0), dl)
                        link(v.tensor_reduce(att[0:w, i, 2 * f + r, 16 * h:16 * h + 16], masked[0:w], AX.X, ALU.add),
                             "att_ready")
            for i in range(3):
                w = TW[i]
                for r in range(2):
                    empty(o_n[0:w, i, :].rearrange("p (f r d) -> p r f d", r=2, d=128)[:, r],
                          lambda o: o[0:w, 0:256].rearrange("p (f d) -> p f d", d=128), "v_chain")
                oo = o_n[0:w, i, :].rearrange("p (h d) -> p h d", h=4)
                m = stat[0:w, 2:6]
                sq = xs[0:w, 0:512].rearrange("p (h d) -> p h d", h=4)
                link(v.tensor_tensor(sq, oo, oo, ALU.mult))
                link(v.tensor_reduce(m, sq, AX.X, ALU.add))
                rsqrt_mean(m, m, 128)
                link(v.tensor_tensor(oo, oo, bc(m, 2, 128), ALU.mult))
                link(v.tensor_tensor(oo, oo, bc(g_gla_b[0:w, :], 1, 4), ALU.mult))
                if i == 0:
                    v.wait_ge(S("z_ready"), 9)
                link(v.tensor_tensor(o_n[0:w, i, :], o_n[0:w, i, :], zr[0:w, i, :], ALU.mult), "og_ready")
            for i in range(3):
                empty(hT[:, 4:8, TO[i]:TO[i] + TW[i]], lambda o: as4(o, 4, TW[i]), "mixT_ready")
            v.wait_ge(S("stored1"), 16 * 4)
            for i in range(2):
                for g in range(4):
                    h = g // 2 * 4 + g % 2
                    empty(Sb[:, h:h + 3:2, :], lambda o: o[:, :].rearrange("p (a b) -> p a b", b=256), "v_chain",
                          op=lambda d, s: v.scalar_tensor_tensor(d, s, MD ** -0.5, bc(causal[:, i, :], 1, 2),
                                                                 ALU.mult, ALU.add))
                softmax(Sb, 8, "p_ready")
                for g in range(4):
                    empty(pT[:, 4 * g:4 * g + 4, :], as4, "pT_ready")
                empty(hT[:, 0:4, TO[i]:TO[i] + P], as4, "mixT_ready")
            for q in range(4):
                sample_scores(1, q)
            for g in range(2):
                empty(Sm[g][:, PAST:PAST + 32], lambda o: o[:, 0:32], "v_chain",
                      op=lambda d, s: v.scalar_tensor_tensor(d, s, MD ** -0.5, newmask[:, g, :], ALU.mult, ALU.add))

            def sample_softmax(g):
                S_ = Sm[g]
                past = S_[:, 0:PAST].rearrange("p (a b) -> p a b", b=256)
                gt, top, pen = stat[:, 8:16], stat[:, 16:24], stat[:, 24:32]
                link(v.tensor_reduce(gt, past, AX.X, ALU.add))
                link(v.max(top, gt))
                link(v.max_index(sel_ix[:, :], top, gt))
                link(v.tensor_copy(top, sel_ix[:, :]))
                link(v.tensor_tensor(sel, bc(iota[:, 0:8], 1, 3), bc(top[:, 0:3], 2, 8), ALU.is_equal))
                link(v.tensor_reduce(pen, sel.rearrange("p a b -> p b a"), AX.X, ALU.add))
                link(v.tensor_scalar(pen, pen, 1.0, -NEG, ALU.subtract, ALU.mult))
                link(v.tensor_tensor(past, past, bc(pen, 2, 256), ALU.add))
                m = stat[:, 32:33]
                link(v.tensor_reduce(m, S_, AX.X, ALU.max))
                link(v.tensor_scalar(m, m, -1.0, None, ALU.mult), "to_exps")
                need("exps_done")
                link(v.reciprocal(stat[:, 34:35], stat[:, 33:34]))
                link(v.tensor_scalar(S_, S_, stat[:, 34:35], None, ALU.mult), "ps_ready")

            for g in range(2):
                sample_softmax(g)
                for k in range(4):
                    empty(pTs[:, 4 * k:4 * k + 4, :], as4, "psT_ready")
                empty(pTn[0:32, :], lambda o: o[0:32, 0:128], "psT_ready")
                empty(osb, lambda o: o[:, :], "osb_ready", el)
                o = dl.take(v)[:, :].rearrange("p (a b h t) -> p a b h t", a=4, b=4, h=8)
                for h in range(MH):
                    rr = slice(64 * (h % 2), 64 * (h % 2) + 64)
                    dst = hT[rr, h // 2, NP_TOK + 16 * g:NP_TOK + 16 * g + 16].rearrange("p (b t) -> p b t", t=4)
                    link(v.tensor_copy(dst, o[rr, h // 2, :, h, :]), "mixT_ready")
                freed(v.memset(stat[:, 62:63], 0.0), dl)

            def residual():
                for c in range(2):
                    for i in range(3):
                        d = x[0:TW[i], i, 512 * c:512 * c + 512]
                        empty(d, lambda o: o[0:TW[i], :], "v_chain",
                              op=lambda d, s: v.tensor_tensor(d, d, s, ALU.add))

            residual()
            norm_stage(x, gains[:, 1, :], (0, 1, 2))
            need("q2T_ready", 8)
            v.wait_ge(S("mem_in"), 32)
            norm_stage(memx, gains[:, 2, :], (0, 1))
            for i in range(2):
                for g in range(2):
                    empty(mkT[:, 4 * g:4 * g + 4, i * P:(i + 1) * P], as4, "mkT_ready")
            for i in range(2):
                for g in range(2):
                    empty(S2[:, 2 * g:2 * g + 2, :], lambda o: o[:, :].rearrange("p (a b) -> p a b", b=256), "v_chain",
                          op=lambda d, s: v.tensor_scalar(d, s, 1.0 / 16, None, ALU.mult))
                softmax(S2, 4, "p2_ready")
                for g in range(2):
                    empty(p2T[:, 4 * g:4 * g + 4, :], as4, "p2T_ready")
                for g in range(2):
                    empty(hT[:, 4 * g:4 * g + 4, TO[i]:TO[i] + P], as4, "o2T_ready")
            for b in range(NB):
                for kt in range(2):
                    for g in range(2):
                        empty(mkTs[b % 2][:, 4 * g:4 * g + 4, kt * P:(kt + 1) * P], as4, "mkTs_ready")
            empty(sT2, lambda o: as4(o, 2), "sT2_ready", el)
            empty(S2[:, 0, :], lambda o: o[:, 0:256], "v_chain",
                  op=lambda d, s: v.tensor_scalar(d, s, 1.0 / 16, None, ALU.mult))
            softmax(S2, 1, "p2_ready")
            empty(p2T[:, 0:2, :], lambda o: as4(o, 2), "p2T_ready")
            empty(hT[:, :, NP_TOK:T], lambda o: o[:, 0:256].rearrange("p (a b) -> p a b", b=32), "o2T_ready", el)
            residual()
            v.wait_ge(S("stored2"), 16 * 2)
            v.wait_ge(S("g_row"), 16)

            def scaled_rows(i):
                link(v.tensor_tensor(xn[0:TW[i], i, :], xs[0:TW[i], :], g_row[0:TW[i], :], ALU.mult))

            norm_stage(x, g_ffn_t, (0, 1, 2), scaled_rows)
            for g in range(4):
                link(v.tensor_copy(xns[32 * g:32 * g + 32, :], xn[0:32, 2, :]), "g_row_used")
            for g in range(4):
                empty(skT[:, 4 * g:4 * g + 4, :], as4, "skT_ready")

            def top16(vals, spare, out_v, out_i):
                link(v.max(out_v[:, 0:8], vals))
                link(v.max_index(out_i[:, 0:8], out_v[:, 0:8], vals))
                link(v.match_replace(spare, out_v[:, 0:8], vals, -3e38))
                link(v.max(out_v[:, 8:16], spare))
                link(v.max_index(out_i[:, 8:16], out_v[:, 8:16], spare))

            def route(i, piece):
                w = TW[i]
                if piece < 4:
                    empty(sc[0:w, :, :], lambda o: as4(o)[0:w], "v_chain")
                    for j in range(4):
                        f = 4 * piece + j
                        top16(sc[0:w, j, :], sc2[0:w, j, :], ts[0:w, f, :], ti[0:w, f, :])
                    return
                if piece == 4:
                    link(v.tensor_copy(tif[0:w], ti[0:w, :, :]))
                for h in range(2 * piece - 8, 2 * piece - 6):
                    link(v.tensor_tensor(cand[0:w, :].rearrange("p (a b) -> p a b", b=16), bc(ts[0:w, 2 * h, :], 2, 16),
                                         bc(ts[0:w, 2 * h + 1, :], 1, 16), ALU.add))
                    top16(cand[0:w, :], cand2[0:w, :], fs[0:w, h, :], fpos[0:w, h, :])
                if piece < 7:
                    return
                link(v.tensor_single_scalar(ti[0:w, 0:8, :], fpos[0:w], 4, ALU.logical_shift_right))
                link(v.tensor_single_scalar(ti[0:w, 8:16, :], fpos[0:w], 15, ALU.bitwise_and))
                link(v.tensor_copy(pa[0:w], ti[0:w, 0:8, :]))
                link(v.tensor_copy(pb[0:w], ti[0:w, 8:16, :]))
                for half, (pos, key) in enumerate(((pa, i1), (pb, i2))):
                    for h in range(PH):
                        link(v.tensor_tensor(hot[0:w, h], bc(iota[0:w, :], 1, 16), bc(pos[0:w, h, :], 2, 16), ALU.is_equal))
                        link(v.tensor_tensor(hot[0:w, h], hot[0:w, h], bc(tif[0:w, 2 * h + half, :], 1, 16), ALU.mult))
                    link(v.tensor_reduce(key[0:w], hot[0:w], AX.X, ALU.add))
                ef = eidf[0:w, i, :].rearrange("p (h k) -> p h k", h=PH)
                link(v.scalar_tensor_tensor(ef, i1[0:w], float(NKEY), i2[0:w], ALU.mult, ALU.add))
                link(v.tensor_copy(eid[0:w, i, :], eidf[0:w, i, :]), "eid_ready")
                gg = gate[0:w, i, :].rearrange("p (h k) -> p h k", h=PH)
                m = stat[0:w, 40:48]
                link(v.tensor_tensor(gg, fs[0:w], fs[0:w, :, 0:1].to_broadcast([w, PH, TOPK]), ALU.subtract), "to_exp")
                need("exp_done")
                link(v.tensor_reduce(m, gg, AX.X, ALU.add))
                link(v.reciprocal(m, m))
                link(v.tensor_tensor(gg, gg, bc(m, 2, 16), ALU.mult))
                if i == 2:
                    for g in range(4):
                        link(v.tensor_copy(eid_s[32 * g:32 * g + 32, :], eid[0:32, 2, 32 * g:32 * g + 32]), "eid_s_ready")
                        link(v.tensor_copy(gate_s[32 * g:32 * g + 32, :], gate[0:32, 2, 32 * g:32 * g + 32]))

            def finish(i):
                w = TW[i]
                for g in range(2):
                    empty(x[0:w, i, 512 * g:512 * g + 512], lambda o: o[0:w, :], "v_chain", el,
                          op=lambda d, s: v.tensor_tensor(d, d, s, ALU.add))
                norm(x[0:w, i, :], w, "v_chain")
                if i == 0:
                    v.wait_ge(S("g_row"), 32)
                link(v.tensor_tensor(x[0:w, i, :], xs[0:w, :], g_row[0:w, :], ALU.mult), "y_ready")

            for piece in range(8):
                route(0, piece)
            for m, (i, k) in enumerate(runs):
                for j in range(RUN * k, RUN * k + RUN):
                    n = row_at["u", i, j]
                    v.wait_ge(S(f"g{n % GSLOT}"), 16 * (n // GSLOT + 1))
                    row = gslot[n % GSLOT]
                    dst, xr = (dots[:, i, j:j + 1], xn[:, i, :]) if i < 2 else (dots_s[:, j:j + 1], xns)
                    link(v.tensor_tensor_reduce(row, row, xr, 1.0, 0.0, ALU.mult, ALU.add, dst), "dot_done")
                signal("to_gelu")
                if m >= 2 and runs[m - 2][0] != runs[m - 1][0]:
                    finish(runs[m - 2][0])
                if i < 2:
                    route(i + 1, k)
                need("gelu_done")
                c = slice(RUN * k, RUN * k + RUN)
                gt, dt_ = (gate[:, i, c], dots[:, i, c]) if i < 2 else (gate_s[:, c], dots_s[:, c])
                link(v.tensor_tensor(gt, gt, dt_, ALU.mult), "coef_ready")
            finish(2)

        @block.scalar
        def _(a):
            counts, seen = {}, {}

            def link(ins, name="a_chain"):
                counts[name] = counts.get(name, 0) + 1
                ins.then_inc(S(name), 1)
                a.wait_ge(S(name), counts[name])

            def need(name, n=1):
                seen[name] = seen.get(name, 0) + n
                a.wait_ge(S(name), seen[name])

            def empty(dst, src_of, name, scale=1.0, func=ACT.Copy):
                o = al.take(a)
                link(a.activation(dst, src_of(o), func, scale=scale), name)
                link(a.activation(junk, junk, ACT.Copy), "a_free")

            junk = sb("junk", [1, 1])[:, :]
            a.wait_ge(S("consts"), 16)
            link(a.activation(junk, cst[0:1, 0:1], ACT.Copy))

            def square_roots(n):
                for _ in range(n):
                    r = roots[seen.get("to_sqrt", 0)]
                    need("to_sqrt")
                    link(a.activation(r, r, ACT.Sqrt), "sqrt_done")

            square_roots(3)
            for z in (zq, zk):
                for i in range(3):
                    empty(z[0:TW[i], i, :], lambda o: o[0:TW[i], :], "qk_ready")
            for f in range(4):
                empty(gT[:, f, :], lambda o: o[:, 0:T], "gT_ready", scale=0.125 if f < 2 else 1.0)
            empty(agT[0:16, :], lambda o: o[0:16, 0:T], "gT_ready")
            for z in (zv, zg, zr):
                for i in range(3):
                    empty(z[0:TW[i], i, :], lambda o: o[0:TW[i], :], "z_ready", func=ACT.Silu if z is zr else ACT.Copy)
            for f in range(2):
                need("to_log1p")
                link(a.activation(t1, t1, ACT.Exp))
                link(a.activation(t1, t1, ACT.Ln, bias=1.0), "log1p_done")
            need("A_ready")
            link(a.activation(eA, la, ACT.Exp))
            link(a.activation(dk, dk, ACT.Exp), "eA_done")

            def decay(n):
                need("to_decay")
                link(a.activation(X[n % 3], X[n % 3], ACT.Exp), "decay_done")

            def keys(k):
                if k >= 3:
                    full = (k - 3) // 8 + (k - 3) % 8 // 7
                    if (k - 3) % 8 == 7:
                        a.wait_ge(el.full, (k - 3) // 8 + 1)
                    else:
                        a.wait_ge(S("kT_used"), (k - 3) + 1 - full)
                for half in range(2):
                    empty(kTp[k // 32][k % 3][:, :, half * P:(half + 1) * P],
                          lambda o: o[:, :].rearrange("p (a b) -> p a b", b=128), "kT_ready")

            decay(0)
            for n in range(18):
                if n < 17:
                    decay(n + 1)
                if n < 16:
                    keys(2 * n)
                    keys(2 * n + 1)
            square_roots(3)
            for i in range(2):
                need("to_exp")
                link(a.activation(Sb, Sb, ACT.Exp), "exp_done")
            def sample_exp(g):
                need("to_exps")
                link(a.activation(Sm[g], Sm[g], ACT.Exp, bias=stat[:, 32:33], accum_out=stat[:, 33:34]), "exps_done")

            for k in range(32, 64):
                keys(k)
            for g in range(2):
                sample_exp(g)
            a.wait_ge(S("stored1"), 16 * 4)
            square_roots(3)
            for f in range(8):
                empty(q2T[:, f, :], lambda o: o[:, 0:T], "q2T_ready")
            square_roots(2)
            for dst in (mkn, mvn):
                for c in range(2):
                    for i in range(2):
                        empty(dst[:, i, 512 * c:512 * c + 512], lambda o: o[:, :], "mk_ready")
            for i in range(2):
                need("to_exp")
                link(a.activation(S2, S2, ACT.Exp), "exp_done")
            need("to_exp")
            link(a.activation(S2[:, 0, :], S2[:, 0, :], ACT.Exp), "exp_done")
            a.wait_ge(S("stored2"), 16 * 2)
            square_roots(3)
            for f in range(16):
                empty(qvT[:, f, :], lambda o: o[:, 0:T], "qvT_ready")
            def gates(i):
                need("to_exp")
                link(a.activation(gate[0:TW[i], i, :], gate[0:TW[i], i, :], ACT.Exp), "exp_done")

            gates(0)
            nd = 0
            for m, (i, k) in enumerate(runs):
                c = slice(RUN * k, RUN * k + RUN)
                d = dots[:, i, c] if i < 2 else dots_s[:, c]
                need("to_gelu")
                link(a.activation(d, d, ACT.Gelu), "gelu_done")
                if m >= 2 and runs[m - 2][0] != runs[m - 1][0]:
                    square_roots(1)
                if i < 2 and k == 7:
                    gates(i + 1)
                need("coef_ready")
                for j in range(RUN * k, RUN * k + RUN):
                    if nd >= 4:
                        a.wait_ge(*v_done[nd - 4])
                    src, w, co = (ident, P, gate[:, i, j:j + 1]) if i < 2 else (C("fold"), 32, gate_s[:, j:j + 1])
                    link(a.activation(diag[nd % 4][:, 0:w], src, ACT.Copy, scale=co), "diag_ready")
                    nd += 1
            square_roots(1)

        @block.sync
        def _(sp):
            sp.dma_start(cst[:, :], consts).then_inc(S("consts"), 16)
            xp = x_prompt[0].rearrange("(i p) d -> i p d", p=P)
            xsm = x_sample.rearrange("b t d -> (b t) d")
            for i in range(2):
                sp.dma_start(x[:, i, :], xp[i]).then_inc(S("x_in"), 16)
            sp.dma_start(x[0:32, 2, :], xsm).then_inc(S("x_in"), 16)
            with nc.allow_non_contiguous_dma(reason="gains with features on partitions"):
                for n, g in enumerate((g_mix, g_mem_q, g_mem_kv)):
                    sp.dma_start(gains[:, n, :], g[0].rearrange("(c p) -> p c", p=P)).then_inc(S("small"), 16)
                sp.dma_start(g_ffn_t[:, :], g_ffn[0].rearrange("(c p) -> p c", p=P)).then_inc(S("small"), 16)
                sp.dma_start(b_al[:, :], b_alpha[0].rearrange("(c p) -> p c", p=P)).then_inc(S("small"), 16)
            sp.dma_start(w_al[:, :], w_alpha_up[0]).then_inc(S("small"), 16)
            sp.dma_start(g_gla_b[:, :], g_gla_out[0].partition_broadcast(P)).then_inc(S("small"), 16)
            for k, src in enumerate(stream):
                if k >= WSLOT:
                    sp.wait_ge(*w_done[k - WSLOT])
                if k == 7:
                    sp.wait_ge(el.full, 4)
                    sp.dma_start(g_row[:, :], g_ffn[0].partition_broadcast(P)).then_inc(S("g_row"), 16)
                    sp.wait_ge(*block_done[-1])
                n = src.shape[2]
                sp.dma_start(wslot[k % WSLOT][:, 0:KC * n].rearrange("p (c n) -> p c n", c=KC), src)\
                  .then_inc(S(f"w{k % WSLOT}"), 16)
            sp.wait_ge(S("g_row_used"), 4)
            sp.dma_start(g_row[:, :], g_final.partition_broadcast(P)).then_inc(S("g_row"), 16)
            for i in range(2):
                sp.wait_ge(S("y_ready"), i + 1)
                sp.dma_start(y_prompt[0].rearrange("(i p) d -> i p d", p=P)[i], x[:, i, :]).then_inc(S("y_out"), 16)
            sp.wait_ge(S("y_ready"), 3)
            sp.dma_start(y_sample.rearrange("b t d -> (b t) d"), x[0:32, 2, :]).then_inc(S("y_out"), 16)
            sp.wait_ge(S("y_out"), 48)
            sp.wait_ge(S("stored1"), 64)
            sp.wait_ge(S("stored2"), 32)
            sp.wait_ge(S("kv_out"), 96)

        @block.gpsimd
        def _(g):
            g.dma_start(table[:, :], page_table.rearrange("b n -> (b n)").partition_broadcast(P))\
             .then_inc(S("table_in"), 16)
            for f in range(2):
                g.dma_start(St_s[:, :, f, :], state_gla[0, :, 2 * f:2 * f + 2].rearrange("b r k v -> (r k) b v"))\
                 .then_inc(S("state_in"), 16)
            g.wait_ge(S("rope_done"), 3)
            g.wait_ge(S("z_ready"), 9)
            for z, op_, os_ in ((zk, k_prompt, k_sample), (zv, v_prompt, v_sample)):
                for i in range(2):
                    g.dma_start(op_[0, 0].rearrange("(i p) h d -> i p (h d)", p=P)[i], z[:, i, :]).then_inc(S("kv_out"), 16)
                g.dma_start(os_[0].rearrange("b t h d -> (b t) (h d)"), z[0:32, 2, :]).then_inc(S("kv_out"), 16)
            g.wait_ge(S("newstate_ready"), 1)
            for f in range(2):
                g.dma_start(gla_sample[0, :, 2 * f:2 * f + 2].rearrange("b r k v -> (r k) b v"), St_n[:, :, f, :])\
                 .then_inc(S("stored1"), 16)
                g.dma_start(gla_prompt[0, 0, 2 * f:2 * f + 2].rearrange("r k v -> (r k) v"), St_p[:, 7, f, :])\
                 .then_inc(S("stored1"), 16)
            g.wait_ge(S("stored1"), 64)
            g.wait_ge(*w_done[6])
            g.wait_ge(S("block_ix_ready"), 1)
            loads = [(cache_k, 4 * g + b4, 2 * q + h) for g in range(2) for q in range(4) for b4 in range(4) for h in range(2)]
            loads += [(cache_v, b, blk) for b in range(NB) for blk in range(NBLK)]
            for n, (cache, b, blk) in enumerate(loads):
                pairs = cache[0].rearrange("n (a two) h d -> (n a) (two h d)", two=2)
                at = b * NBLK + blk
                if n >= KSLOT:
                    g.wait_ge(*block_done[n - KSLOT])
                g.indirect_dma_start(ring[:, (n % KSLOT) * D:(n % KSLOT + 1) * D], None, pairs,
                                     bass.IndirectOffsetOnAxis(ap=block_ix[:, at:at + 1], axis=0))\
                 .then_inc(S(f"kv{n % KSLOT}"), 16)
            g.wait_ge(S("mixT_ready"), 21)
            g.wait_ge(S("kv_out"), 96)
            for i in range(2):
                g.dma_start(memx[:, i, :], mem_prompt[0].rearrange("(i p) d -> i p d", p=P)[i]).then_inc(S("mem_in"), 16)
            n = 0
            for cache in (cache_mem_k, cache_mem_v):
                if cache is cache_mem_v:
                    g.wait_ge(S("mk_ready"), 8)
                    for src, dst in ((mkn, mem_k_prompt), (mvn, mem_v_prompt)):
                        g.dma_start(dst[0, 0].rearrange("(i p) h d -> p i (h d)", p=P), src).then_inc(S("stored2"), 16)
                for b in range(NB):
                    if n >= 3:
                        g.wait_ge(*mem_done[n - 3])
                    g.dma_start(memkv[n % 3], cache[0, b].rearrange("(k p) h d -> p k (h d)", p=P))\
                     .then_inc(S(f"mem{n % 3}"), 16)
                    n += 1
            g.wait_ge(S("o2T_ready"), 5)
            for p_ in range(2):
                g.dma_start(skn[:, 8 * p_:8 * p_ + 8, :], peer_sub_keys[0, p_].rearrange("h k d -> k h d"))\
                 .then_inc(S("subkeys"), 16)
            g.wait_ge(*w_done[-1])
            g.wait_ge(S("skT_ready"), 4)
            done = []
            for n, (kind, i, j) in enumerate(rows):
                if j == 0 and kind == "u":
                    g.wait_ge(S("eid_ready"), i + 1)
                    if i == 2:
                        g.wait_ge(S("eid_s_ready"), 4)
                if n >= GSLOT:
                    g.wait_ge(*done[n - GSLOT])
                idx = eid[:, i, j:j + 1] if i < 2 else eid_s[:, j:j + 1]
                g.indirect_dma_start(gslot[n % GSLOT], None, (expert_u if kind == "u" else expert_v)[0],
                                     bass.IndirectOffsetOnAxis(ap=idx, axis=0)).then_inc(S(f"g{n % GSLOT}"), 16)
                nth = sum(1 for r in rows[0:n] if r[0] == kind)
                done.append((S("dot_done"), nth + 1) if kind == "u" else v_done[nth])


_INS = ['x_prompt', 'x_sample', 'cache_k', 'cache_v', 'state_gla', 'cache_mem_k', 'cache_mem_v', 'page_table',
        'mem_prompt', 'g_mix', 'w_in', 'w_alpha_up', 'b_alpha', 'g_gla_out', 'w_out', 'g_mem_q', 'g_mem_kv', 'w_mem_q',
        'w_mem_k', 'w_mem_v', 'w_mem_o', 'g_ffn', 'w_peer_q', 'peer_sub_keys', 'expert_u', 'expert_v', 'g_final']
_OUTS = [(1, 256, 1024), (8, 4, 1024), (1, 1, 256, 8, 64), (1, 1, 256, 8, 64), (1, 1, 4, 64, 128),
         (1, 1, 256, 4, 256), (1, 1, 256, 4, 256), (1, 8, 4, 8, 64), (1, 8, 4, 8, 64), (1, 8, 4, 64, 128)]


def kernel(**inputs):
    import numpy as _np
    import concourse.bacc as _bacc
    from concourse import mybir as _mybir
    from concourse.bass_utils import run_bass_kernel_spmd as _run

    nc = _bacc.Bacc("TRN2", target_bir_lowering=False, num_devices=1)
    arrays, args = {}, []
    for name in _INS + ["consts"]:
        a = shape_constants() if name == "consts" else _np.ascontiguousarray(inputs[name])
        arrays[f"in_{name}_dram"] = a
        args.append(nc.dram_tensor(f"in_{name}_dram", a.shape, _mybir.dt.from_np(a.dtype), kind="ExternalInput").ap())
    for i, shape in enumerate(_OUTS):
        args.append(nc.dram_tensor(f"out_{i}_dram", shape, _mybir.dt.float32, kind="ExternalOutput").ap())
    hybrid_step(nc, *args)
    r = _run(nc, [arrays], core_ids=[0])
    return tuple(r.results[0][f"out_{i}_dram"] for i in range(len(_OUTS)))
```

```python
from contextlib import ExitStack

import numpy as np

import concourse.bass as bass
from concourse import mybir

F32 = mybir.dt.float32
I32 = mybir.dt.int32
U32 = mybir.dt.uint32
ALU = mybir.AluOpType
ACT = mybir.ActivationFunctionType
AX = mybir.AxisListType

P = 128
D = 1024
KC = D // P
NP_TOK, NS_TOK = 256, 32
T = NP_TOK + NS_TOK
TW, TO = [128, 128, 32], [0, 128, 256]
NB, NT = 8, 4
MH, MD = 8, 64
NPAGE, PAGE, NPOOL = 16, 128, 160
NBLK = 8
PAST = NPAGE * PAGE
GC = 32
EPS = 1e-6
NEG = -1e30
NKEY, NEXP, PH, TOPK = 128, 128 * 128, 8, 16
NPAIR = PH * TOPK
NBLK_ALL = NB * NBLK
RUN = 16
WSLOT, GSLOT = 3, 18
WIDE, KSLOT = 9, 5
N_EARLY = 6
N_WIDE = 96
KAHEAD = 24
KEYS_AT = [4] + [2] * 16 + [0]
KEYS_MORE = 4
VALUES_AT = [0] * 8 + [2] * 8 + [4, 4]
assert KAHEAD + sum(KEYS_AT) + KEYS_MORE == NBLK_ALL


CONSTS = [("ident", 128), ("rope", 48), ("causal", 512), ("newmask", 64), ("gmask", 512), ("gmask_s", 512),
          ("reset", T), ("bmask", 256), ("rowmask", 8), ("iota", 16), ("ones", 32), ("fold", 32), ("half_row", 1), ("row", 1), ("first_half", 1), ("eps", 1)]
COFF = {}
_o = 0
for _n, _w in CONSTS:
    COFF[_n] = (_o, _w)
    _o += _w
CW = _o


def shape_constants():
    c = np.zeros((P, CW), np.float32)

    def put(name, a):
        o, w = COFF[name]
        c[:a.shape[0], o:o + w] = a.reshape(a.shape[0], w)

    p = np.arange(P)
    put("ident", np.eye(P, dtype=np.float32))
    inv = (1.0 / (np.float32(500000.0) ** (np.arange(8, dtype=np.float32) * np.float32(2.0 / 16)))).astype(np.float32)
    rope = np.zeros((P, 3, 16), np.float32)
    for i in range(3):
        pos = p + P * i if i < 2 else PAST + p % NT
        ang = pos.astype(np.float32)[:, None] * inv[None, :]
        rope[:, i, 0:8], rope[:, i, 8:16] = np.cos(ang), np.sin(ang)
    put("rope", rope)
    k = np.arange(256)
    put("causal", np.stack([np.where(k[None] <= (p + P * i)[:, None], 0, NEG) for i in range(2)], 1).astype(np.float32))
    nb, ns = np.arange(32) // NT, np.arange(32) % NT
    b4, t = p // 32, p % NT
    put("newmask", np.stack([np.where((nb[None] == (g * 4 + b4)[:, None]) & (ns[None] <= t[:, None]), 0, NEG)
                             for g in range(2)], 1).astype(np.float32))
    hh, tt, ss = np.arange(2)[None, :, None, None], np.arange(16)[None, None, :, None], np.arange(16)[None, None, None, :]
    sp = (p % 32)[:, None, None, None]
    put("gmask", ((hh * 16 + ss == sp) & (tt >= ss)).astype(np.float32))
    put("gmask_s", ((hh * 16 + ss == sp) & (tt >= ss) & (tt // NT == ss // NT)).astype(np.float32))
    r = np.ones(T, np.float32)
    r[0:NP_TOK:GC] = 0
    r[NP_TOK::NT] = 0
    put("reset", np.tile(r, (P, 1)))
    put("bmask", np.tile((nb[None, :] == np.arange(8)[:, None]).astype(np.float32).reshape(1, 256), (P, 1)))
    put("rowmask", ((p[:, None] // NT) == np.arange(8)[None]).astype(np.float32))
    put("iota", np.tile(np.arange(16, dtype=np.float32), (P, 1)))
    put("ones", np.ones((P, 32), np.float32))
    put("fold", (p[:, None] % 32 == np.arange(32)[None]).astype(np.float32))
    put("half_row", (p % 64).astype(np.float32)[:, None])
    put("first_half", (p % 32 < 16).astype(np.float32)[:, None])
    put("eps", np.full((P, 1), EPS, np.float32))
    put("row", p.astype(np.float32)[:, None])
    return c


class Lane:

    def __init__(self, banks, full, free):
        self.banks, self.full, self.free = banks, full, free
        self.filled = self.taken = 0

    def open(self, pe):
        n, r = self.filled, len(self.banks)
        self.filled += 1
        if n >= r:
            pe.wait_ge(self.free, n - r + 1)
        return self.banks[n % r]

    def take(self, eng):
        self.taken += 1
        eng.wait_ge(self.full, self.taken)
        return self.banks[(self.taken - 1) % len(self.banks)]


def bc(ap, axis, n):
    a = ap.unsqueeze(axis)
    shape = list(a.shape)
    shape[axis] = n
    return a.to_broadcast(shape)


def hybrid_step(nc, x_prompt, x_sample, cache_k, cache_v, state_gla, cache_mem_k, cache_mem_v, page_table, mem_prompt,
                g_mix, w_in, w_alpha_up, b_alpha, g_gla_out, w_out, g_mem_q, g_mem_kv, w_mem_q, w_mem_k, w_mem_v,
                w_mem_o, g_ffn, w_peer_q, peer_sub_keys, expert_u, expert_v, g_final, consts,
                y_prompt, y_sample, k_prompt, v_prompt, gla_prompt, mem_k_prompt, mem_v_prompt,
                k_sample, v_sample, gla_sample):
    ctx = ExitStack()
    with ctx:
        def sb(name, shape, dt=F32):
            return ctx.enter_context(nc.sbuf_tensor(name, shape, dt))

        sems = {}

        def S(name):
            if name not in sems:
                sems[name] = ctx.enter_context(nc.semaphore(name))
            return sems[name]

        cst = sb("cst", [P, CW])

        def C(name, *dims):
            o, w = COFF[name]
            a = cst[:, o:o + w]
            if len(dims) == 2:
                a = a.rearrange("p (a b) -> p a b", b=dims[1])
            return a

        ident = C("ident")
        rope = C("rope", 3, 16)
        causal = C("causal", 2, 256)
        newmask = C("newmask", 2, 32)
        reset, iota, ones = C("reset"), C("iota"), C("ones")
        bmask = C("bmask", 8, 32)
        rowmask = C("rowmask")
        gains = sb("gains", [P, 3, KC])
        g_ffn_t = sb("g_ffn_t", [P, KC])
        g_row = sb("g_row", [P, D])
        g_gla_b = sb("g_gla_b", [P, 128])
        b_al = sb("b_al", [P, 2])
        w_al = sb("w_al", [16, 256])
        table = sb("table", [P, NB * NPAGE], I32)
        block_ix = sb("block_ix", [P, NBLK_ALL], I32)
        page_ix = sb("page_ix", [P, NB * NPAGE], I32)
        x = sb("x", [P, 3, D])
        hT = sb("hT", [P, KC, T])
        xs = sb("xs", [P, D])
        stat = sb("stat", [P, 64])
        mem_rstd = stat[:, 50:52]
        x_rstd = stat[:, 53:56]
        ring = sb("ring", [P, WSLOT * KC * 512])
        wslot = [ring[:, s * 4096:(s + 1) * 4096] for s in range(WSLOT)]
        gslot = [ring[:, s * D:(s + 1) * D] for s in range(WSLOT * 4)]
        bslot = gslot[0:WIDE]
        wslot.append(ring[:, KSLOT * D:(KSLOT + 4) * D])
        scores_at = (KSLOT + 4) * D
        zone = sb("zone", [P, 15 * 512])
        ARENA = 20800
        arena = sb("arena", [P, ARENA])


        class Carve:

            def __init__(self, start=0):
                self.at = start

            def __call__(self, *dims):
                n = int(np.prod(dims))
                a = arena[:, self.at:self.at + n]
                self.at += n
                assert self.at <= ARENA, self.at
                if len(dims) == 2:
                    return a.rearrange("p (a b) -> p a b", b=dims[1])
                if len(dims) == 3:
                    return a.rearrange("p (a b c) -> p a b c", b=dims[1], c=dims[2])
                if len(dims) == 4:
                    return a.rearrange("p (a b c d) -> p a b c d", b=dims[1], c=dims[2], d=dims[3])
                return a

        zq, zk, zv, zg, zr = [zone[:, j * 1536:(j + 1) * 1536].rearrange("p (a b) -> p a b", b=512) for j in range(5)]
        memkv = [zone[:, j * 2048:(j + 1) * 2048].rearrange("p (a b) -> p a b", b=D) for j in range(3)]

        ar = Carve()
        qT, kT = ar(4, T), ar(4, T)
        QB = ar(4, NB, 32)
        Sm = [ar(PAST + 32), ring[:, scores_at:scores_at + PAST + 32]]
        pTs = [ar(16, 128), None]
        pTn = [ar(128) for _ in range(2)]
        sel = ar(3, 8)
        keep = ar.at
        gT, la, eA, qe, dk = ar(4, T), ar(2, T), ar(2, T), ar(2, T), ar(2, T)
        qem = dk[:, 0:2, 0:256].rearrange("p f (b t) -> p f b t", t=32)
        kdn = ar(3, 256)
        X = [ar(32, 16) for _ in range(3)]
        halves = ar(2, 8, 2, 16)
        kdm = arena[:, ar.at - 2048:ar.at].rearrange("p (a b) -> p a b", b=256)
        att = ar(3, 4, 32)
        at = ar.at
        St_p = ar(8, 2, 128)
        St_s = ar(NB, 2, 128)
        squares = arena[:, ar.at:ar.at + D]
        spare_memory = arena[:, ar.at:ar.at + 2 * D].rearrange("p (a b) -> p a b", b=D)
        St_n = ar(NB, 2, 128)
        bslot = bslot + [a[:, j * D:(j + 1) * D] for a in (
            pTs[0].rearrange("p a b -> p (a b)"), Sm[0][:, 0:2048], St_n.rearrange("p a b c -> p (a b c)")) for j in range(2)]
        ar = Carve(at)
        mkn, mvn = ar(2, D), ar(2, D)
        memT = ar(KC, 256)
        mem_sq = hT[:, :, 0:256]
        o_n = zq
        t1, t2, agT = xs[:, 0:T], xs[:, T:2 * T], xs[:, 2 * T:3 * T]
        masked = xs[:, 0:512].rearrange("p (a b) -> p a b", b=16)
        ar = Carve(keep)
        osb = ar(512)
        Sb = ar(8, 256)
        pT = ar(16, 128)
        pTs[1] = ar(16, 128)
        ar = Carve()
        q2T = ar(KC, T)
        mkT = ar(KC, 256)
        QM = ar(KC, NB, 32)
        S2 = [ar(4, 256) for _ in range(2)]
        p2T = [ar(8, 128) for _ in range(2)]
        S2s = ar(1, 256)
        pM = ar(2, NB, 32)
        osb2 = ar(D)
        memkv += [ar(2, D), spare_memory]
        assert ar.at <= at
        ar = Carve()
        qvT = ar(16, T)
        skT = ar(16, 128)
        xn = ar(3, D)
        sc, sc2 = ar(4, 128), ar(4, 128)
        ts = ar(16, 16)
        tif = ar(16, 16)
        cand, cand2 = ar(2, 256), ar(256)
        fs = ar(PH, TOPK)
        posf = ar(2 * PH, TOPK)
        keyno = ar(2 * PH, TOPK)
        gate = ar(3, NPAIR)
        eidf = ar(3, NPAIR)
        gate_s = ar(32)
        wslot.append(arena[:, ar.at:ar.at + 4096])
        gslot += [ar(D) for _ in range(GSLOT - WSLOT * 4)]
        diag = [ar(128) for _ in range(4)]
        hot = [zone[:, j * 1024:(j + 1) * 1024].rearrange("p (a b c) -> p a b c", b=TOPK, c=TOPK) for j in range(4)]
        xns = zone[:, 4096:5120]
        ti = sb("ti", [P, 16, 16], U32)
        fpos = sb("fpos", [P, PH, TOPK], U32)
        posn = sb("posn", [P, 4, TOPK], U32)
        eid = sb("eid", [P, 3, NPAIR], I32)
        eid_s = sb("eid_s", [P, 32], I32)
        dots = sb("dots", [P, 3, NPAIR])
        dots_s = sb("dots_s", [P, 32])
        sel_ix = sb("sel_ix", [P, 8], U32)

        bank = [ctx.enter_context(nc.psum_tensor(f"bank{j}", [P, 512], F32)) for j in range(8)]
        dl = Lane(bank[0:4], S("d_full"), S("d_free"))
        al = Lane(bank[4:6], S("a_full"), S("a_free"))
        el = Lane(bank[6:8], S("e_full"), S("e_free"))

        def wsrc(w, c0, n):
            return w[0, :, c0:c0 + n].rearrange("(c p) n -> p c n", p=P)

        stream = [wsrc(w_in, 0, 512), wsrc(w_in, 512, 512), wsrc(w_in, 1536, 512), wsrc(w_in, 3072, 16),
                  wsrc(w_in, 1024, 512), wsrc(w_in, 2048, 512), wsrc(w_in, 2560, 512)]
        stream += [wsrc(w_mem_k, 512 * j, 512) for j in range(2)]
        stream += [wsrc(w_mem_v, 512 * j, 512) for j in range(2)]
        stream += [wsrc(w_out, 512 * j, 512) for j in range(2)]
        stream += [wsrc(w_mem_q, 512 * j, 512) for j in range(2)]
        stream += [wsrc(w_mem_o, 512 * j, 512) for j in range(2)]
        stream += [wsrc(w_peer_q, 0, 2048)[:, :, 512 * j:512 * j + 512] for j in range(4)]
        slot_of = [k % WSLOT for k in range(7)] + [WSLOT] * 4 + [k % WSLOT for k in range(9)] + [WSLOT + 1]
        runs = [(i, k) for i in range(3) for k in range((NPAIR if i < 2 else 32) // RUN)]
        rows = []
        for m in range(len(runs) + 1):
            for kind, q in (("u", m), ("v", m - 1)):
                if 0 <= q < len(runs):
                    i, k = runs[q]
                    rows += [(kind, i, RUN * k + j) for j in range(RUN)]
        row_at = {r: n for n, r in enumerate(rows)}
        v_done = {}
        roots = []
        w_done = []
        block_done, mem_done, taken = [], [], []

        block = ctx.enter_context(nc.Block())

        @block.tensor
        def _(pe):
            seen = {}

            def need(name, n=1):
                seen[name] = seen.get(name, 0) + n
                pe.wait_ge(S(name), seen[name])

            def weights(n):
                k = len(w_done)
                pe.wait_ge(S(f"w{slot_of[k]}"), 16 * slot_of[0:k + 1].count(slot_of[k]))
                return wslot[slot_of[k]][:, 0:KC * n].rearrange("p (c n) -> p c n", c=KC)

            def natural(src, lane, before_samples=None):
                w = weights(512)
                for i in range(2):
                    o = lane.open(pe)
                    for c in range(KC):
                        mm = pe.matmul(o[:, :], src[:, c, TO[i]:TO[i] + P], w[:, c, :], start=(c == 0), stop=(c == KC - 1))
                    mm.then_inc(lane.full, 1)
                if before_samples:
                    need(*before_samples)
                o = lane.open(pe)
                for c in range(KC):
                    for q in range(4):
                        mm = pe.matmul(o[32 * q:32 * q + 32, 0:P], src[:, c, NP_TOK:T], w[:, c, q * P:(q + 1) * P],
                                       start=(c == 0), stop=(c == KC - 1), skip_group_check=True)
                mm.then_inc(lane.full, 1)
                w_done.append((lane.full, lane.filled))

            def transposed(src, lane, n=512):
                w = weights(n)
                for f in range(0, n, P):
                    m = min(P, n - f)
                    o = lane.open(pe)
                    for c in range(KC):
                        mm = pe.matmul(o[0:m, 0:T], w[:, c, f:f + m], src[:, c, :], start=(c == 0), stop=(c == KC - 1))
                    mm.then_inc(lane.full, 1)
                w_done.append((lane.full, lane.filled))

            def turn(blocks, rows, lane=None):
                lane = lane or dl
                o = lane.open(pe)
                for j, b in enumerate(blocks):
                    mm = pe.transpose(o[0:b.shape[1], j * 128:j * 128 + rows], b, ident[0:rows, 0:rows])
                mm.then_inc(lane.full, 1)

            def norm_turns():
                for i in range(3):
                    need("norm_diag_ready")
                    for j in range(2):
                        o = dl.open(pe)
                        for q in range(4):
                            mm = pe.matmul(o[:, q * P:q * P + TW[i]], x[0:TW[i], i, (4 * j + q) * P:(4 * j + q + 1) * P],
                                           xs[0:TW[i], i * P:i * P + TW[i]], start=True, stop=True)
                        mm.then_inc(dl.full, 1)

            pe.wait_ge(S("consts"), 16)
            norm_turns()
            need("hT_ready", 6)
            natural(hT, al)
            natural(hT, al)
            transposed(hT, al)
            transposed(hT, al, 16)
            natural(hT, al)
            need("rope_done", 3)
            for i in range(3):
                for z in (zq, zk):
                    turn([z[0:TW[i], i, q * P:(q + 1) * P] for q in range(4)], TW[i])
            need("gT_ready", 5)
            pe.wait_ge(S("small"), 16 * 7)
            for f in range(2):
                o = dl.open(pe)
                pe.matmul(o[:, 0:T], w_al[:, f * P:(f + 1) * P], agT[0:16, :], start=True, stop=True).then_inc(dl.full, 1)
            natural(hT, al)
            need("kd_ready", 1)
            for i in range(3):
                turn([dk[:, f, TO[i]:TO[i] + TW[i]] for f in range(2)], P)
            natural(hT, al)
            nkey = 0
            scores = None
            key_order = [(4 * g + b4, 2 * q + h) for g in range(2) for q in range(4) for h in range(2) for b4 in range(4)]
            in_slot = [0] * (WIDE + N_EARLY)

            def next_block(kind, b, blk):
                n = len(taken)
                s_ = WIDE + n if n < N_EARLY else (n - N_EARLY + 4) % WIDE if n < N_WIDE else (n - N_WIDE) % KSLOT
                taken.append((kind, b, blk, s_))
                in_slot[s_] += 32 if kind == "key" else 16
                pe.wait_ge(S(f"kv{s_}"), in_slot[s_])
                return bslot[s_]

            def key_scores(n):
                nonlocal nkey, scores
                for _ in range(0, n, 2):
                    if nkey % 8 == 0:
                        scores = el.open(pe)
                    two = key_order[nkey:nkey + 2]
                    kb = [next_block("key", *bb).rearrange("p (r c two a) -> p c two r a", r=2, c=4, two=2) for bb in two]
                    for hp in range(4):
                        for t, (b, blk) in enumerate(two):
                            r0, c0 = 32 * (b % 4), (blk % 2) * 256
                            mm = pe.matmul(scores[r0:r0 + 32, c0:c0 + 256], QB[:, hp, b, :], kb[t][:, hp],
                                           start=(hp == 0), stop=(hp == 3), skip_group_check=True)
                            if hp == 3 and t == 0:
                                mm.then_inc(S("k_used"), 1)
                                block_done.append((S("k_used"), nkey - nkey // 8 + 1))
                    nkey += 2
                    if nkey % 8 == 0:
                        mm.then_inc(el.full, 1)
                        block_done.append((el.full, el.filled))
                    else:
                        mm.then_inc(S("k_used"), 1)
                        block_done.append((S("k_used"), nkey - nkey // 8))

            def new_key_scores(g):
                o = dl.open(pe)
                for b4 in range(4):
                    for hp in range(4):
                        mm = pe.matmul(o[32 * b4:32 * b4 + 32, 0:32], QB[:, hp, 4 * g + b4, :], kT[:, hp, NP_TOK:T],
                                       start=(hp == 0), stop=(hp == 3), skip_group_check=True)
                mm.then_inc(dl.full, 1)

            def sample_turns(g):
                need("ps_ready")
                for m in range(4):
                    turn([Sm[g][:, (4 * m + j) * P:(4 * m + j + 1) * P] for j in range(4)], P)
                turn([Sm[g][:, PAST:PAST + 32]], P)

            nval = 0
            value_order = [(4 * g + 2 * q + t, blk) for g in range(2) for q in range(2) for blk in range(NBLK) for t in range(2)]

            def sample_values(o, n):
                nonlocal nval
                for _ in range(0, n, 2):
                    two = value_order[nval:nval + 2]
                    vb = [next_block("value", *bb).rearrange("p (a b) -> p a b", b=512) for bb in two]
                    for j in range(2):
                        for t, (b, blk) in enumerate(two):
                            rows_ = slice(32 * (b % 4), 32 * (b % 4) + 32)
                            mm = pe.matmul(o[rows_, :], pTs[b // 4][:, 2 * blk + j, rows_], vb[t][:, j, :],
                                           start=(blk == 0 and j == 0), stop=False, skip_group_check=True)
                            if j == 1:
                                nval += 1
                                mm.then_inc(S("v_used"), 1)
                                block_done.append((S("v_used"), nval))
                    if blk == NBLK - 1:
                        for b, _ in two:
                            rows_ = slice(32 * (b % 4), 32 * (b % 4) + 32)
                            mm = pe.matmul(o[rows_, :], pTn[b // 4][0:32, rows_], zv[0:32, 2, :], start=False, stop=True,
                                           skip_group_check=True)
                return mm

            need("QB_ready")
            need("kdn_ready", 3)
            need("z_ready", 6)
            for c in range(NP_TOK // GC):
                i, q = c // 4, 32 * (c % 4)
                o = dl.open(pe)
                for f in range(2):
                    mm = pe.matmul(o[:, f * 256:(f + 1) * 256], kdn[q:q + 32, i, f * P:(f + 1) * P],
                                   zg[q:q + 32, i, f * 256:(f + 1) * 256], start=True, stop=True)
                mm.then_inc(dl.full, 1)
                if c % 2:
                    key_scores(2)
            need("kdm_ready", 1)
            for b in range(NB):
                o = dl.open(pe)
                for f in range(2):
                    mm = pe.matmul(o[:, f * 256:(f + 1) * 256], kdm[0:32, b, f * P:(f + 1) * P],
                                   zg[0:32, 2, f * 256:(f + 1) * 256], start=True, stop=True)
                mm.then_inc(dl.full, 1)
                key_scores(2)
            unit = 0
            for i in range(3):
                n = 4 if i < 2 else 1
                for f in range(2):
                    os = [dl.open(pe) for _ in range(2)]
                    for c in range(n):
                        buf = X[unit % 3]
                        need("pairs_ready")
                        for r in range(2):
                            mm = pe.matmul(os[r][32 * c:32 * c + 32, :], ones[64 * r:64 * r + 64, :],
                                           buf[64 * r:64 * r + 64, :, :], start=True, stop=True)
                            if c == n - 1:
                                mm.then_inc(dl.full, 1)
                        if c < n - 1:
                            mm.then_inc(S("pairs_used"), 1)
                        key_scores(KEYS_AT[unit])
                        if VALUES_AT[unit]:
                            sample_values(first_values, VALUES_AT[unit])
                        unit += 1
                    if unit == 4:
                        new_key_scores(0)
                        key_scores(KEYS_MORE)
                    if unit == 8:
                        sample_turns(0)
                        need("psT_ready", 5)
                        first_values = al.open(pe)
                    if unit == 12:
                        need("mem_sq_ready")
                        o = dl.open(pe)
                        for t in range(2):
                            for c in range(KC):
                                mm = pe.matmul(o[:, t:t + 1], mem_sq[:, c, t * P:(t + 1) * P], ones[:, 0:1],
                                               start=(c == 0), stop=(c == KC - 1))
                        mm.then_inc(dl.full, 1)
            need("halves_ready")
            for i in range(2):
                for r in range(2):
                    o = dl.open(pe)
                    kr = slice(64 * r, 64 * r + 64)
                    for c in range(4):
                        for f in range(2):
                            mm = pe.matmul(o[32 * c:32 * c + 32, f * 16:(f + 1) * 16],
                                           halves[kr, f, 4 * i + c].rearrange("p a b -> p (a b)"),
                                           halves[kr, f, 4 * i + c, 1, :], start=True, stop=True)
                    mm.then_inc(dl.full, 1)
            new_key_scores(1)
            sample_values(first_values, NBLK_ALL // 2 - sum(VALUES_AT)).then_inc(al.full, 1)
            def sample_output_turns():
                need("osb_ready")
                turn([osb[:, q * P:(q + 1) * P] for q in range(4)], P)

            need("att_ready", 16)
            need("qe_ready", 1)
            need("state_ready", 8)
            pe.wait_ge(S("state_in"), 32)
            for i in range(3):
                for r in range(2):
                    o = dl.open(pe)
                    kr = slice(64 * r, 64 * r + 64)
                    for f in range(2):
                        h = 2 * f + r
                        to, cols = slice(f * P, (f + 1) * P), slice(h * P, (h + 1) * P)
                        for q in range(4 if i < 2 else 1):
                            c = 4 * i + q
                            rows = slice(32 * q, 32 * q + 32)
                            mm = pe.matmul(o[rows, to], att[rows, i, h, :], zg[rows, i, cols], start=True, stop=(c == 0),
                                           skip_group_check=True)
                        for q in range(4 if i < 2 else 0):
                            c = 4 * i + q
                            if c > 0:
                                mm = pe.matmul(o[32 * q:32 * q + 32, to], qe[kr, f, c * GC:(c + 1) * GC],
                                               St_p[kr, c - 1, f, :], start=False, stop=True, skip_group_check=True)
                        for b in range(NB if i == 2 else 0):
                            mm = pe.matmul(o[0:32, to], qem[kr, f, b, :], St_s[kr, b, f, :],
                                           start=False, stop=(b == NB - 1), skip_group_check=True)
                    mm.then_inc(dl.full, 1)
            need("memT_ready")
            nbank = 0

            def memory_banks(n):
                nonlocal nbank, w
                for _ in range(n):
                    if nbank % 2 == 0:
                        w = weights(512)
                    o = al.open(pe)
                    i = nbank % 2
                    for c in range(KC):
                        mm = pe.matmul(o[:, :], memT[:, c, TO[i]:TO[i] + P], w[:, c, :], start=(c == 0), stop=(c == KC - 1))
                    mm.then_inc(al.full, 1)
                    nbank += 1
                    if nbank % 2 == 0:
                        w_done.append((al.full, al.filled))

            w = None
            memory_banks(2)
            sample_output_turns()
            for i in range(3):
                need("og_ready")
                turn([o_n[0:TW[i], i, q * P:(q + 1) * P] for q in range(4)], TW[i])
            need("qkT_ready", 6)

            def prompt_scores(i):
                for g in range(4):
                    o = dl.open(pe)
                    r = g % 2
                    for j in range(2):
                        hp = g // 2 * 2 + j
                        mm = pe.matmul(o[:, j * 256:(j + 1) * 256], qT[64 * r:64 * r + 64, hp, TO[i]:TO[i] + P],
                                       kT[64 * r:64 * r + 64, hp, 0:256], start=True, stop=True)
                    mm.then_inc(dl.full, 1)

            def prompt_turns():
                need("p_ready")
                for g in range(4):
                    turn([Sb[:, 2 * g + j // 2, (j % 2) * P:(j % 2 + 1) * P] for j in range(4)], P)

            def prompt_values():
                need("pT_ready", 4)
                o = dl.open(pe)
                for h in range(MH):
                    for kt in range(2):
                        mm = pe.matmul(o[64 * (h % 2):64 * (h % 2) + 64, (h // 2) * P:(h // 2 + 1) * P],
                                       zv[:, kt, h * MD:(h + 1) * MD], pT[:, 2 * h + kt, :],
                                       start=(kt == 0), stop=(kt == 1), skip_group_check=True)
                mm.then_inc(dl.full, 1)

            sample_turns(1)
            prompt_scores(0)
            need("psT_ready", 5)
            o = el.open(pe)
            sample_values(o, 4)
            memory_banks(1)
            sample_values(o, 4)
            memory_banks(1)
            prompt_turns()
            sample_values(o, 4)
            prompt_values()
            prompt_scores(1)
            sample_values(o, 4)
            memory_banks(1)
            sample_values(o, 4)
            prompt_turns()
            memory_banks(1)
            sample_values(o, 4)
            prompt_values()
            sample_values(o, 4)
            sample_values(o, 4).then_inc(el.full, 1)
            memory_banks(1)
            sample_output_turns()
            memory_banks(1)
            need("mixT_ready", 8 + 3 + 2)
            natural(hT, dl, before_samples=("mixT_ready", 8))
            natural(hT, dl)
            norm_turns()
            need("hT_ready", 6)
            transposed(hT, al)
            need("mk_ready", 8)
            for i in range(2):
                for g in range(2):
                    turn([mkn[:, i, (4 * g + j) * P:(4 * g + j + 1) * P] for j in range(4)], P)
            transposed(hT, al)
            need("mkT_ready", 4)
            need("q2T_ready", 8)
            for i in range(2):
                for g in range(2):
                    o = dl.open(pe)
                    for j in range(2):
                        for c in range(2):
                            f = 4 * g + 2 * j + c
                            mm = pe.matmul(o[:, j * 256:(j + 1) * 256], q2T[:, f, TO[i]:TO[i] + P], mkT[:, f, :],
                                           start=(c == 0), stop=(c == 1))
                    mm.then_inc(dl.full, 1)
            nm = 0

            def next_memory():
                nonlocal nm
                pe.wait_ge(S(f"mem{nm % 5}"), 16 * (nm // 5 + 1))
                nm += 1
                return memkv[(nm - 1) % 5]

            need("QM_ready")
            o = dl.open(pe)
            for b in range(NB):
                mk = next_memory().rearrange("p a b -> p (a b)").rearrange("p (c m) -> p c m", m=256)
                for c in range(KC):
                    mm = pe.matmul(o[b // 2 * 32:b // 2 * 32 + 32, 0:256], QM[:, c, b, :], mk[:, c, :],
                                   start=(b % 2 == 0 and c == 0), stop=(b % 2 == 1 and c == KC - 1), skip_group_check=True)
                if b < NB - 1:
                    mm.then_inc(S("mk_used"), 1)
                    mem_done.append((S("mk_used"), b + 1))
                else:
                    mm.then_inc(dl.full, 1)
                    mem_done.append((dl.full, dl.filled))
            for i in range(2):
                need("p2_ready")
                for g in range(2):
                    turn([S2[i][:, 2 * g + j // 2, (j % 2) * P:(j % 2 + 1) * P] for j in range(4)], P)
            need("p2s_ready")
            turn([S2s[:, 0, kt * P:(kt + 1) * P] for kt in range(2)], P)
            for i in range(2):
                need("p2T_ready", 2)
                for g in range(2):
                    o = dl.open(pe)
                    for j in range(4):
                        f = 4 * g + j
                        for kt in range(2):
                            mm = pe.matmul(o[:, j * P:(j + 1) * P], mvn[:, kt, f * P:(f + 1) * P],
                                           p2T[i][:, f // 2 * 2 + kt, :], start=(kt == 0), stop=(kt == 1))
                    mm.then_inc(dl.full, 1)
            need("pM_ready")
            oo = [el.open(pe), el.open(pe)]
            for b in range(NB):
                mv = next_memory()
                for c in range(2):
                    for kt in range(2):
                        mm = pe.matmul(oo[c][b // 2 * 32:b // 2 * 32 + 32, :], pM[:, kt, b, :], mv[:, kt, 512 * c:512 * c + 512],
                                       start=(b % 2 == 0 and kt == 0), stop=(b % 2 == 1 and kt == 1), skip_group_check=True)
                    if b == NB - 1:
                        mm.then_inc(el.full, 1)
                if b < NB - 1:
                    mm.then_inc(S("mv_used"), 1)
                    mem_done.append((S("mv_used"), b + 1))
            for g in range(2):
                need("osb2_ready")
                turn([osb2[:, (4 * g + j) * P:(4 * g + j + 1) * P] for j in range(4)], P)
            need("o2T_ready", 12)
            natural(hT, dl)
            natural(hT, dl)
            norm_turns()
            pe.wait_ge(S("subkeys"), 16)

            def router_queries(g, lo, hi):
                k = len(stream) - 4 + g
                pe.wait_ge(S(f"w{slot_of[k]}"), 16 * slot_of[0:k + 1].count(slot_of[k]))
                w = wslot[slot_of[k]].rearrange("p (c n) -> p c n", c=KC)
                for f in range(4):
                    o = al.open(pe)
                    for c in range(KC):
                        mm = pe.matmul(o[:, 0:hi - lo], w[:, c, f * P:(f + 1) * P], hT[:, c, lo:hi],
                                       start=(c == 0), stop=(c == KC - 1))
                    mm.then_inc(al.full, 1)

            def router_scores(i, g):
                o = dl.open(pe)
                for j in range(4):
                    f = 4 * g + j
                    mm = pe.matmul(o[0:TW[i], j * P:(j + 1) * P], qvT[:, f, TO[i]:TO[i] + TW[i]],
                                   skT[:, (f % 2) * PH + f // 2, :], start=True, stop=True)
                mm.then_inc(dl.full, 1)

            need("hT_ready", 2)
            router_queries(0, 0, P)
            need("qvT_ready", 4)
            router_scores(0, 0)
            router_queries(1, 0, P)
            for g in range(2, 4):
                router_queries(g, 0, P)
                need("qvT_ready", 4)
                router_scores(0, g - 1)
            need("hT_ready", 4)
            for g in range(4):
                router_queries(g, P, T)
                w_done.append((al.full, al.filled))
                if g == 0:
                    need("qvT_ready", 4)
                    router_scores(0, 3)
            need("qvT_ready", 16)
            for g in range(4):
                router_scores(1, g)
            nv = 0
            for m, (i, k) in enumerate(runs):
                w = TW[i]
                if k == 0:
                    oo = [el.open(pe), el.open(pe)]
                last = k == len([r for r in runs if r[0] == i]) - 1
                for j in range(RUN):
                    n = row_at["v", i, k * RUN + j]
                    pe.wait_ge(S(f"g{n % GSLOT}"), 16 * (n // GSLOT + 1))
                    need("diag_ready")
                    turns, r0 = (1, 0) if i < 2 else (2, 32 * (j % 2))
                    for c in range(2):
                        mm = pe.matmul(oo[c][r0:r0 + w, :], diag[nv % 4][:, 0:w], gslot[n % GSLOT][:, 512 * c:512 * c + 512],
                                       start=(k == 0 and j < turns), stop=(last and j >= RUN - turns), skip_group_check=True)
                        if last and j == RUN - 1:
                            mm.then_inc(el.full, 1)
                    nv += 1
                    if not (last and j == RUN - 1):
                        mm.then_inc(S("v_row_used"), 1)
                        v_done[nv - 1] = (S("v_row_used"), nv - sum(1 for q in v_done if v_done[q][0] is el.full))
                    else:
                        v_done[nv - 1] = (el.full, el.filled)
                if (i, k) == (0, 4):
                    for g in range(4):
                        router_scores(2, g)

        @block.vector
        def _(v):
            counts = {}

            def link(ins, name="v_chain"):
                counts[name] = counts.get(name, 0) + 1
                ins.then_inc(S(name), 1)
                v.wait_ge(S(name), counts[name])

            def freed(ins, lane):
                ins.then_inc(lane.free, 1)
                v.wait_ge(lane.free, lane.taken)

            seen = {}

            def need(name, n=1):
                seen[name] = seen.get(name, 0) + n
                v.wait_ge(S(name), seen[name])

            def signal(name):
                link(v.memset(stat[:, 63:64], 0.0), name)

            def rsqrt_mean(dst, src, n):
                link(v.tensor_scalar(dst, src, 1.0 / n, EPS, ALU.mult, ALU.add), "to_sqrt")
                roots.append(dst)
                need("sqrt_done")
                link(v.reciprocal(dst, dst))

            def norm(src, w, name):
                link(v.tensor_tensor_reduce(xs[0:w, :], src, src, 1.0, 0.0, ALU.mult, ALU.add, stat[0:w, 0:1]))
                rsqrt_mean(stat[0:w, 1:2], stat[0:w, 0:1], D)
                link(v.tensor_scalar(xs[0:w, :], src, stat[0:w, 1:2], None, ALU.mult), name)

            def norm_diag(i):
                w = TW[i]
                need("root_ready")
                link(v.reciprocal(x_rstd[0:w, i:i + 1], x_rstd[0:w, i:i + 1]))
                link(v.tensor_scalar(xs[0:w, i * P:i * P + w], ident[0:w, 0:w], x_rstd[0:w, i:i + 1], None, ALU.mult),
                     "norm_diag_ready")

            def norm_turned(gain):
                for i in range(3):
                    for j in range(2):
                        o = dl.take(v)[:, :].rearrange("p (a b) -> p a b", b=128)[:, :, 0:TW[i]]
                        link(v.tensor_tensor(hT[:, 4 * j:4 * j + 4, TO[i]:TO[i] + TW[i]], o,
                                             bc(gain[:, 4 * j:4 * j + 4], 2, TW[i]), ALU.mult), "hT_ready")
                        freed(v.memset(stat[:, 62:63], 0.0), dl)

            def empty(dst, src_of, name, lane=None, op=None):
                lane = lane or dl
                o = lane.take(v)
                link(op(dst, src_of(o)) if op else v.tensor_copy(dst, src_of(o)), name)
                freed(v.memset(stat[:, 62:63], 0.0), lane)

            def as4(o, n=4, w=128):
                return o[:, 0:n * 128].rearrange("p (a b) -> p a b", b=128)[:, :, 0:w]

            def softmax(buf, heads, name):
                b = buf[:, 0:heads, :]
                m = stat[:, 2:2 + heads]
                link(v.tensor_reduce(m, b, AX.X, ALU.max))
                link(v.tensor_tensor(b, b, bc(m, 2, 256), ALU.subtract), "to_exp")
                need("exp_done")
                link(v.tensor_reduce(m, b, AX.X, ALU.add))
                link(v.reciprocal(m, m))
                link(v.tensor_tensor(b, b, bc(m, 2, 256), ALU.mult), name)

            v.wait_ge(S("consts"), 16)
            v.wait_ge(S("small"), 16 * 7)
            for i in range(3):
                norm_diag(i)
            norm_turned(gains[:, 0, :])
            v.wait_ge(S("table_in"), 16)
            link(v.tensor_copy(xs[:, 0:128], table[:, :]))
            for r in range(2):
                rr = slice(64 * r, 64 * r + 64)
                link(v.tensor_scalar(xs[rr, 128:192], xs[rr, r:128:2], 64.0, C("half_row")[rr, :], ALU.mult, ALU.add))
            link(v.tensor_copy(block_ix[:, :], xs[:, 128:192]))
            link(v.tensor_scalar(xs[:, 0:128], xs[:, 0:128], float(P), C("row"), ALU.mult, ALU.add))
            link(v.tensor_copy(page_ix[:, :], xs[:, 0:128]), "block_ix_ready")
            need("qk_ready", 6)
            rt = [xs[:, 64 * j:64 * j + 64].rearrange("p (h d) -> p h d", h=8) for j in range(4)]
            for i in range(3):
                w = TW[i]
                for n, z in enumerate((zq, zk)):
                    zz = z[0:w, i, :].rearrange("p (h d) -> p h d", h=8)
                    x1, x2 = zz[:, :, 0:8], zz[:, :, 8:16]
                    co, si = bc(rope[0:w, i, 0:8], 1, 8), bc(rope[0:w, i, 8:16], 1, 8)
                    a = [r[0:w] for r in rt]
                    link(v.tensor_tensor(a[0], x1, co, ALU.mult))
                    link(v.tensor_tensor(a[1], x2, si, ALU.mult))
                    link(v.tensor_tensor(a[2], x2, co, ALU.mult))
                    link(v.tensor_tensor(a[3], x1, si, ALU.mult))
                    link(v.tensor_tensor(x1, a[0], a[1], ALU.subtract))
                    link(v.tensor_tensor(x2, a[2], a[3], ALU.add), "rope_done" if n else "v_chain")
            for i in range(3):
                for z in (qT, kT):
                    empty(z[:, :, TO[i]:TO[i] + TW[i]], lambda o: as4(o, 4, TW[i]), "qkT_ready")
            link(v.memset(QB, 0.0))
            for r in range(2):
                rr = slice(64 * r, 64 * r + 64)
                for hp in range(4):
                    link(v.tensor_copy(QB[rr, hp, :, 8 * hp + 4 * r:8 * hp + 4 * r + 4],
                                       qT[rr, hp, NP_TOK:T].rearrange("p (b t) -> p b t", t=4)))
            signal("QB_ready")
            def sample_scores(g, q):
                empty(Sm[g][:, 512 * q:512 * q + 512], lambda o: o[:, :], "v_chain", el,
                      op=lambda d, s: v.tensor_scalar(d, s, MD ** -0.5, None, ALU.mult))

            for f in range(2):
                empty(t1, lambda o: o[:, 0:T], "v_chain",
                      op=lambda d, s: v.tensor_scalar(d, s, b_al[:, f:f + 1], None, ALU.add))
                link(v.tensor_scalar(t2, t1, -1.0, None, ALU.mult))
                link(v.tensor_scalar(la[:, f, :], t1, 0.0, None, ALU.min))
                link(v.tensor_tensor(t1, t1, t2, ALU.min), "to_log1p")
                need("log1p_done")
                link(v.tensor_tensor(la[:, f, :], la[:, f, :], t1, ALU.subtract))
                link(v.tensor_scalar(la[:, f, :], la[:, f, :], 1.0 / 16, None, ALU.mult))
                link(v.tensor_tensor_scan(t2, reset, la[:, f, :], 0.0, ALU.mult, ALU.add))
                link(v.tensor_copy(la[:, f, :], t2))
            for f in range(2):
                for lo, n, c in ((0, 8, GC), (NP_TOK, NB, NT)):
                    A = la[:, f, lo:lo + n * c].rearrange("p (a b) -> p a b", b=c)
                    link(v.tensor_tensor(dk[:, f, lo:lo + n * c].rearrange("p (a b) -> p a b", b=c),
                                         A[:, :, c - 1:c].to_broadcast([P, n, c]), A, ALU.subtract))
            signal("A_ready")
            need("eA_done")
            link(v.tensor_tensor(dk, dk, gT[:, 2:4, :], ALU.mult), "kd_ready")
            link(v.tensor_tensor(qe, eA, gT[:, 0:2, :], ALU.mult))
            for i in range(3):
                empty(kdn[0:TW[i], i, :], lambda o: o[0:TW[i], 0:256], "kdn_ready")
            for f in range(2):
                link(v.tensor_tensor(qem[:, f, :, :], bc(qe[:, f, NP_TOK:T], 1, NB), bmask, ALU.mult))
            signal("qe_ready")
            link(v.tensor_tensor(kdm[0:32, :, :], bc(kdn[0:32, 2, :], 1, NB), bc(rowmask[0:32, :], 2, 256), ALU.mult),
                 "kdm_ready")
            v.wait_ge(S("state_in"), 32)
            for c in range(NP_TOK // GC):
                o = dl.take(v)
                for f in range(2):
                    for r in range(2):
                        rr = slice(64 * r, 64 * r + 64)
                        u = o[rr, f * 256 + r * 128:f * 256 + r * 128 + 128]
                        if c == 0:
                            link(v.tensor_copy(St_p[rr, 0, f, :], u))
                        else:
                            link(v.scalar_tensor_tensor(St_p[rr, c, f, :], St_p[rr, c - 1, f, :],
                                                        eA[rr, f, c * GC + GC - 1:c * GC + GC], u, ALU.mult, ALU.add))
                signal("state_ready")
                freed(v.memset(stat[:, 62:63], 0.0), dl)
            sample_scores(0, 0)
            for f in range(2):
                link(v.tensor_tensor(St_n[:, :, f, :], St_s[:, :, f, :], bc(eA[:, f, NP_TOK + NT - 1:T:NT], 2, 128), ALU.mult))
            for b in range(NB):
                o = dl.take(v)[:, :].rearrange("p (f r d) -> p f r d", f=2, r=2)
                for r in range(2):
                    rr = slice(64 * r, 64 * r + 64)
                    link(v.tensor_tensor(St_n[rr, b, :, :], St_n[rr, b, :, :], o[rr, :, r, :], ALU.add))
                freed(v.memset(stat[:, 62:63], 0.0), dl)
            signal("newstate_ready")
            for f in range(2):
                A = la[:, f, 0:NP_TOK].rearrange("p (c a b) -> p c a b", a=2, b=16)
                mid = A[:, :, 0, 15:16].to_broadcast([P, 8, 16])
                link(v.tensor_tensor(halves[:, f, :, 0, :], mid, A[:, :, 0, :], ALU.subtract))
                link(v.tensor_tensor(halves[:, f, :, 1, :], A[:, :, 1, :], mid, ALU.subtract))
            signal("to_halves")
            need("halves_done")
            for f in range(2):
                for a, src in ((0, gT[:, 2 + f]), (1, gT[:, f])):
                    link(v.tensor_tensor(halves[:, f, :, a, :], halves[:, f, :, a, :],
                                         src[:, 0:NP_TOK].rearrange("p (c a b) -> p c a b", a=2, b=16)[:, :, a, :], ALU.mult))
            signal("halves_ready")
            units = [(i, f, c) for i in range(3) for f in range(2) for c in range(4 if i < 2 else 1)]

            def ends(n):
                return n + 1 == len(units) or units[n + 1][0:2] != units[n][0:2]

            def decay(n):
                i, f, c = units[n]
                if n >= 3:
                    v.wait_ge(S("pairs_used"), sum(not ends(q) for q in range(n - 2)))
                s0 = TO[i] + c * GC
                A = la[:, f, s0:s0 + 32].rearrange("p (a b) -> p a b", b=16)
                link(v.tensor_tensor(X[n % 3].rearrange("p (a t) s -> p a t s", a=2), bc(A, 3, 16), bc(A, 2, 16),
                                     ALU.subtract))
                link(v.tensor_scalar(X[n % 3], X[n % 3], 0.0, None, ALU.min), "to_decay")

            def new_keys(g):
                empty(Sm[g][:, PAST:PAST + 32], lambda o: o[:, 0:32], "v_chain",
                      op=lambda d, s: v.scalar_tensor_tensor(d, s, MD ** -0.5, newmask[:, g, :], ALU.mult, ALU.add))

            def sample_softmax(g):
                S_ = Sm[g]
                past = S_[:, 0:PAST].rearrange("p (a b) -> p a b", b=256)
                gt, top, pen = stat[:, 8:16], stat[:, 16:24], stat[:, 24:32]
                link(v.tensor_reduce(gt, past, AX.X, ALU.add))
                link(v.max(top, gt))
                link(v.max_index(sel_ix[:, :], top, gt))
                link(v.tensor_copy(top, sel_ix[:, :]))
                link(v.tensor_tensor(sel, bc(iota[:, 0:8], 1, 3), bc(top[:, 0:3], 2, 8), ALU.is_equal))
                link(v.tensor_reduce(pen, sel.rearrange("p a b -> p b a"), AX.X, ALU.add))
                link(v.tensor_scalar(pen, pen, 1.0, -NEG, ALU.subtract, ALU.mult))
                link(v.tensor_tensor(past, past, bc(pen, 2, 256), ALU.add))
                m = stat[:, 32:33]
                link(v.tensor_reduce(m, S_, AX.X, ALU.max))
                link(v.tensor_scalar(m, m, -1.0, None, ALU.mult), "to_exps")
                need("exps_done")
                link(v.reciprocal(stat[:, 34:35], stat[:, 33:34]))
                link(v.tensor_scalar(S_, S_, stat[:, 34:35], None, ALU.mult), "ps_ready")

            def sample_turned(g):
                for k in range(4):
                    empty(pTs[g][:, 4 * k:4 * k + 4, :], as4, "psT_ready")
                empty(pTn[g][0:32, :], lambda o: o[0:32, 0:128], "psT_ready")

            for q in (1, 2):
                sample_scores(0, q)
            full_at = {}
            for q in range(KAHEAD // 8, 8):
                n = min(u for u in range(18) if KAHEAD + sum(KEYS_AT[0:u + 1]) + (KEYS_MORE if u > 3 else 0) >= 8 * q + 8)
                full_at[n + 1] = q
            assert len(full_at) == 8 - KAHEAD // 8 and max(full_at) < 18
            decay(0)
            for n, (i, f, c) in enumerate(units):
                if n + 1 < len(units):
                    decay(n + 1)
                buf, s0 = X[n % 3].rearrange("p (a t) s -> p a t s", a=2), TO[i] + c * GC
                q, k = [gT[:, ff, s0:s0 + 32].rearrange("p (a b) -> p a b", b=16) for ff in (f, 2 + f)]
                need("decay_done")
                link(v.tensor_tensor(buf, buf, bc(k, 2, 16), ALU.mult))
                link(v.tensor_tensor(buf, buf, bc(q, 3, 16), ALU.mult), "pairs_ready")
                if n in full_at:
                    sample_scores(full_at[n] // 4, full_at[n] % 4)
                if n == 10:
                    v.wait_ge(S("mem_in"), 16)
                    v.wait_ge(S("z_ready"), 9)
                    link(v.tensor_tensor(mem_sq, memT, memT, ALU.mult), "mem_sq_ready")
                    link(v.tensor_tensor(memT, memT, bc(gains[:, 2, :], 2, 256), ALU.mult), "memT_ready")
                if not ends(n):
                    continue
                w = TW[i]
                gm = C("gmask", 32, 16) if i < 2 else C("gmask_s", 32, 16)
                for r in range(2):
                    o = dl.take(v)[0:w, :].rearrange("p (a b) -> p a b", b=16)
                    link(v.tensor_tensor(masked[0:w], o, gm[0:w], ALU.mult))
                    freed(v.memset(stat[:, 62:63], 0.0), dl)
                    link(v.tensor_reduce(att[0:w, i, 2 * f + r, :], masked[0:w], AX.X, ALU.add), "att_ready")
                if n == 3:
                    new_keys(0)
                    sample_softmax(0)
                if n == 7:
                    sample_turned(0)
                if n == 11:
                    empty(mem_rstd, lambda o: o[:, 0:2], "v_chain")
                    rsqrt_mean(mem_rstd, mem_rstd, D)
                    signal("mem_rstd_ready")
            for i in range(2):
                for r in range(2):
                    a = att[:, i, r:r + 3:2, 16:32]
                    empty(a, lambda o: o[:, 0:32].rearrange("p (a b) -> p a b", b=16), "att_ready",
                          op=lambda d, s: v.scalar_tensor_tensor(d, s, C("first_half"), d, ALU.mult, ALU.add))
            new_keys(1)
            sample_softmax(1)
            def sample_output(g):
                o = dl.take(v)[:, :].rearrange("p (a b h t) -> p a b h t", a=4, b=4, h=8)
                for h in range(MH):
                    rr = slice(64 * (h % 2), 64 * (h % 2) + 64)
                    dst = hT[rr, h // 2, NP_TOK + 16 * g:NP_TOK + 16 * g + 16].rearrange("p (b t) -> p b t", t=4)
                    link(v.tensor_copy(dst, o[rr, h // 2, :, h, :]), "mixT_ready")
                freed(v.memset(stat[:, 62:63], 0.0), dl)

            for i in range(3):
                w = TW[i]
                for r in range(2):
                    empty(o_n[0:w, i, :].rearrange("p (f r d) -> p r f d", r=2, d=128)[:, r],
                          lambda o: o[0:w, 0:256].rearrange("p (f d) -> p f d", d=128), "v_chain")
                oo = o_n[0:w, i, :].rearrange("p (h d) -> p h d", h=4)
                m = stat[0:w, 2:6]
                sq = xs[0:w, 0:512].rearrange("p (h d) -> p h d", h=4)
                link(v.tensor_tensor(sq, oo, oo, ALU.mult))
                link(v.tensor_reduce(m, sq, AX.X, ALU.add))
                rsqrt_mean(m, m, 128)
                link(v.tensor_tensor(oo, oo, bc(m, 2, 128), ALU.mult))
                link(v.tensor_tensor(oo, oo, bc(g_gla_b[0:w, :], 1, 4), ALU.mult))
                if i == 0:
                    v.wait_ge(S("z_ready"), 9)
                link(v.tensor_tensor(o_n[0:w, i, :], o_n[0:w, i, :], zr[0:w, i, :], ALU.mult), "og_ready")
            sample_output(0)
            for i in range(3):
                empty(hT[:, 4:8, TO[i]:TO[i] + TW[i]], lambda o: as4(o, 4, TW[i]), "mixT_ready")
            v.wait_ge(S("stored1"), 16 * 4)
            def prompt_softmax(i):
                for g in range(4):
                    h = g // 2 * 4 + g % 2
                    empty(Sb[:, h:h + 3:2, :], lambda o: o[:, :].rearrange("p (a b) -> p a b", b=256), "v_chain",
                          op=lambda d, s: v.scalar_tensor_tensor(d, s, MD ** -0.5, bc(causal[:, i, :], 1, 2),
                                                                 ALU.mult, ALU.add))
                softmax(Sb, 8, "p_ready")

            def prompt_turned():
                for g in range(4):
                    empty(pT[:, 4 * g:4 * g + 4, :], as4, "pT_ready")

            sample_turned(1)
            for i in range(2):
                prompt_softmax(i)
                prompt_turned()
                empty(hT[:, 0:4, TO[i]:TO[i] + P], as4, "mixT_ready")
            empty(osb, lambda o: o[:, :], "osb_ready", el)
            sample_output(1)

            def residual():
                for c in range(2):
                    for i in range(3):
                        d = x[0:TW[i], i, 512 * c:512 * c + 512]
                        if i < 2:
                            empty(d, lambda o: o[:, :], "x_ready" if c else "v_chain",
                                  op=lambda d, s: v.tensor_tensor(d, d, s, ALU.add))
                        else:
                            o = dl.take(v)
                            quarters = xs[0:32, 512:1024]
                            for q in range(4):
                                link(v.tensor_copy(quarters[:, q * P:(q + 1) * P], o[32 * q:32 * q + 32, 0:P]))
                            link(v.tensor_tensor(d, d, quarters, ALU.add), "x_ready" if c else "v_chain")
                            freed(v.memset(stat[:, 62:63], 0.0), dl)
                        if c and i:
                            norm_diag(i - 1)
                norm_diag(2)

            residual()
            norm_turned(gains[:, 1, :])
            for i in range(2):
                for g in range(2):
                    empty(mkT[:, 4 * g:4 * g + 4, i * P:(i + 1) * P], as4, "mkT_ready")
            link(v.memset(QM, 0.0))
            link(v.memset(pM, 0.0))
            need("q2T_ready", 8)
            for r in range(2):
                for h in range(4):
                    link(v.tensor_copy(QM[:, 2 * h:2 * h + 2, r::2, 16 * r + 4 * h:16 * r + 4 * h + 4],
                                       q2T[:, 2 * h:2 * h + 2, NP_TOK:T].rearrange("p f (g r t) -> p f g r t", r=2, t=NT)[:, :, :, r]))
            signal("QM_ready")
            for i in range(2):
                for g in range(2):
                    empty(S2[i][:, 2 * g:2 * g + 2, :], lambda o: o[:, :].rearrange("p (a b) -> p a b", b=256), "v_chain",
                          op=lambda d, s: v.tensor_scalar(d, s, 1.0 / 16, None, ALU.mult))
                softmax(S2[i], 4, "p2_ready")
            empty(S2s[:, 0, :], lambda o: o[:, 0:256], "v_chain",
                  op=lambda d, s: v.tensor_scalar(d, s, 1.0 / 16, None, ALU.mult))
            softmax(S2s, 1, "p2s_ready")
            for i in range(2):
                for g in range(2):
                    empty(p2T[i][:, 4 * g:4 * g + 4, :], as4, "p2T_ready")
            o = dl.take(v)[:, 0:256].rearrange("p (k g r c) -> p k g r c", k=2, r=2, c=16)
            for kt in range(2):
                for r in range(2):
                    link(v.tensor_copy(pM[:, kt, r::2, 16 * r:16 * r + 16], o[:, kt, :, r, :]))
            freed(v.memset(stat[:, 62:63], 0.0), dl)
            signal("pM_ready")
            for i in range(2):
                for g in range(2):
                    empty(hT[:, 4 * g:4 * g + 4, TO[i]:TO[i] + P], as4, "o2T_ready")
            for c in range(2):
                empty(osb2[:, 512 * c:512 * c + 512], lambda o: o[:, :], "osb2_ready", el)
            for g in range(2):
                o = dl.take(v)[:, :].rearrange("p (f b h t) -> p f b h t", f=4, b=NB, h=4)
                for h in range(2 * g, 2 * g + 2):
                    for f in range(2):
                        link(v.tensor_copy(hT[:, 2 * h + f, NP_TOK:T].rearrange("p (b t) -> p b t", t=NT),
                                           o[:, 2 * (h % 2) + f, :, h, :]), "o2T_ready")
                freed(v.memset(stat[:, 62:63], 0.0), dl)
            residual()

            norm_turned(g_ffn_t)
            v.wait_ge(S("stored2"), 16 * 2)
            v.wait_ge(S("g_row"), 16)

            def scaled_rows(i):
                w = TW[i]
                link(v.scalar_tensor_tensor(xn[0:w, i, :], x[0:w, i, :], x_rstd[0:w, i:i + 1], g_row[0:w, :],
                                            ALU.mult, ALU.mult))

            def top16(vals, spare, out_v, out_i):
                link(v.max(out_v[:, 0:8], vals))
                link(v.max_index(out_i[:, 0:8], out_v[:, 0:8], vals))
                link(v.match_replace(spare, out_v[:, 0:8], vals, -3e38))
                link(v.max(out_v[:, 8:16], spare))
                link(v.max_index(out_i[:, 8:16], out_v[:, 8:16], spare))

            def route(i, piece):
                w = TW[i]
                if piece < 4:
                    empty(sc[0:w, :, :], lambda o: as4(o)[0:w], "v_chain")
                    for j in range(4):
                        f = 4 * piece + j
                        top16(sc[0:w, j, :], sc2[0:w, j, :], ts[0:w, f, :], ti[0:w, f, :])
                    hh, ff = slice(2 * piece, 2 * piece + 2), slice(4 * piece, 4 * piece + 4)
                    link(v.tensor_tensor(cand[0:w].rearrange("p h (a b) -> p h a b", b=16), bc(ts[0:w, ff.start:ff.stop:2, :], 3, 16),
                                         bc(ts[0:w, ff.start + 1:ff.stop:2, :], 2, 16), ALU.add))
                    for j in range(2):
                        h = 2 * piece + j
                        top16(cand[0:w, j, :], cand2[0:w, :], fs[0:w, h, :], fpos[0:w, h, :])
                    link(v.tensor_copy(tif[0:w, ff, :], ti[0:w, ff, :]))
                    link(v.tensor_single_scalar(posn[0:w, 0::2, :], fpos[0:w, hh, :], 4, ALU.logical_shift_right))
                    link(v.tensor_single_scalar(posn[0:w, 1::2, :], fpos[0:w, hh, :], 15, ALU.bitwise_and))
                    link(v.tensor_copy(posf[0:w, ff, :], posn[0:w, :, :]))
                    iota4 = iota[0:w, :].unsqueeze(1).unsqueeze(1).to_broadcast([w, 4, TOPK, TOPK])
                    hot_ = hot[piece][0:w]
                    link(v.tensor_tensor(hot_, iota4, bc(posf[0:w, ff, :], 3, 16), ALU.is_equal), "hot_ready")
                    if i == 0:
                        return
                    link(v.tensor_tensor(hot_, hot_, bc(tif[0:w, ff, :], 2, 16), ALU.mult))
                    link(v.tensor_reduce(keyno[0:w, ff, :], hot_, AX.X, ALU.add))
                    return
                if piece > 4:
                    return
                if i == 0:
                    need("keyno_ready", 4)
                ef = eidf[0:w, i, :].rearrange("p (h k) -> p h k", h=PH)
                link(v.scalar_tensor_tensor(ef, keyno[0:w, 0::2, :], float(NKEY), keyno[0:w, 1::2, :], ALU.mult, ALU.add))
                link(v.tensor_copy(eid[0:w, i, :], eidf[0:w, i, :]), "eid_ready")
                if i == 0:
                    scaled_rows(0)
                gg = gate[0:w, i, :].rearrange("p (h k) -> p h k", h=PH)
                m = stat[0:w, 40:48]
                link(v.tensor_tensor(gg, fs[0:w], fs[0:w, :, 0:1].to_broadcast([w, PH, TOPK]), ALU.subtract), "to_exp")
                need("exp_done")
                link(v.tensor_reduce(m, gg, AX.X, ALU.add))
                link(v.reciprocal(m, m))
                link(v.tensor_tensor(gg, gg, bc(m, 2, 16), ALU.mult))
                if i == 2:
                    for g in range(4):
                        link(v.tensor_copy(eid_s[32 * g:32 * g + 32, :], eid[0:32, 2, 32 * g:32 * g + 32]), "eid_s_ready")
                        link(v.tensor_copy(gate_s[32 * g:32 * g + 32, :], gate[0:32, 2, 32 * g:32 * g + 32]))

            def finish(i):
                w = TW[i]
                for g in range(2):
                    d = x[0:w, i, 512 * g:512 * g + 512]
                    o = el.take(v)
                    if i == 2:
                        link(v.tensor_copy(xs[0:w, 0:512], o[32:64, :]))
                        link(v.tensor_tensor(d, d, xs[0:w, 0:512], ALU.add))
                    link(v.tensor_tensor(d, d, o[0:w, :], ALU.add))
                    freed(v.memset(stat[:, 62:63], 0.0), el)
                norm(x[0:w, i, :], w, "v_chain")
                if i == 0:
                    v.wait_ge(S("g_row"), 32)
                link(v.tensor_tensor(x[0:w, i, :], xs[0:w, :], g_row[0:w, :], ALU.mult), "y_ready")

            for piece in range(5):
                route(0, piece)
            for m, (i, k) in enumerate(runs):
                for j in range(RUN * k, RUN * k + RUN):
                    n = row_at["u", i, j]
                    v.wait_ge(S(f"g{n % GSLOT}"), 16 * (n // GSLOT + 1))
                    row = gslot[n % GSLOT]
                    dst, xr = (dots[:, i, j:j + 1], xn[:, i, :]) if i < 2 else (dots_s[:, j:j + 1], xns)
                    link(v.tensor_tensor_reduce(row, row, xr, 1.0, 0.0, ALU.mult, ALU.add, dst), "dot_done")
                signal("to_gelu")
                if m >= 2 and runs[m - 2][0] != runs[m - 1][0]:
                    finish(runs[m - 2][0])
                if i < 2:
                    route(i + 1, k)
                if m == 2:
                    scaled_rows(1)
                if m == 4:
                    scaled_rows(2)
                    for g in range(4):
                        link(v.tensor_copy(xns[32 * g:32 * g + 32, :], xn[0:32, 2, :]), "g_row_used")
                need("gelu_done")
                c = slice(RUN * k, RUN * k + RUN)
                gt, dt_ = (gate[:, i, c], dots[:, i, c]) if i < 2 else (gate_s[:, c], dots_s[:, c])
                link(v.tensor_tensor(gt, gt, dt_, ALU.mult), "coef_ready")
            finish(2)

        @block.scalar
        def _(a):
            counts, seen = {}, {}

            def link(ins, name="a_chain"):
                counts[name] = counts.get(name, 0) + 1
                ins.then_inc(S(name), 1)
                a.wait_ge(S(name), counts[name])

            def need(name, n=1):
                seen[name] = seen.get(name, 0) + n
                a.wait_ge(S(name), seen[name])

            def empty(dst, src_of, name, scale=1.0, func=ACT.Copy):
                o = al.take(a)
                link(a.activation(dst, src_of(o), func, scale=scale), name)
                link(a.activation(junk, junk, ACT.Copy), "a_free")

            junk = sb("junk", [1, 1])[:, :]
            a.wait_ge(S("consts"), 16)
            link(a.activation(junk, cst[0:1, 0:1], ACT.Copy))

            def square_roots(n):
                for _ in range(n):
                    r = roots[seen.get("to_sqrt", 0)]
                    need("to_sqrt")
                    link(a.activation(r, r, ACT.Sqrt), "sqrt_done")

            def norm_roots():
                for i in range(3):
                    w, r = TW[i], x_rstd[0:TW[i], i:i + 1]
                    if counts.get("root_ready", 0) < 3:
                        a.wait_ge(S("x_in"), 48)
                    else:
                        need("x_ready")
                    link(a.activation(squares[0:w, :], x[0:w, i, :], ACT.Square, accum_out=r))
                    link(a.activation(r, r, ACT.Sqrt, bias=C("eps")[0:w, :], scale=1.0 / D), "root_ready")

            norm_roots()
            def projection(z, tiles, name, func=ACT.Copy):
                for i in tiles:
                    if i < 2:
                        empty(z[:, i, :], lambda o: o[:, :], name, func=func)
                        continue
                    o = al.take(a)
                    for q in range(4):
                        link(a.activation(z[0:32, 2, q * P:(q + 1) * P], o[32 * q:32 * q + 32, 0:P], func),
                             name if q == 3 else "a_chain")
                    link(a.activation(junk, junk, ACT.Copy), "a_free")

            for z in (zq, zk):
                projection(z, range(3), "qk_ready")
            for f in range(4):
                empty(gT[:, f, :], lambda o: o[:, 0:T], "gT_ready", scale=0.125 if f < 2 else 1.0)
            empty(agT[0:16, :], lambda o: o[0:16, 0:T], "gT_ready")
            projection(zv, range(3), "z_ready")
            for f in range(2):
                need("to_log1p")
                link(a.activation(t1, t1, ACT.Exp))
                link(a.activation(t1, t1, ACT.Ln, bias=1.0), "log1p_done")
            projection(zg, (0,), "z_ready")
            need("A_ready")
            link(a.activation(eA, la, ACT.Exp))
            link(a.activation(dk, dk, ACT.Exp), "eA_done")
            projection(zg, (1, 2), "z_ready")
            projection(zr, range(3), "z_ready", ACT.Silu)

            def decay(n):
                need("to_decay")
                link(a.activation(X[n % 3], X[n % 3], ACT.Exp), "decay_done")

            def sample_exp(g):
                need("to_exps")
                link(a.activation(Sm[g], Sm[g], ACT.Exp, bias=stat[:, 32:33], accum_out=stat[:, 33:34]), "exps_done")

            need("to_halves")
            link(a.activation(halves, halves, ACT.Exp), "halves_done")
            decay(0)
            for n in range(18):
                if n < 17:
                    decay(n + 1)
                if n == 3:
                    sample_exp(0)
                if n == 11:
                    square_roots(1)
            sample_exp(1)
            empty(osb, lambda o: o[:, :], "osb_ready")
            square_roots(3)
            def memory_projection(dst, c):
                for i in range(2):
                    empty(dst[:, i, 512 * c:512 * c + 512], lambda o: o[:, :], "mk_ready", scale=mem_rstd[:, i:i + 1])

            def prompt_exp():
                need("to_exp")
                link(a.activation(Sb, Sb, ACT.Exp), "exp_done")

            need("mem_rstd_ready")
            memory_projection(mkn, 0)
            prompt_exp()
            memory_projection(mkn, 1)
            prompt_exp()
            memory_projection(mvn, 0)
            memory_projection(mvn, 1)
            a.wait_ge(S("stored1"), 16 * 4)
            norm_roots()
            for f in range(8):
                empty(q2T[:, f, :], lambda o: o[:, 0:T], "q2T_ready")
            for d in (S2[0], S2[1], S2s):
                need("to_exp")
                link(a.activation(d, d, ACT.Exp), "exp_done")
            norm_roots()
            a.wait_ge(S("stored2"), 16 * 2)
            for lo, hi in ((0, P), (P, T)):
                for f in range(16):
                    empty(qvT[:, f, lo:hi], lambda o: o[:, 0:hi - lo], "qvT_ready")
            def gates(i):
                need("to_exp")
                link(a.activation(gate[0:TW[i], i, :], gate[0:TW[i], i, :], ACT.Exp), "exp_done")

            gates(0)
            nd = 0
            for m in range(len(runs) + 1):
                if m < len(runs):
                    i, k = runs[m]
                    c = slice(RUN * k, RUN * k + RUN)
                    d = dots[:, i, c] if i < 2 else dots_s[:, c]
                    need("to_gelu")
                    link(a.activation(d, d, ACT.Gelu), "gelu_done")
                    if m >= 2 and runs[m - 2][0] != runs[m - 1][0]:
                        square_roots(1)
                    if i < 2 and k == 4:
                        gates(i + 1)
                if m == 0:
                    continue
                i, k = runs[m - 1]
                need("coef_ready")
                for j in range(RUN * k, RUN * k + RUN):
                    if nd >= 4:
                        a.wait_ge(*v_done[nd - 4])
                    src, w, co = (ident, P, gate[:, i, j:j + 1]) if i < 2 else (C("fold"), 32, gate_s[:, j:j + 1])
                    link(a.activation(diag[nd % 4][:, 0:w], src, ACT.Copy, scale=co), "diag_ready")
                    nd += 1
            square_roots(1)

        @block.sync
        def _(sp):
            xp = x_prompt[0].rearrange("(i p) d -> i p d", p=P)
            xsm = x_sample.rearrange("b t d -> (b t) d")
            for i in range(2):
                sp.dma_start(x[:, i, :], xp[i]).then_inc(S("x_in"), 16)
            sp.dma_start(x[0:32, 2, :], xsm).then_inc(S("x_in"), 16)
            sp.dma_start(cst[:, :], consts).then_inc(S("consts"), 16)
            with nc.allow_non_contiguous_dma(reason="gains with features on partitions"):
                for n, g in enumerate((g_mix, g_mem_q, g_mem_kv)):
                    sp.dma_start(gains[:, n, :], g[0].rearrange("(c p) -> p c", p=P)).then_inc(S("small"), 16)
                sp.dma_start(g_ffn_t[:, :], g_ffn[0].rearrange("(c p) -> p c", p=P)).then_inc(S("small"), 16)
                sp.dma_start(b_al[:, :], b_alpha[0].rearrange("(c p) -> p c", p=P)).then_inc(S("small"), 16)
            sp.dma_start(w_al[:, :], w_alpha_up[0]).then_inc(S("small"), 16)
            sp.dma_start(g_gla_b[:, :], g_gla_out[0].partition_broadcast(P)).then_inc(S("small"), 16)
            def store_keys_and_values():
                sp.wait_ge(S("rope_done"), 3)
                sp.wait_ge(S("z_ready"), 9)
                for z, op_, os_ in ((zk, k_prompt, k_sample), (zv, v_prompt, v_sample)):
                    for i in range(2):
                        sp.dma_start(op_[0, 0].rearrange("(i p) h d -> i p (h d)", p=P)[i], z[:, i, :])\
                         .then_inc(S("kv_out"), 16)
                    sp.dma_start(os_[0].rearrange("b t h d -> (b t) (h d)"), z[0:32, 2, :]).then_inc(S("kv_out"), 16)

            def store_states():
                sp.wait_ge(S("newstate_ready"), 1)
                for f in range(2):
                    sp.dma_start(gla_sample[0, :, 2 * f:2 * f + 2].rearrange("b r k v -> (r k) b v"), St_n[:, :, f, :])\
                     .then_inc(S("stored1"), 16)
                    sp.dma_start(gla_prompt[0, 0, 2 * f:2 * f + 2].rearrange("r k v -> (r k) v"), St_p[:, 7, f, :])\
                     .then_inc(S("stored1"), 16)

            for k, src in enumerate(stream):
                before = [j for j in range(k) if slot_of[j] == slot_of[k]]
                if before:
                    sp.wait_ge(*w_done[before[-1]])
                if k == 7:
                    for s_ in range(KSLOT, WIDE):
                        sp.wait_ge(*block_done[max(m for m in range(N_WIDE) if taken[m][3] == s_)])
                if k == 11:
                    sp.dma_start(g_row[:, :], g_ffn[0].partition_broadcast(P)).then_inc(S("g_row"), 16)
                    sp.wait_ge(*block_done[-1])
                if k == 12:
                    sp.wait_ge(*w_done[10])
                if k == len(stream) - 1:
                    sp.wait_ge(S("o2T_ready"), 12)
                    sp.wait_ge(S("stored2"), 32)
                n = src.shape[2]
                sp.dma_start(wslot[slot_of[k]][:, 0:KC * n].rearrange("p (c n) -> p c n", c=KC), src)\
                  .then_inc(S(f"w{slot_of[k]}"), 16)
                if k == 6:
                    store_keys_and_values()
                    store_states()
                    sp.wait_ge(S("stored1"), 64)
                    sp.dma_start(memT.rearrange("p c m -> p (c m)"), mem_prompt).then_inc(S("mem_in"), 16)
            sp.wait_ge(S("g_row_used"), 4)
            sp.dma_start(g_row[:, :], g_final.partition_broadcast(P)).then_inc(S("g_row"), 16)
            for i in range(2):
                sp.wait_ge(S("y_ready"), i + 1)
                sp.dma_start(y_prompt[0].rearrange("(i p) d -> i p d", p=P)[i], x[:, i, :]).then_inc(S("y_out"), 16)
            sp.wait_ge(S("y_ready"), 3)
            sp.dma_start(y_sample.rearrange("b t d -> (b t) d"), x[0:32, 2, :]).then_inc(S("y_out"), 16)
            sp.wait_ge(S("y_out"), 48)
            sp.wait_ge(S("stored1"), 64)
            sp.wait_ge(S("stored2"), 32)
            sp.wait_ge(S("kv_out"), 96)

        @block.gpsimd
        def _(g):
            g.dma_start(table[:, :], page_table.rearrange("b n -> (b n)").partition_broadcast(P))\
             .then_inc(S("table_in"), 16)
            for f in range(2):
                g.dma_start(St_s[:, :, f, :], state_gla[0, :, 2 * f:2 * f + 2].rearrange("b r k v -> (r k) b v"))\
                 .then_inc(S("state_in"), 16)
            g.wait_ge(S("block_ix_ready"), 1)
            pairs = cache_v[0].rearrange("n (a two) h d -> (n a) (two h d)", two=2)
            for n, (kind, b, blk, s_) in enumerate(taken):
                if n - N_EARLY in (0, 4, 5):
                    g.wait_ge(*w_done[{0: 4, 4: 5, 5: 6}[n - N_EARLY]])
                if n == 4:
                    g.wait_ge(S("root_ready"), 3)
                before = [m for m in range(n) if taken[m][3] == s_]
                if before:
                    g.wait_ge(*block_done[before[-1]])
                slot = bslot[s_]
                if kind == "key":
                    for r in range(2):
                        at = b * NPAGE + 2 * blk + r
                        g.indirect_dma_start(slot[:, r * 512:(r + 1) * 512], None, cache_k,
                                             bass.IndirectOffsetOnAxis(ap=page_ix[:, at:at + 1], axis=0))\
                         .then_inc(S(f"kv{s_}"), 16)
                else:
                    at = b * NBLK + blk
                    g.indirect_dma_start(slot, None, pairs,
                                         bass.IndirectOffsetOnAxis(ap=block_ix[:, at:at + 1], axis=0))\
                     .then_inc(S(f"kv{s_}"), 16)
            g.wait_ge(S("mk_ready"), 8)
            for src, dst in ((mkn, mem_k_prompt), (mvn, mem_v_prompt)):
                g.dma_start(dst[0, 0].rearrange("(i p) h d -> p i (h d)", p=P), src).then_inc(S("stored2"), 16)
            g.wait_ge(S("mixT_ready"), 21)
            g.wait_ge(S("kv_out"), 96)
            n = 0
            for cache in (cache_mem_k, cache_mem_v):
                for b in range(NB):
                    if n == 4:
                        g.wait_ge(S("root_ready"), 6)
                    if n >= 5:
                        g.wait_ge(*mem_done[n - 5])
                    if cache is cache_mem_k:
                        src, dst = cache[b], memkv[n % 5].rearrange("p a b -> p (a b)")
                    else:
                        src, dst = cache[0, b].rearrange("(k p) h d -> p k (h d)", p=P), memkv[n % 5]
                    g.dma_start(dst, src)\
                     .then_inc(S(f"mem{n % 5}"), 16)
                    n += 1
            g.wait_ge(S("o2T_ready"), 12)
            g.wait_ge(S("stored2"), 32)
            g.dma_start(skT.rearrange("p f k -> p (f k)"), peer_sub_keys).then_inc(S("subkeys"), 16)
            for piece in range(4):
                ff = slice(4 * piece, 4 * piece + 4)
                g.wait_ge(S("hot_ready"), piece + 1)
                h_ = hot[piece]
                nc.gpsimd.tensor_tensor(h_, h_, bc(tif[:, ff, :], 2, 16), ALU.mult).then_inc(S("hot_summed"), 1)
                g.wait_ge(S("hot_summed"), 4 * piece + 1)
                for step, half in enumerate((8, 4, 2)):
                    nc.gpsimd.tensor_tensor(h_[:, :, :, 0:half], h_[:, :, :, 0:half], h_[:, :, :, half:2 * half], ALU.add)\
                      .then_inc(S("hot_summed"), 1)
                    g.wait_ge(S("hot_summed"), 4 * piece + 2 + step)
                nc.gpsimd.tensor_tensor(keyno[:, ff, :], h_[:, :, :, 0], h_[:, :, :, 1], ALU.add)\
                  .then_inc(S("keyno_ready"), 1)
                g.wait_ge(S("keyno_ready"), piece + 1)
            g.wait_ge(*w_done[-1])
            done = []
            for n, (kind, i, j) in enumerate(rows):
                if j == 0 and kind == "u":
                    g.wait_ge(S("eid_ready"), i + 1)
                    if i == 2:
                        g.wait_ge(S("eid_s_ready"), 4)
                if n >= GSLOT:
                    g.wait_ge(*done[n - GSLOT])
                idx = eid[:, i, j:j + 1] if i < 2 else eid_s[:, j:j + 1]
                g.indirect_dma_start(gslot[n % GSLOT], None, (expert_u if kind == "u" else expert_v)[0],
                                     bass.IndirectOffsetOnAxis(ap=idx, axis=0)).then_inc(S(f"g{n % GSLOT}"), 16)
                nth = sum(1 for r in rows[0:n] if r[0] == kind)
                done.append((S("dot_done"), nth + 1) if kind == "u" else v_done[nth])


_INS = ['x_prompt', 'x_sample', 'cache_k', 'cache_v', 'state_gla', 'cache_mem_k', 'cache_mem_v', 'page_table',
        'mem_prompt', 'g_mix', 'w_in', 'w_alpha_up', 'b_alpha', 'g_gla_out', 'w_out', 'g_mem_q', 'g_mem_kv', 'w_mem_q',
        'w_mem_k', 'w_mem_v', 'w_mem_o', 'g_ffn', 'w_peer_q', 'peer_sub_keys', 'expert_u', 'expert_v', 'g_final']
_OUTS = [(1, 256, 1024), (8, 4, 1024), (1, 1, 256, 8, 64), (1, 1, 256, 8, 64), (1, 1, 4, 64, 128),
         (1, 1, 256, 4, 256), (1, 1, 256, 4, 256), (1, 8, 4, 8, 64), (1, 8, 4, 8, 64), (1, 8, 4, 64, 128)]


def kernel(**inputs):
    import numpy as _np
    import concourse.bacc as _bacc
    from concourse import mybir as _mybir
    from concourse.bass_utils import run_bass_kernel_spmd as _run

    nc = _bacc.Bacc("TRN2", target_bir_lowering=False, num_devices=1)
    arrays, args = {}, []
    for name in _INS + ["consts"]:
        a = shape_constants() if name == "consts" else _np.asarray(inputs[name])
        if name == "cache_mem_k":
            a = a.reshape(NB, 256, KC, P).transpose(0, 3, 2, 1).reshape(NB, P, KC * 256)
        if name == "cache_k":
            a = a.reshape(NPOOL, 64, 2, 4, P).transpose(0, 4, 3, 2, 1).reshape(NPOOL * P, 4 * PAGE)
        if name == "mem_prompt":
            a = a.reshape(256, KC, P).transpose(2, 1, 0).reshape(P, KC * 256)
        if name == "peer_sub_keys":
            a = a[0].transpose(3, 0, 1, 2).reshape(P, 16 * 128)
        a = _np.ascontiguousarray(a)
        arrays[f"in_{name}_dram"] = a
        args.append(nc.dram_tensor(f"in_{name}_dram", a.shape, _mybir.dt.from_np(a.dtype), kind="ExternalInput").ap())
    for i, shape in enumerate(_OUTS):
        args.append(nc.dram_tensor(f"out_{i}_dram", shape, _mybir.dt.float32, kind="ExternalOutput").ap())
    hybrid_step(nc, *args)
    r = _run(nc, [arrays], core_ids=[0])
    return tuple(r.results[0][f"out_{i}_dram"] for i in range(len(_OUTS)))
```
